# Optimizing a Trainium2 kernel written in Bass

```python
import math
import jax, jax.numpy as jnp
from jax import lax
import numpy as np

D_MODEL = 2048
BATCH = 1
SEQ = 512
DEPTH = 1

CHUNK = 64

CONV_WIDTH = D_MODEL
CONV_K = 3
SSM_WIDTH = D_MODEL // 2
SSM_GROUP = 16
SSM_GROUPS = SSM_WIDTH // SSM_GROUP
SSM_STATE = 64
DT_MIN = 0.001
DT_MAX = 0.1
RMS_EPS = 1e-6

_SIZES = (CONV_WIDTH, CONV_WIDTH, CONV_WIDTH, CONV_WIDTH,
          SSM_WIDTH, SSM_WIDTH,
          D_MODEL, D_MODEL)
N_IN = int(sum(_SIZES))
SPLITS = tuple(int(s) for s in np.cumsum(_SIZES)[:-1])


def rmsnorm(x, g):
    x32 = x.astype(jnp.float32)
    y = x32 * lax.rsqrt(jnp.mean(x32 * x32, axis=-1, keepdims=True) + RMS_EPS)
    return (y * g.astype(jnp.float32)).astype(x.dtype)

def causal_depthwise_conv(v, w):
    L = v.shape[1]
    vp = jnp.pad(v, ((0, 0), (CONV_K - 1, 0), (0, 0)))
    out = w[0] * vp[:, 0:L]
    for k in range(1, CONV_K):
        out = out + w[k] * vp[:, k:k + L]
    return out

def s5_scan(u, a_re, a_im, log_dt, b_re, b_im, c_re, c_im, d_skip):
    bsz, L, _ = u.shape
    f32 = jnp.float32
    ug = u.astype(f32).reshape(bsz, L, SSM_GROUPS, SSM_GROUP)
    lam = lax.complex(a_re.astype(f32), a_im.astype(f32))
    dt = jnp.exp(log_dt.astype(f32))[:, None]
    lam_bar = jnp.exp(lam * dt)
    b = lax.complex(b_re.astype(f32), b_im.astype(f32))
    b_bar = ((lam_bar - 1.0) / lam)[..., None] * b
    bu = jnp.einsum('gpc,blgc->blgp', b_bar, ug.astype(jnp.complex64))
    a = jnp.broadcast_to(lam_bar, bu.shape)

    def combine(e1, e2):
        a1, h1 = e1
        a2, h2 = e2
        return a1 * a2, a2 * h1 + h2

    _, h = lax.associative_scan(combine, (a, bu), axis=1)
    c = lax.complex(c_re.astype(f32), c_im.astype(f32))
    y = jnp.einsum('gcp,blgp->blgc', c, h).real + d_skip.astype(f32) * ug
    return y.reshape(bsz, L, SSM_WIDTH)

def hybrid_layer(x, norm_g, w_in, conv_w, w_out_a, a_re, a_im, log_dt, b_re, b_im,
                 c_re, c_im, d_skip, w_glu, b_glu, w_out_b, w_o):
    h = rmsnorm(x, norm_g)
    proj = jnp.einsum('bld,dn->bln', h, w_in)
    v, bg, cg, za, u, zb, ga, gb = jnp.split(proj, SPLITS, axis=-1)
    ya = bg * causal_depthwise_conv(cg * v, conv_w)
    ya = jnp.einsum('blc,cd->bld', ya * jax.nn.silu(za), w_out_a)
    yb = jax.nn.gelu(s5_scan(u, a_re, a_im, log_dt, b_re, b_im, c_re, c_im, d_skip))
    yb = yb * jax.nn.sigmoid(jnp.einsum('blc,ce->ble', yb, w_glu.astype(jnp.float32))
                             + b_glu.astype(jnp.float32))
    yb = yb.astype(x.dtype)
    yb = jnp.einsum('blc,cd->bld', yb * jax.nn.silu(zb), w_out_b)
    m = jax.nn.sigmoid(ga) * ya + jax.nn.sigmoid(gb) * yb
    return x + jnp.einsum('bld,de->ble', m, w_o)

def first_inputs(seed: int = 0) -> dict:
    key = jax.random.key(seed)
    ks = jax.random.split(key, 20)
    f32 = jnp.float32
    n = lambda k, shape, s: jax.random.normal(k, shape, f32) * s
    res_scale = 1.0 / math.sqrt(2.0 * DEPTH)
    G, P, c = SSM_GROUPS, SSM_STATE, SSM_GROUP
    a_im_base = math.pi * jnp.arange(P, dtype=f32)
    return {
        "x": n(ks[0], (BATCH, SEQ, D_MODEL), 1.0),
        "norm_g": 1.0 + n(ks[1], (DEPTH, D_MODEL), 0.02),
        "w_in": n(ks[2], (DEPTH, D_MODEL, N_IN), D_MODEL ** -0.5),
        "conv_w": n(ks[3], (DEPTH, CONV_K, CONV_WIDTH), CONV_K ** -0.5),
        "w_out_a": n(ks[4], (DEPTH, CONV_WIDTH, D_MODEL), CONV_WIDTH ** -0.5),
        "a_re": -0.5 + n(ks[5], (DEPTH, G, P), 0.01),
        "a_im": a_im_base + n(ks[6], (DEPTH, G, P), 0.01),
        "log_dt": jax.random.uniform(ks[7], (DEPTH, G), f32,
                                     math.log(DT_MIN), math.log(DT_MAX)),
        "b_re": n(ks[8], (DEPTH, G, P, c), (2.0 * c) ** -0.5),
        "b_im": n(ks[9], (DEPTH, G, P, c), (2.0 * c) ** -0.5),
        "c_re": n(ks[10], (DEPTH, G, c, P), (2.0 * P) ** -0.5),
        "c_im": n(ks[11], (DEPTH, G, c, P), (2.0 * P) ** -0.5),
        "d_skip": n(ks[12], (DEPTH, G, c), 1.0),
        "w_glu": n(ks[13], (DEPTH, SSM_WIDTH, SSM_WIDTH), SSM_WIDTH ** -0.5),
        "b_glu": n(ks[14], (DEPTH, SSM_WIDTH), 0.02),
        "w_out_b": n(ks[15], (DEPTH, SSM_WIDTH, D_MODEL), SSM_WIDTH ** -0.5),
        "w_o": n(ks[16], (DEPTH, D_MODEL, D_MODEL), D_MODEL ** -0.5 * res_scale),
        "final_g": 1.0 + n(ks[17], (D_MODEL,), 0.02),
    }

def first_block(x, norm_g, w_in, conv_w, w_out_a, a_re, a_im, log_dt, b_re, b_im,
              c_re, c_im, d_skip, w_glu, b_glu, w_out_b, w_o, final_g):
    for i in range(DEPTH):
        x = hybrid_layer(x, norm_g[i], w_in[i], conv_w[i], w_out_a[i], a_re[i], a_im[i],
                         log_dt[i], b_re[i], b_im[i], c_re[i], c_im[i], d_skip[i],
                         w_glu[i], b_glu[i], w_out_b[i], w_o[i])
    return rmsnorm(x, final_g)


D_MIX = D_MODEL
WIDTH_A = D_MIX // 2
WIDTH_B = D_MIX - WIDTH_A
CHUNK_2 = 128
HEADS_A = 8
DH_A = WIDTH_A // HEADS_A
HEADS_B = 16
DH_B = WIDTH_B // HEADS_B
Q_BLOCK = 128
EPS = 1e-6
SPLIT_SIZES = (WIDTH_A, WIDTH_A, WIDTH_A, WIDTH_B, WIDTH_B, WIDTH_B, WIDTH_B, HEADS_B)
D_IN = sum(SPLIT_SIZES)


def _split_points(sizes):
    pts, acc = [], 0
    for s in sizes[:-1]:
        acc += s
        pts.append(acc)
    return pts

def rms_norm(x, g):
    xf = x.astype(jnp.float32)
    y = xf * lax.rsqrt(jnp.mean(xf * xf, axis=-1, keepdims=True) + EPS)
    return (y * g.astype(jnp.float32)).astype(x.dtype)

def layer_norm(x, g, b):
    xf = x.astype(jnp.float32)
    mu = jnp.mean(xf, axis=-1, keepdims=True)
    xc = xf - mu
    var = jnp.mean(xc * xc, axis=-1, keepdims=True)
    y = xc * lax.rsqrt(var + EPS) * g.astype(jnp.float32) + b.astype(jnp.float32)
    return y.astype(x.dtype)

def chunked_spatial_gating(u, v, ln_g, ln_b, w_s, b_s):
    bsz, s, _ = v.shape
    n = s // CHUNK_2
    v = layer_norm(v, ln_g, ln_b)
    vc = v.reshape(bsz, n, CHUNK_2, HEADS_A, DH_A)
    causal = jnp.tril(jnp.ones((CHUNK_2, CHUNK_2), dtype=bool))
    w = jnp.where(causal[None], w_s, jnp.zeros_like(w_s))
    mixed = jnp.einsum('hts,bnshd->bnthd', w, vc) + b_s.T[None, None, :, :, None]
    return u * mixed.reshape(bsz, s, WIDTH_A)

def forgetting_attention(q, k, v, f_logit, b_f):
    bsz, s, _ = q.shape
    nb = s // Q_BLOCK
    to_heads = lambda t: t.reshape(bsz, s, HEADS_B, DH_B).transpose(0, 2, 1, 3)
    q, k, v = to_heads(q), to_heads(k), to_heads(v)
    log_f = jax.nn.log_sigmoid(f_logit.astype(jnp.float32) + b_f.astype(jnp.float32))
    F = jnp.cumsum(log_f, axis=1).transpose(0, 2, 1)
    qb = q.reshape(bsz, HEADS_B, nb, Q_BLOCK, DH_B).transpose(2, 0, 1, 3, 4)
    Fb = F.reshape(bsz, HEADS_B, nb, Q_BLOCK).transpose(2, 0, 1, 3)
    k_pos = jnp.arange(s)
    scale = DH_B ** -0.5

    def block(args):
        qi, Fi, i = args
        q_pos = i * Q_BLOCK + jnp.arange(Q_BLOCK)
        logits = jnp.einsum('bhqd,bhkd->bhqk', qi, k).astype(jnp.float32) * scale
        logits = logits + (Fi[..., :, None] - F[..., None, :])
        logits = jnp.where(q_pos[:, None] >= k_pos[None, :], logits, -jnp.inf)
        p = jax.nn.softmax(logits, axis=-1)
        return jnp.einsum('bhqk,bhkd->bhqd', p.astype(v.dtype), v)

    out = lax.map(block, (qb, Fb, jnp.arange(nb)))
    return out.transpose(1, 0, 3, 2, 4).reshape(bsz, s, WIDTH_B)

def second_inputs(seed: int = 0) -> dict:
    key = jax.random.key(seed)
    ks = jax.random.split(key, 16)
    f32 = jnp.float32
    nrm = lambda k, shape: jax.random.normal(k, shape, dtype=f32)
    row_scale = (1.0 / jnp.sqrt(jnp.arange(1, CHUNK_2 + 1, dtype=f32)))[None, None, :, None]
    b_f = jnp.linspace(1.0, 5.0, HEADS_B, dtype=f32)[None, :] + 0.1 * nrm(ks[11], (DEPTH, HEADS_B))
    return {
        "x": nrm(ks[0], (BATCH, SEQ, D_MODEL)),
        "c": nrm(ks[1], (BATCH, D_MODEL)),
        "norm_g": 1.0 + 0.1 * nrm(ks[2], (DEPTH, D_MODEL)),
        "w_ada": nrm(ks[3], (DEPTH, D_MODEL, 3 * D_MODEL)) * D_MODEL ** -0.5,
        "b_ada": 0.01 * nrm(ks[4], (DEPTH, 3 * D_MODEL)),
        "w_in": nrm(ks[5], (DEPTH, D_MODEL, D_IN)) * D_MODEL ** -0.5,
        "ln_v_g": 1.0 + 0.1 * nrm(ks[6], (DEPTH, WIDTH_A)),
        "ln_v_b": 0.01 * nrm(ks[7], (DEPTH, WIDTH_A)),
        "w_s": nrm(ks[8], (DEPTH, HEADS_A, CHUNK_2, CHUNK_2)) * row_scale,
        "b_s": 1.0 + 0.1 * nrm(ks[9], (DEPTH, HEADS_A, CHUNK_2)),
        "b_f": b_f,
        "w_out": nrm(ks[10], (DEPTH, D_MIX, D_MODEL)) * D_MIX ** -0.5,
        "final_g": 1.0 + 0.1 * nrm(ks[12], (D_MODEL,)),
    }

def second_block(x, c, norm_g, w_ada, b_ada, w_in, ln_v_g, ln_v_b, w_s, b_s, b_f, w_out, final_g):
    cond = jax.nn.silu(c)
    pts = _split_points(SPLIT_SIZES)
    for l in range(DEPTH):
        mod = cond @ w_ada[l] + b_ada[l]
        shift, scale, gate = jnp.split(mod, 3, axis=-1)
        h = rms_norm(x, norm_g[l]) * (1.0 + scale[:, None, :]) + shift[:, None, :]
        z = h @ w_in[l]
        u_a, v_a, g_a, q_b, k_b, v_b, g_b, f_b = jnp.split(z, pts, axis=-1)
        y_a = chunked_spatial_gating(jax.nn.gelu(u_a, approximate=False),
                                     jax.nn.gelu(v_a, approximate=False),
                                     ln_v_g[l], ln_v_b[l], w_s[l], b_s[l]) * jax.nn.silu(g_a)
        y_b = forgetting_attention(q_b, k_b, v_b, f_b, b_f[l]) * jax.nn.silu(g_b)
        y = jnp.concatenate([y_a, y_b], axis=-1) @ w_out[l]
        x = x + gate[:, None, :] * y
    return rms_norm(x, final_g)


def setup_inputs(seed=0):
    out = dict(first_inputs(seed))
    for name, value in second_inputs(seed + 1).items():
        if name != "x":
            out[name + "_2"] = value
    return out


def reference(
    x, norm_g, w_in, conv_w, w_out_a, a_re, a_im, log_dt, b_re, b_im, c_re, c_im, d_skip, w_glu,
    b_glu, w_out_b, w_o, final_g, c_2, norm_g_2, w_ada_2, b_ada_2, w_in_2, ln_v_g_2, ln_v_b_2,
    w_s_2, b_s_2, b_f_2, w_out_2, final_g_2,
):
    x = first_block(
        x, norm_g, w_in, conv_w, w_out_a, a_re, a_im, log_dt, b_re, b_im, c_re, c_im, d_skip,
        w_glu, b_glu, w_out_b, w_o, final_g,
    )
    return second_block(
        x, c_2, norm_g_2, w_ada_2, b_ada_2, w_in_2, ln_v_g_2, ln_v_b_2, w_s_2, b_s_2, b_f_2,
        w_out_2, final_g_2,
    )


_drawn_inputs = setup_inputs


def setup_inputs(seed=0):
    import zlib

    import numpy as np

    out = dict(_drawn_inputs(seed))
    spreads = {}
    factors = {'norm_g': 5.152,
     'a_re': 64.0,
     'a_im': 64.0,
     'log_dt': 64.0,
     'b_re': 64.0,
     'b_im': 64.0,
     'c_re': 64.0,
     'c_im': 64.0,
     'b_glu': 200.0,
     'b_ada_2': 4.881,
     'ln_v_b_2': 8.0,
     'd_skip': 3.435,
     'w_glu': 4.84,
     'w_out_b': 2.993}
    for name, (base, spread) in spreads.items():
        noise = np.random.default_rng([zlib.crc32(name.encode()), seed]).standard_normal(out[name].shape)
        drawn = base * np.exp(spread * noise) if base else spread * noise
        out[name] = __import__('jax').numpy.asarray(drawn.astype(out[name].dtype))
    for name, factor in factors.items():
        out[name] = (out[name] * factor).astype(out[name].dtype)
    return out
```

```python
from collections import deque

import numpy as np

import concourse.bass as bass
from concourse import mybir

F32 = mybir.dt.float32
F32R = mybir.dt.float32r
I32 = mybir.dt.int32
ALU = mybir.AluOpType
ACT = mybir.ActivationFunctionType
AX = mybir.AxisListType.X

S = 512
EPS = 1e-6
KB = 1024
BASE = 16512
MAGIC = 12582912.0
NW = 3
NB = 3
AHEAD = 2

PARAMS = [
    "xT", "w1", "wg", "wa", "wb", "wo", "w2", "wvv", "wf", "w3", "ada", "cols", "are", "aim", "ldt",
    "bre", "bim", "cre", "cim", "wsT", "bsb",
]
COLS = [("g1", 16), ("fg", 16), ("g2", 16), ("fg2", 16), ("cw", 48), ("bglu", 8), ("dsk", 8),
        ("bada", 48), ("c2", 16), ("lng", 8), ("lnb", 8), ("bf", 1)]


class Flow:

    def __init__(self, engines, sems):
        self.engines = engines
        self.sems = sems
        self.count = {e: 0 for e in sems}
        self.seen = {e: {} for e in engines}

    def _wait(self, eng, after):
        todo = list(after)
        while todo:
            t = todo.pop()
            if t is None:
                continue
            if isinstance(t, list):
                todo.extend(t)
                continue
            sem, value = t
            if self.seen[eng].get(id(sem), 0) < value:
                self.seen[eng][id(sem)] = value
                self.engines[eng].wait_ge(sem, value)

    def op(self, eng, fn, *after):
        self._wait(eng, after)
        fn(self.engines[eng]).then_inc(self.sems[eng], 1)
        self.count[eng] += 1
        return self.sems[eng], self.count[eng]

    def quiet(self, eng, fn, *after):
        self._wait(eng, after)
        fn(self.engines[eng])

    def dma(self, slot, fn, *after):
        self._wait("sp", after)
        fn(self.engines["sp"]).then_inc(slot[0], 16)
        slot[1] += 16
        return slot[0], slot[1]


def stream_order(t):
    out = []

    def tiles(tag, w, m):
        for c in range(w.shape[1]):
            out.append((tag, w[m, c]))

    for m in range(8):
        tiles("u", t["w1"], 64 + m)
    for m in range(8):
        tiles("zb", t["w1"], 72 + m)
    for m in range(32):
        tiles("gate", t["w1"], 80 + m)
    n = 0
    for c in range(16):
        for part in (0, 2, 1, 3):
            for kc in range(2):
                out.append(("a", t["w1"][16 * part + c, kc]))
                if n < 96:
                    out.append(("ada", t["ada"][n // 16, n % 16]))
                    n += 1
    for m in range(16):
        tiles("wa", t["wa"], m)
    for m in range(8):
        tiles("wg", t["wg"], m)
    for m in range(16):
        tiles("wb", t["wb"], m)
    for m in range(16):
        tiles("wo", t["wo"], m)
    for half in (2, 3):
        tiles("v", t["wvv"], half)
    for j in range(8):
        for m in (24 + j, 32 + j, 48 + j):
            tiles("qkg", t["w2"], m)
    for half in (0, 1):
        tiles("v", t["wvv"], half)
    for h in range(8):
        for m in (h, 16 + h):
            tiles("ug", t["w2"], m)
    for m in range(16):
        tiles("w3", t["w3"], m)
    return out


def program(nc, t, out):
    sem_names = ["pe", "act", "dve", "pool"]
    fl = Flow({"pe": nc.tensor, "act": nc.scalar, "dve": nc.vector, "pool": nc.gpsimd, "sp": nc.sync},
              {e: nc.alloc_semaphore("s_" + e) for e in sem_names})
    op, quiet = fl.op, fl.quiet

    def slot(name):
        return [nc.alloc_semaphore("d_" + name), 0]

    def at(name, kb, shape, dt=F32):
        return nc.alloc_sbuf_tensor_at(name, shape, dt, offset=BASE + int(kb * KB))

    bank = [nc.alloc_psum_tensor(f"bank{i}", [128, 512], F32) for i in range(8)]
    free = [[] for _ in range(8)]

    scratch = {n: nc.dram_tensor("scr_" + n, [k, 128, 512], F32, kind="Internal").ap()
               for n, k in (("zb", 8), ("ga", 16), ("gb", 16), ("x1", 16))}

    hH, hL = at("hH", 0, [128, 16, 512], F32R), at("hL", 32, [128, 16, 512], F32R)
    MA = at("MA", 0, [128, 16, 512])
    ybH, ybL = at("ybH", 32, [128, 8, 512], F32R), at("ybL", 48, [128, 8, 512], F32R)
    mL = at("mL", 32, [128, 16, 512], F32R)
    X1 = at("X1", 0, [128, 16, 512])
    QA = at("QA", 0, [65, 2, 2, 512])
    KA = at("KA", 8, [65, 2, 2, 512])
    PR = at("PR", 16, [128, 4, 512])
    PT = at("PT", 24, [128, 4, 512])
    WS = at("WS", 0, [128, 8, 128])
    BSB = at("BSB", 4, [128, 8, 128])
    CON = at("CON", 8, [128, 8, 128])
    SQ = at("SQ", 12, [128, 1024])
    YF = at("YF", 32, [128, 16, 512])
    X2 = at("X2", 0, [128, 16, 512])
    AH, AL = at("AH", 64, [128, 16, 512], F32R), at("AL", 96, [128, 16, 512], F32R)
    XS = at("XS", 96, [128, 16, 512])
    BH, BL = at("BH", 64, [128, 8, 512], F32R), at("BL", 80, [128, 8, 512], F32R)
    mH = at("mH", 96, [128, 16, 512], F32R)
    h2H, h2L = at("h2H", 64, [128, 16, 512], F32R), at("h2L", 96, [128, 16, 512], F32R)
    yH, yL = at("yH", 64, [128, 16, 512], F32R), at("yL", 96, [128, 16, 512], F32R)
    BT = at("BT", 64, [128, 2, 8, 128])
    CB = at("CB", 72, [128, 2, 32, 32])
    CR = at("CR", 80, [128, 2, 32, 16])
    SM = at("SM", 84, [128, 32, 32])
    E0 = at("E0", 88, [128, 2, 32, 32])
    W0 = at("W0", 96, [128, 2, 32, 16])
    TAB = at("TAB", 100, [128, 2, 2, 512])
    V = at("V", 108, [128, 6, 512])
    HH = at("HH", 120, [128, 2, 2, 512])
    W = at("W", 128, [128, NW, 1024])
    WH, WL = at("WH", 140, [128, NB, 1024], F32R), at("WL", 152, [128, NB, 1024], F32R)
    U = at("U", 164, [128, 8, 512])
    VV = at("VV", 164, [128, 4, 1024])
    SO = at("SO", 180, [128, 2, 512])
    SI = at("SI", 184, [128, 2, 512])
    T = at("T", 188, [128, 4, 512])
    CV = at("CV", 196, [128, 514])
    ACC = at("ACC", 198.25, [128, 1024])
    RS = at("RS", 198.25, [128, 2, 512])
    ncol = sum(n for _, n in COLS)
    PC = at("PC", 202.25, [128, ncol])
    ONE = at("ONE", 203.25, [128, 128])
    IDT = at("IDT", 203.75, [128, 128])
    CAU = at("CAU", 204.25, [128, 128])
    MOD = at("MOD", 204.75, [128, 48])
    SC = at("SC", 205, [128, 16])
    ST = at("ST", 205.25, [128, 64])
    NF = at("NF", 205.5, [16, 512])
    col, k = {}, 0
    for name, n in COLS:
        col[name] = PC[:, k:k + n]
        k += n

    order = stream_order(t)
    wsl = [slot(f"w{i}") for i in range(NW)]
    landed, wfree, parts, used = {}, {}, {}, {}
    state = {"next": 0, "split": 0, "use": 0, "cur": [], "lag": 0}
    ada = {"n": 0, "acc": None, "free": None}

    def fetch(i):
        if i < len(order):
            src = order[i][1]
            landed[i] = fl.dma(wsl[i % NW], lambda e, i=i, src=src: e.dma_start(W[:, i % NW, :], src),
                               wfree.get(i - NW))

    low_on = {"every": 0}

    def ada_chunk(i):
        n = ada["n"]
        cb, kt = n // 16, n % 16
        w, c = W[:, i % NW, :], SC[:, kt:kt + 1]
        if kt == 0:
            m = op("dve", lambda e: e.tensor_scalar(ACC[:, :], w, c, None, ALU.mult),
                   landed[i], ada["free"], ada["c"])
        else:
            m = op("dve", lambda e: e.scalar_tensor_tensor(out=ACC[:, :], in0=w, scalar=c, in1=ACC[:, :],
                                                           op0=ALU.mult, op1=ALU.add),
                   landed[i], ada["acc"])
        ada["acc"] = m
        wfree[i] = m
        ada["n"] += 1
        if kt == 15:
            for q in range(8):
                mm = op("pe", lambda e, q=q: e.matmul(bank[3][:, q:q + 1], ACC[:, q * 128:(q + 1) * 128],
                                                      ONE[:, 0:1], start=True, stop=True), m, free[3])
            k0 = cb * 8
            free[3] = [op("dve", lambda e: e.tensor_tensor(MOD[:, k0:k0 + 8], bank[3][:, 0:8],
                                                           col["bada"][:, k0:k0 + 8], ALU.add), mm)]
            ada["free"] = free[3]
            ada["mod"] = free[3]

    def prepare():
        i = state["next"]
        if i >= len(order):
            return False
        state["next"] += 1
        if order[i][0] == "ada":
            ada_chunk(i)
        else:
            n = state["split"]
            state["split"] += 1
            b = n % NB
            w, wh, wl = W[:, i % NW, :], WH[:, b, :], WL[:, b, :]
            mh = op("act", lambda e: e.activation(wh, w, ACT.Copy), landed[i], used.get(n - NB))
            who = "pool" if low_on["every"] and n % low_on["every"] == 0 else "dve"
            ml = op(who, lambda e: e.tensor_tensor(wl, w, wh.bitcast(F32), ALU.subtract),
                    mh, landed[i], used.get(n - NB))
            wfree[i] = [mh, ml]
            parts[n] = (b, [mh, ml])
        fetch(i + NW)
        return True

    for i in range(NW):
        fetch(i)

    def chunk():
        n = state["use"]
        state["use"] += 1
        while state["split"] <= n + AHEAD and prepare():
            pass
        return n, parts[n][0], parts[n][1]

    beside = deque()
    debt = [0.0]

    def pump(budget):
        debt[0] += budget
        while beside and debt[0] > 0:
            try:
                debt[0] -= next(beside[0])
            except StopIteration:
                beside.popleft()
        if not beside:
            debt[0] = 0.0

    def drain_beside():
        while beside:
            pump(1.0)

    BUDGET = {"v": 0.0}

    def project(b, nch, XH, XL, ready):
        for kc in range(nch):
            n, s, m = chunk()
            for k8 in range(8):
                k = 8 * kc + k8
                wh, wl = WH[:, s, 128 * k8:128 * k8 + 128], WL[:, s, 128 * k8:128 * k8 + 128]
                first, last = k == 0, k == 8 * nch - 1
                quiet("pe", lambda e, wh=wh, k=k, first=first: e.matmul(bank[b][:, :], wh, XH[:, k, :],
                                                                        start=first, stop=False),
                      m, ready[k], free[b] if first else None)
                quiet("pe", lambda e, wh=wh, k=k: e.matmul(bank[b][:, :], wh, XL[:, k, :],
                                                           start=False, stop=False))

                def lo(e, wl=wl, k=k, last=last):
                    return e.matmul(bank[b][:, :], wl, XH[:, k, :], start=False, stop=last)

                if k8 == 7:
                    mark = op("pe", lo)
                else:
                    quiet("pe", lo)
            used[n] = mark
            if kc < nch - 1:
                pump(BUDGET["v"])
        return mark

    ring = {"n": 0}

    def next_bank():
        ring["n"] += 1
        return ring["n"] % 3

    def split(H, L, src, after, war=None):
        mh = op("act", lambda e: e.activation(H, src, ACT.Copy), after, war)
        ml = op("dve", lambda e: e.tensor_tensor(L, src, H.bitcast(F32), ALU.subtract), mh, after, war)
        return [mh, ml]

    d_par = slot("par")
    pc = fl.dma(d_par, lambda e: e.dma_start(PC[:, :], t["cols"]))
    one = op("pool", lambda e: e.memset(ONE[:, :], 1.0))
    z1 = op("pool", lambda e: e.memset(IDT[:, :], 0.0))
    z2 = op("pool", lambda e: e.memset(CAU[:, :], 0.0))
    idt = op("pool", lambda e: e.affine_select(out=IDT[:, :], in_=IDT[:, :], compare_op=ALU.not_equal,
                                               fill=1.0, base=0, pattern=[[-1, 128]],
                                               channel_multiplier=1), z1)
    cau = op("pool", lambda e: e.affine_select(out=CAU[:, :], in_=CAU[:, :], compare_op=ALU.is_ge,
                                               fill=-1e30, base=0, pattern=[[-1, 128]],
                                               channel_multiplier=1), z2)

    dx = [slot(f"x{i}") for i in range(4)]
    xin = [fl.dma(dx[i], lambda e, i=i: e.dma_start(XS[:, 4 * i:4 * i + 4, :],
                                                    t["xT"][4 * i:4 * i + 4].rearrange("k p s -> p k s")))
           for i in range(4)]
    d_ssm = [slot(f"ssm{i}") for i in range(4)]

    def inv_rms(dst, b, mm, pre=None, sbt=(T[:, 2, :], T[:, 3, :])):
        v, y = sbt
        m = op("dve", lambda e: e.tensor_scalar(v, bank[b][:, :], 1.0 / 2048, None, ALU.mult), mm)
        free[b] = [m]
        if pre is not None:
            m = op("dve", lambda e: e.tensor_tensor(v, v, pre, ALU.mult), m)
            m = op("dve", lambda e: e.tensor_tensor(v, v, pre, ALU.mult), m)
        m = op("dve", lambda e: e.tensor_scalar(v, v, EPS, None, ALU.add), m)
        m = op("act", lambda e: e.activation(y, v, ACT.Sqrt), m)
        m = op("dve", lambda e: e.reciprocal(dst, y), m)
        m = op("dve", lambda e: e.tensor_tensor(y, dst, dst, ALU.mult), m)
        m = op("dve", lambda e: e.tensor_tensor(y, y, v, ALU.mult), m)
        m = op("dve", lambda e: e.tensor_scalar(y, y, -0.5, 1.5, ALU.mult, ALU.add), m)
        return op("dve", lambda e: e.tensor_tensor(dst, dst, y, ALU.mult), m)

    acc = None
    tfree = [None, None]
    for k in range(16):
        tk = T[:, k % 2, :]
        sq = op("act", lambda e, tk=tk, k=k: e.activation(tk, XS[:, k, :], ACT.Square), xin[k // 4], tfree[k % 2])
        if k == 0:
            acc = op("dve", lambda e, tk=tk: e.tensor_copy(SO[:, 0, :], tk), sq)
        else:
            acc = op("dve", lambda e, tk=tk: e.tensor_tensor(SO[:, 0, :], SO[:, 0, :], tk, ALU.add), sq, acc)
        tfree[k % 2] = acc
    mm = op("pe", lambda e: e.matmul(bank[0][:, :], ONE[:, :], SO[:, 0, :], start=True, stop=True), acc, one)
    rs = inv_rms(RS[:, 0, :], 0, mm)
    hready = []
    for k in range(16):
        x = XS[:, k, :]
        m = op("dve", lambda e, x=x, k=k: e.scalar_tensor_tensor(out=x, in0=x, scalar=col["g1"][:, k:k + 1],
                                                                 in1=RS[:, 0, :], op0=ALU.mult, op1=ALU.mult),
               rs, pc)
        hready.append(split(hH[:, k, :], hL[:, k, :], x, m))
    xs_free = hready[-1]
    ada["free"] = hready[-1]
    ada["c"] = op("act", lambda e: e.activation(SC[:, :], col["c2"], ACT.Silu), pc)

    dve_last = [None]

    def dv(fn, *after):
        dve_last[0] = op("dve", fn, dve_last[0], *after)
        return dve_last[0]

    def ts(o, a, s1, s2, o0, o1=None, *after):
        if o1 is None:
            return dv(lambda e: e.tensor_scalar(o, a, s1, None, o0), *after)
        return dv(lambda e: e.tensor_scalar(o, a, s1, s2, o0, o1), *after)

    def tt(o, a, b, o0, *after):
        return dv(lambda e: e.tensor_tensor(o, a, b, o0), *after)

    def stt(o, a, s, b, o0, o1, *after):
        return dv(lambda e: e.scalar_tensor_tensor(out=o, in0=a, scalar=s, in1=b, op0=o0, op1=o1), *after)

    def exp_steps(dst, x, n, r, sc, *after):
        ts(dst, x, -87.3, 88.7, ALU.max, ALU.min, *after)
        ts(n, dst, 1.4426950408889634, MAGIC, ALU.mult, ALU.add)
        ts(n, n, -MAGIC, None, ALU.add)
        stt(r, n, -0.693359375, dst, ALU.mult, ALU.add)
        stt(r, n, 2.12194440e-4, r, ALU.mult, ALU.add)
        yield 0.5
        ts(dst, r, 1.0 / 5040, None, ALU.mult)
        for c in (1.0 / 720, 1.0 / 120, 1.0 / 24, 1.0 / 6, 0.5, 1.0):
            stt(dst, dst, c, r, ALU.add, ALU.mult)
        yield 0.7
        ts(dst, dst, 1.0, None, ALU.add)
        ts(sc, n, 127.0, 8388608.0, ALU.add, ALU.mult)
        tt(dst, dst, sc.bitcast(F32), ALU.mult)
        stt(dst, x, -87.3, dst, ALU.is_gt, ALU.mult)
        yield 0.5

    def sm(i):
        return SM[:, i, :]

    SMI = at("SMI", 84 + 3.75, [128, 32], I32)

    ssm = {}

    def ssm_params():
        da = fl.dma(d_ssm[0], lambda e: e.dma_start(sm(0), t["are"]))
        db = fl.dma(d_ssm[1], lambda e: e.dma_start(sm(1), t["aim"]))
        dc = fl.dma(d_ssm[2], lambda e: e.dma_start(sm(2), t["ldt"]))
        d_c = slot("cr")
        fl.dma(d_c, lambda e: e.dma_start(CR[:, 0], t["cre"]))
        dcr = fl.dma(d_c, lambda e: e.dma_start(CR[:, 1], t["cim"]))
        fl.dma(d_ssm[3], lambda e: e.dma_start(BT[:, 0], t["bre"]))
        ssm["bt"] = fl.dma(d_ssm[3], lambda e: e.dma_start(BT[:, 1], t["bim"]))
        cz = op("pool", lambda e: e.memset(CB[:, :, :, :], 0.0))
        yield 0.1
        are, aim, ldt, dt, zr, zi, n, r, mag = (sm(i) for i in range(9))
        yield from exp_steps(dt, ldt, n, r, SMI[:, :], dc)
        tt(zr, are, dt, ALU.mult, da)
        tt(zi, aim, dt, ALU.mult, db)
        yield from exp_steps(mag, zr, n, r, SMI[:, :])
        m, y, q, y2, sn, cs, aq, sq_, t0 = (sm(i) for i in range(9, 18))
        ts(m, zi, 0.6366197723675814, MAGIC, ALU.mult, ALU.add)
        ts(m, m, -MAGIC, None, ALU.add)
        rest = np.pi / 2
        for i, bits in enumerate((7, 19, 30, 60)):
            part = float(np.floor(rest * 2.0 ** bits) / 2.0 ** bits) if i < 3 else float(rest)
            rest -= part
            stt(y, m, -part, zi if i == 0 else y, ALU.mult, ALU.add)
        ts(q, m, 0.25, MAGIC, ALU.mult, ALU.add)
        ts(q, q, -MAGIC, None, ALU.add)
        stt(q, q, -4.0, m, ALU.mult, ALU.add)
        yield 0.9
        tt(y2, y, y, ALU.mult)
        ts(sn, y2, 1.0 / 362880, None, ALU.mult)
        for c in (-1.0 / 5040, 1.0 / 120, -1.0 / 6):
            stt(sn, sn, c, y2, ALU.add, ALU.mult)
        stt(sn, sn, 1.0, y, ALU.add, ALU.mult)
        ts(cs, y2, -1.0 / 3628800, None, ALU.mult)
        for c in (1.0 / 40320, -1.0 / 720, 1.0 / 24, -0.5):
            stt(cs, cs, c, y2, ALU.add, ALU.mult)
        ts(cs, cs, 1.0, None, ALU.add)
        yield 1.3
        stt(aq, q, -1.0, q, ALU.mult, ALU.max)
        ts(t0, aq, -1.0, 2.0, ALU.mult, ALU.add)
        tt(sq_, t0, q, ALU.mult)
        ts(aq, aq, -1.0, 1.0, ALU.mult, ALU.add)
        sinz, cosz, t1, t2 = (sm(i) for i in range(18, 22))
        tt(t1, sn, aq, ALU.mult)
        tt(t2, cs, sq_, ALU.mult)
        tt(sinz, t1, t2, ALU.add)
        tt(t1, cs, aq, ALU.mult)
        tt(t2, sn, sq_, ALU.mult)
        tt(cosz, t1, t2, ALU.subtract)
        yield 1.0
        lr, li, fr, fi, den = (sm(i) for i in range(22, 27))
        tt(lr, mag, cosz, ALU.mult)
        ts(lr, lr, -1.0, None, ALU.add)
        tt(li, mag, sinz, ALU.mult)
        tt(den, are, are, ALU.mult)
        tt(t1, aim, aim, ALU.mult)
        tt(den, den, t1, ALU.add)
        dv(lambda e: e.reciprocal(den, den))
        tt(t1, lr, are, ALU.mult)
        tt(t2, li, aim, ALU.mult)
        tt(t1, t1, t2, ALU.add)
        tt(fr, t1, den, ALU.mult)
        tt(t1, li, are, ALU.mult)
        tt(t2, lr, aim, ALU.mult)
        tt(t1, t1, t2, ALU.subtract)
        tt(fi, t1, den, ALU.mult)
        yield 1.6
        t3, t4 = V[:, 0, :].rearrange("p (j c) -> p j c", c=16), V[:, 1, :].rearrange("p (j c) -> p j c", c=16)
        frb = fr.unsqueeze(2).to_broadcast([128, 32, 16])
        fib = fi.unsqueeze(2).to_broadcast([128, 32, 16])
        tt(t3, CR[:, 0], frb, ALU.mult, dcr, xs_free)
        tt(t4, CR[:, 1], fib, ALU.mult)
        for g in range(2):
            p = slice(64 * g, 64 * g + 64)
            tt(CB[p, 0, :, 16 * g:16 * g + 16], t3[p], t4[p], ALU.subtract, cz)
        tt(t3, CR[:, 0], fib, ALU.mult)
        tt(t4, CR[:, 1], frb, ALU.mult)
        yield 3.0
        tt(t3, t3, t4, ALU.add)
        for g in range(2):
            p = slice(64 * g, 64 * g + 64)
            ts(CB[p, 1, :, 16 * g:16 * g + 16], t3[p], -1.0, None, ALU.mult)
        ssm["cb"] = dve_last[0]
        yield 1.2
        pr, pi, nr, ni = (sm(i) for i in range(27, 30)), None, None, None
        pr, pi, nr = pr
        ni = sm(0)
        tmp = V[:, 2:4, :].rearrange("p a (j n) -> p (a j) n", n=16)[:, 0:32, :]
        tmp2 = V[:, 4:6, :].rearrange("p a (j n) -> p (a j) n", n=16)[:, 0:32, :]
        dv(lambda e: e.tensor_copy(pr, cosz))
        dv(lambda e: e.tensor_copy(pi, sinz))
        for big, levels in ((E0, 5), (W0, 4)):
            dv(lambda e, big=big: e.memset(big[:, 0, :, 0:1], 1.0))
            dv(lambda e, big=big: e.memset(big[:, 1, :, 0:1], 0.0))
            for lv in range(levels):
                w = 1 << lv
                a_r, a_i = big[:, 0, :, 0:w], big[:, 1, :, 0:w]
                o_r, o_i = big[:, 0, :, w:2 * w], big[:, 1, :, w:2 * w]
                b_r = pr.unsqueeze(2).to_broadcast([128, 32, w])
                b_i = pi.unsqueeze(2).to_broadcast([128, 32, w])
                x1_, x2_ = tmp[:, :, 0:w], tmp2[:, :, 0:w]
                tt(x1_, a_r, b_r, ALU.mult)
                tt(x2_, a_i, b_i, ALU.mult)
                tt(o_r, x1_, x2_, ALU.subtract)
                tt(x1_, a_r, b_i, ALU.mult)
                tt(x2_, a_i, b_r, ALU.mult)
                tt(o_i, x1_, x2_, ALU.add)
                yield 0.5 + 0.2 * w
                tt(t1, pr, pr, ALU.mult)
                tt(t2, pi, pi, ALU.mult)
                tt(nr, pr, pi, ALU.mult)
                tt(pr, t1, t2, ALU.subtract)
                ts(pi, nr, 2.0, None, ALU.mult)
                yield 0.5
        ssm["turn"] = dve_last[0]
        ssm["mag"] = mag

    uready = [None] * 8
    ssm["y"] = [None] * 8

    def ssm_tiles():
        mag = ssm["mag"]
        tabfree, hfree, tab, hm = [None] * 2, [None] * 2, {}, {}
        bufree = [None, None]
        bu = {}

        def table(j):
            b = j % 2
            er = E0[:, 0, j:j + 1, :].to_broadcast([128, 16, 32])
            ei = E0[:, 1, j:j + 1, :].to_broadcast([128, 16, 32])
            wr = W0[:, 0, j, :].unsqueeze(2).to_broadcast([128, 16, 32])
            wi = W0[:, 1, j, :].unsqueeze(2).to_broadcast([128, 16, 32])
            c = TAB[:, b, 0, :].rearrange("p (a i) -> p a i", i=32)
            s = TAB[:, b, 1, :].rearrange("p (a i) -> p a i", i=32)
            x1_ = T[:, 2, :].rearrange("p (a i) -> p a i", i=32)
            x2_ = T[:, 3, :].rearrange("p (a i) -> p a i", i=32)
            P = "pool"
            m = op(P, lambda e: e.tensor_tensor(c, er, wr, ALU.mult), ssm["turn"], tabfree[b])
            m2 = op(P, lambda e: e.tensor_tensor(x1_, ei, wi, ALU.mult), tab.get(j - 1))
            m = op(P, lambda e: e.tensor_tensor(c, c, x1_, ALU.subtract), m, m2)
            m3 = op(P, lambda e: e.tensor_tensor(s, er, wi, ALU.mult))
            m4 = op(P, lambda e: e.tensor_tensor(x2_, ei, wr, ALU.mult))
            tab[j] = op(P, lambda e: e.tensor_tensor(s, s, x2_, ALU.add), m3, m4)

        def products(j):
            ut, i = j // 4, j % 4
            p = slice(32 * i, 32 * i + 32)
            b = 4 + 2 * (j % 2)
            for z in range(2):
                bu[j] = op("pe", lambda e, z=z: e.matmul(bank[b + z][:, :], BT[p, z, ut, :], U[p, ut, :],
                                                         start=True, stop=True),
                           ssm["bt"], uready[ut], bufree[j % 2])

        def readout(j):
            ut, i = j // 4, j % 4
            o = bank[3][32 * i:32 * i + 32, :]
            quiet("pe", lambda e: e.matmul(o, CB[:, 0, j, :], HH[:, j % 2, 0, :], start=True, stop=False),
                  hm[j], ssm["cb"], free[3])
            hfree[j % 2] = op("pe", lambda e: e.matmul(o, CB[:, 1, j, :], HH[:, j % 2, 1, :],
                                                       start=False, stop=True))

        def skip_term(ut):
            m = op("dve", lambda e: e.scalar_tensor_tensor(out=U[:, ut, :], in0=U[:, ut, :],
                                                           scalar=col["dsk"][:, ut:ut + 1], in1=bank[3][:, :],
                                                           op0=ALU.mult, op1=ALU.add), hfree[1])
            free[3] = [m]
            ssm["y"][ut] = m

        table(0)
        products(0)
        yield 0.1
        for j in range(32):
            if j + 1 < 32:
                table(j + 1)
                products(j + 1)
            c, s = TAB[:, j % 2, 0, :], TAB[:, j % 2, 1, :]
            br, bi = bank[4 + 2 * (j % 2)][:, :], bank[5 + 2 * (j % 2)][:, :]
            v = [V[:, i, :] for i in range(6)]
            a = op("dve", lambda e: e.tensor_tensor(v[0], c, br, ALU.mult), tab[j], bu[j], dve_last[0])
            b = op("dve", lambda e: e.tensor_tensor(v[1], s, bi, ALU.mult))
            yield 1.2
            c2 = op("dve", lambda e: e.tensor_tensor(v[2], c, bi, ALU.mult))
            d = op("dve", lambda e: e.tensor_tensor(v[3], s, br, ALU.mult))
            bufree[j % 2] = d
            yield 1.2
            a = op("dve", lambda e: e.tensor_tensor(v[4], v[0], v[1], ALU.add), a, b)
            b = op("dve", lambda e: e.tensor_tensor(v[5], v[2], v[3], ALU.subtract), c2, d)
            yield 1.2
            rb = mag[:, j:j + 1].to_broadcast([128, 512])
            a = op("dve", lambda e: e.tensor_tensor_scan(v[0], rb, v[4], 0.0, ALU.mult, ALU.add), a)
            yield 1.1
            b = op("dve", lambda e: e.tensor_tensor_scan(v[1], rb, v[5], 0.0, ALU.mult, ALU.add), b)
            yield 1.1
            if j >= 1 and j % 4 == 0:
                skip_term(j // 4 - 1)
                yield 0.6
            hr, hi = HH[:, j % 2, 0, :], HH[:, j % 2, 1, :]
            c2 = op("dve", lambda e: e.tensor_tensor(v[2], c, v[0], ALU.mult), a)
            d = op("dve", lambda e: e.tensor_tensor(v[3], s, v[1], ALU.mult), b)
            yield 1.2
            f = op("dve", lambda e: e.tensor_tensor(v[4], s, v[0], ALU.mult))
            g = op("dve", lambda e: e.tensor_tensor(v[5], c, v[1], ALU.mult))
            tabfree[j % 2] = g
            yield 1.2
            op("dve", lambda e: e.tensor_tensor(hr, v[2], v[3], ALU.subtract), c2, d, hfree[j % 2])
            hm[j] = op("dve", lambda e: e.tensor_tensor(hi, v[4], v[5], ALU.add), f, g, hfree[j % 2])
            dve_last[0] = hm[j]
            yield 4.0
            debt[0] += 2.8
            readout(j)
        yield 3.0
        skip_term(7)

    BUDGET["v"] = 3.2
    beside.append(ssm_params())
    for m in range(8):
        b = next_bank()
        mk = project(b, 2, hH, hL, hready)
        uready[m] = op("act", lambda e, m=m, b=b: e.activation(U[:, m, :], bank[b][:, :], ACT.Copy), mk)
        free[b] = [uready[m]]
        pump(BUDGET["v"])
    while beside:
        pump(1.0)
    beside.append(ssm_tiles())
    so = [slot(f"so{i}") for i in range(2)]
    so_free = [None, None]
    so_n = [0]

    def spill(func, b, mk, dst):
        i = so_n[0] % 2
        so_n[0] += 1
        m = op("act", lambda e: e.activation(SO[:, i, :], bank[b][:, :], func), mk, so_free[i], acc)
        free[b] = [m]
        so_free[i] = fl.dma(so[i], lambda e: e.dma_start(dst, SO[:, i, :]), m)
        return so_free[i]

    stored = {}
    for m in range(8):
        b = next_bank()
        mk = project(b, 2, hH, hL, hready)
        stored["zb", m] = spill(ACT.Silu, b, mk, scratch["zb"][m])
        pump(BUDGET["v"])
    for m in range(32):
        b = next_bank()
        mk = project(b, 2, hH, hL, hready)
        which, i = ("ga", m) if m < 16 else ("gb", m - 16)
        stored[which, i] = spill(ACT.Sigmoid, b, mk, scratch[which][i])
        pump(BUDGET["v"])
    drain_beside()
    ssm_done = [ssm["y"][7], hm_last(fl)]

    cvz = op("dve", lambda e: e.memset(CV[:, 0:2], 0.0))
    aready = []
    t1free = t0free = t2free = None
    for c in range(16):
        cv, cg, bg, za = None, None, None, None
        b = next_bank()
        mk = project(b, 2, hH, hL, hready)
        v_ = op("act", lambda e, b=b: e.activation(T[:, 0, :], bank[b][:, :], ACT.Copy), mk, t0free)
        free[b] = [v_]
        b = next_bank()
        mk = project(b, 2, hH, hL, hready)
        m = op("dve", lambda e, b=b: e.tensor_tensor(CV[:, 2:514], bank[b][:, :], T[:, 0, :], ALU.mult), mk, v_)
        t0free = m
        free[b] = [m]

        def w(i, c=c):
            return col["cw"][:, 16 * i + c:16 * i + c + 1]

        o = T[:, 1, :]
        m = op("dve", lambda e, o=o, w=w: e.tensor_scalar(o, CV[:, 0:512], w(0), None, ALU.mult), m, cvz, t1free)
        m = op("dve", lambda e, o=o, w=w: e.scalar_tensor_tensor(out=o, in0=CV[:, 1:513], scalar=w(1), in1=o,
                                                                 op0=ALU.mult, op1=ALU.add), m)
        m = op("dve", lambda e, o=o, w=w: e.scalar_tensor_tensor(out=o, in0=CV[:, 2:514], scalar=w(2), in1=o,
                                                                 op0=ALU.mult, op1=ALU.add), m)
        b = next_bank()
        mk = project(b, 2, hH, hL, hready)
        m = op("dve", lambda e, b=b, o=o: e.tensor_tensor(o, o, bank[b][:, :], ALU.mult), mk, m)
        free[b] = [m]
        b = next_bank()
        mk = project(b, 2, hH, hL, hready)
        z = op("act", lambda e, b=b: e.activation(T[:, 2, :], bank[b][:, :], ACT.Silu), mk, t2free, ssm_done)
        free[b] = [z]
        m = op("dve", lambda e, o=o: e.tensor_tensor(o, o, T[:, 2, :], ALU.mult), m, z)
        t2free = m
        aready.append(split(AH[:, c, :], AL[:, c, :], o, m, ssm_done))
        t1free = aready[-1]

    ybready = [None] * 8

    def yb_parts():
        gl = []
        for i in range(8):
            gl.append(op("act", lambda e, i=i: e.activation(U[:, i, :], U[:, i, :], ACT.Gelu_apprx_tanh),
                         ssm["y"][i]))
        yield 4.0
        for i in range(8):
            ybready[i] = split(ybH[:, i, :], ybL[:, i, :], U[:, i, :], gl[i], mk_h)
            yield 1.2

    mk_h = mk
    beside.append(yb_parts())
    si = [slot(f"si{i}") for i in range(2)]
    si_free = [None, None]
    si_n = [0]

    def load(src, after=None):
        i = si_n[0] % 2
        si_n[0] += 1
        return i, SI[:, i, :], fl.dma(si[i], lambda e: e.dma_start(SI[:, i, :], src), after, si_free[i])

    BUDGET["v"] = 3.0
    ma = []
    for d in range(16):
        i, s_, ld = load(scratch["ga"][d], stored["ga", d])
        b = next_bank()
        mk = project(b, 2, AH, AL, aready)
        m = op("dve", lambda e, b=b, d=d, s_=s_: e.tensor_tensor(MA[:, d, :], bank[b][:, :], s_, ALU.mult), mk, ld)
        free[b] = [m]
        si_free[i] = m
        ma.append(m)
        pump(BUDGET["v"])
    drain_beside()
    mk_a = mk

    bready = []
    tf = [None, None]
    for g in range(8):
        i, s_, ld = load(scratch["zb"][g], stored["zb", g])
        b = next_bank()
        mk = project(b, 1, ybH, ybL, ybready)
        o = T[:, g % 2, :]
        m = op("act", lambda e, b=b, g=g, o=o: e.activation(o, bank[b][:, :], ACT.Sigmoid,
                                                            bias=col["bglu"][:, g:g + 1]), mk, tf[g % 2])
        free[b] = [m]
        m = op("dve", lambda e, g=g, o=o: e.tensor_tensor(o, o, U[:, g, :], ALU.mult), m)
        m = op("dve", lambda e, o=o, s_=s_: e.tensor_tensor(o, o, s_, ALU.mult), m, ld)
        si_free[i] = m
        bready.append(split(BH[:, g, :], BL[:, g, :], o, m, mk_a))
        tf[g % 2] = bready[-1]
    mk_g = mk

    mready = []
    for d in range(16):
        i, s_, ld = load(scratch["gb"][d], stored["gb", d])
        b = next_bank()
        mk = project(b, 1, BH, BL, bready)
        o = T[:, d % 2, :]
        m = op("dve", lambda e, b=b, o=o, s_=s_: e.tensor_tensor(o, bank[b][:, :], s_, ALU.mult), mk, ld, tf[d % 2])
        free[b] = [m]
        si_free[i] = m
        m = op("dve", lambda e, o=o, d=d: e.tensor_tensor(o, o, MA[:, d, :], ALU.add), m, ma[d])
        mready.append(split(mH[:, d, :], mL[:, d, :], o, m, [mk_a, mk_g]))
        tf[d % 2] = mready[-1]

    a1, a2 = SO[:, 0, :], SO[:, 1, :]
    x1raw, s1, s2 = [], None, None
    tq = [None, None]
    for d in range(16):
        i, s_, ld = load(t["xT"][d])
        b = next_bank()
        mk = project(b, 2, mH, mL, mready)
        x = X1[:, d, :]
        m = op("dve", lambda e, b=b, x=x, s_=s_: e.tensor_tensor(x, bank[b][:, :], s_, ALU.add), mk, ld)
        free[b] = [m]
        si_free[i] = m
        x1raw.append(m)
        q1 = op("act", lambda e, x=x: e.activation(T[:, 2, :], x, ACT.Square), m, tq[0])
        q2 = op("act", lambda e, x=x, d=d: e.activation(T[:, 3, :], x, ACT.Square, scale=col["fg"][:, d:d + 1]),
                m, tq[1])
        if d == 0:
            s1 = op("dve", lambda e: e.tensor_copy(a1, T[:, 2, :]), q1, so_free)
            s2 = op("dve", lambda e: e.tensor_copy(a2, T[:, 3, :]), q2, so_free)
        else:
            s1 = op("dve", lambda e: e.tensor_tensor(a1, a1, T[:, 2, :], ALU.add), q1, s1)
            s2 = op("dve", lambda e: e.tensor_tensor(a2, a2, T[:, 3, :], ALU.add), q2, s2)
        tq = [s1, s2]
    mk_o = mk
    m1 = op("pe", lambda e: e.matmul(bank[3][:, :], ONE[:, :], a1, start=True, stop=True), s1, free[3])
    m2 = op("pe", lambda e: e.matmul(bank[4][:, :], ONE[:, :], a2, start=True, stop=True), s2, ssm_done)
    r1 = inv_rms(RS[:, 0, :], 3, m1)
    r2 = inv_rms(RS[:, 1, :], 4, m2, pre=RS[:, 0, :])

    g2s = ST[:, 0:16]
    gm = op("dve", lambda e: e.tensor_scalar(g2s, MOD[:, 16:32], 1.0, None, ALU.add), ada["mod"])
    gm = op("dve", lambda e: e.tensor_tensor(g2s, g2s, col["g2"], ALU.mult), gm)
    h2ready, x1out = [], []
    dx1 = [slot(f"dx1{i}") for i in range(2)]
    tf = [None, None]
    for k in range(16):
        x, o = X1[:, k, :], T[:, k % 2, :]
        m = op("dve", lambda e, x=x, k=k: e.scalar_tensor_tensor(out=x, in0=x, scalar=col["fg"][:, k:k + 1],
                                                                 in1=RS[:, 0, :], op0=ALU.mult, op1=ALU.mult),
               r1, x1raw[k], q2)
        x1out.append(fl.dma(dx1[k % 2], lambda e, x=x, k=k: e.dma_start(scratch["x1"][k], x), m,
                            x1out[k - 2] if k >= 2 else None))
        m = op("dve", lambda e, x=x, k=k, o=o: e.scalar_tensor_tensor(out=o, in0=x, scalar=g2s[:, k:k + 1],
                                                                      in1=RS[:, 1, :], op0=ALU.mult, op1=ALU.mult),
               r2, gm, m, tf[k % 2])
        m = op("act", lambda e, k=k, o=o: e.activation(o, o, ACT.Identity, bias=MOD[:, k:k + 1]), m)
        h2ready.append(split(h2H[:, k, :], h2L[:, k, :], o, m, mk_o))
        tf[k % 2] = h2ready[-1]
    h2_all = tf

    WF = at("WF", 0, [128, 16, 16])
    WFH, WFL = at("WFH", 1, [128, 16, 16], F32R), at("WFL", 2, [128, 16, 16], F32R)
    dwf = slot("wf")
    wf = fl.dma(dwf, lambda e: e.dma_start(WF[:, :, :], t["wf"]), x1out, h2_all)
    wfp = split(WFH[:, :, :], WFL[:, :, :], WF[:, :, :], wf, [x1out[-1], x1out[-2], h2_all])
    fps = bank[3][0:16, :]
    for k in range(16):
        f_, l_ = k == 0, k == 15
        quiet("pe", lambda e, k=k, f_=f_: e.matmul(bank[3][0:128, :] if False else fps, WFH[:, k, :], h2H[:, k, :],
                                                   start=f_, stop=False), wfp, h2ready[k], free[3])
        quiet("pe", lambda e, k=k: e.matmul(fps, WFH[:, k, :], h2L[:, k, :], start=False, stop=False))
        if l_:
            fm = op("pe", lambda e, k=k: e.matmul(fps, WFL[:, k, :], h2H[:, k, :], start=False, stop=True))
        else:
            quiet("pe", lambda e, k=k: e.matmul(fps, WFL[:, k, :], h2H[:, k, :], start=False, stop=False))
    EI = at("EI", 196, [16, 512], I32)
    nf = {}

    def forget():
        x, a, b_, c_ = (T[0:16, i, :] for i in range(4))
        n16, e16 = RS[0:16, 0, :], RS[0:16, 1, :]
        bf = col["bf"][0:16, 0:1]
        m = ts(x, fps, bf, None, ALU.add, None, fm, h2_all)
        free[3] = [m]
        stt(a, x, -1.0, x, ALU.mult, ALU.min)
        yield 1.0
        yield from exp_steps(b_, a, n16, c_, EI[:, :])
        yield 8.0
        ts(a, b_, 2.0, None, ALU.add)
        dv(lambda e: e.reciprocal(a, a))
        tt(a, a, b_, ALU.mult)
        tt(c_, a, a, ALU.mult)
        yield 3.0
        ts(b_, c_, 1.0 / 15, None, ALU.mult)
        for n in (13, 11, 9, 7, 5, 3):
            stt(b_, b_, 1.0 / n, c_, ALU.add, ALU.mult)
            yield 0.7
        stt(b_, b_, 1.0, a, ALU.add, ALU.mult)
        ts(x, x, 0.0, None, ALU.min)
        stt(x, b_, -2.0, x, ALU.mult, ALU.add)
        yield 2.0
        ts(x, x, -1.0, None, ALU.mult)
        ones = ONE[0:16, 0:1].to_broadcast([16, 512])
        nf["m"] = dv(lambda e: e.tensor_tensor_scan(NF[:, :], ones, x, 0.0, ALU.mult, ALU.add))
        yield 1.6

    def seq_project(half, dst, func, war):
        bs = [0, 1, 2, 7]
        for kc in range(8):
            n, s, m = chunk()
            for k2 in range(2):
                k = 2 * kc + k2
                wh, wl = WH[:, s, 512 * k2:512 * k2 + 512], WL[:, s, 512 * k2:512 * k2 + 512]
                for q in range(4):
                    b = bs[q]
                    o = slice(128 * q, 128 * q + 128)
                    quiet("pe", lambda e, b=b, o=o, k=k, wh=wh: e.matmul(bank[b][:, :], h2H[:, k, o], wh,
                                                                         start=k == 0, stop=False),
                          m, h2ready[k], free[b] if k == 0 else None)
                    quiet("pe", lambda e, b=b, o=o, k=k, wl=wl: e.matmul(bank[b][:, :], h2H[:, k, o], wl,
                                                                         start=False, stop=False))
                    mark = op("pe", lambda e, b=b, o=o, k=k, wh=wh: e.matmul(bank[b][:, :], h2L[:, k, o], wh,
                                                                             start=False, stop=k == 15))
                    if k == 15:
                        ev = op("act", lambda e, b=b, q=q: e.activation(
                            dst[:, q, 512 * half:512 * half + 512], bank[b][:, :], func), mark, war)
                        free[b] = [ev]
            used[n] = mark
            pump(BUDGET["v"])
        return ev

    free[7] = [*free[7], *ssm_done] if False else ssm_done
    free[5] = free[6] = free[4] = [*ssm_done, r2]
    BUDGET["v"] = 3.0
    beside.append(forget())
    seq_project(0, VV, ACT.Copy, mk_g)
    vb = seq_project(1, VV, ACT.Copy, mk_g)
    drain_beside()

    dka = [slot(f"ka{i}") for i in range(2)]
    qa1 = op("pool", lambda e: e.memset(QA[64:65, :, :, :], 1.0), wfp, x1out[-1], x1out[-2], fm)
    att_free = [None, None]
    prfree = [None]
    ptfree = [None]
    AB = [4, 5, 6, 7]
    yready = {}
    stat = {"n": 0}

    finished = set()

    def attend(j, ready, gate):
        buf = j % 2
        osum = None
        for hh in range(2):
            h = 2 * j + hh
            p = slice(0, 65)
            den = []
            tops = []
            for q in range(4):
                w = 128 * (q + 1)
                b = AB[q]
                mm = op("pe", lambda e, q=q, w=w, b=b: e.matmul(bank[b][:, 0:w], QA[p, buf, hh, 128 * q:128 * q + 128],
                                                                KA[p, buf, hh, 0:w], start=True, stop=True),
                        ready, free[b])
                den.append(mm)
            if hh == 1:
                att_free[buf] = mm
            probs = []
            for q in range(4):
                w = 128 * (q + 1)
                b = AB[q]
                i = stat["n"] % 8
                stat["n"] += 1
                nm, rsum = ST[:, 16 + i:17 + i], ST[:, 24 + i:25 + i]
                m = op("dve", lambda e, b=b, w=w: e.tensor_tensor(bank[b][:, w - 128:w], bank[b][:, w - 128:w],
                                                                  CAU[:, :], ALU.add), den[q], cau)
                m = op("dve", lambda e, b=b, w=w, nm=nm: e.tensor_reduce(nm, bank[b][:, 0:w], AX, ALU.max,
                                                                         negate=True), m)
                m = op("act", lambda e, b=b, w=w, nm=nm, rsum=rsum, q=q: e.activation(
                    PR[:, q, 0:w], bank[b][:, 0:w], ACT.Exp, bias=nm, accum_out=rsum), m, prfree[0])
                free[b] = [m]
                m = op("dve", lambda e, rsum=rsum: e.reciprocal(rsum, rsum), m)
                m = op("dve", lambda e, q=q, w=w, rsum=rsum: e.tensor_scalar(PR[:, q, 0:w], PR[:, q, 0:w], rsum,
                                                                             None, ALU.mult), m)
                probs.append(m)
                yield 1.0
            yield 1.5
            yield 3.0
            pts = []
            for kt in range(4):
                b = AB[kt]
                for q in range(kt, 4):
                    mm = op("pe", lambda e, kt=kt, q=q, b=b: e.transpose(
                        bank[b][:, 128 * q:128 * q + 128], PR[:, q, 128 * kt:128 * kt + 128], IDT[:, :]),
                        probs[q], idt, free[b])
                c0 = 128 * kt
                who = "act" if kt % 2 == 0 else "dve"
                if who == "act":
                    m = op("act", lambda e, b=b, c0=c0, kt=kt: e.activation(PT[:, kt, c0:512], bank[b][:, c0:512],
                                                                            ACT.Copy), mm, ptfree[0])
                else:
                    m = op("dve", lambda e, b=b, c0=c0, kt=kt: e.tensor_copy(PT[:, kt, c0:512], bank[b][:, c0:512]),
                           mm, ptfree[0])
                free[b] = [m]
                pts.append(m)
            prfree[0] = mm
            yield 1.0
            yield 3.0
            o = bank[3][64 * hh:64 * hh + 64, :]
            for kt in range(4):
                c0 = 128 * kt
                mm = op("pe", lambda e, kt=kt, c0=c0, o=o, h=h: e.matmul(
                    o[:, c0:512], VV[:, kt, 64 * h:64 * h + 64], PT[:, kt, c0:512], start=kt == 0, stop=kt == 3,
                    skip_group_check=True), pts[kt], vb, free[3] if hh == 0 else None)
            ptfree[0] = mm
        m = op("dve", lambda e: e.tensor_tensor(YF[:, 8 + j, :], gate[0], bank[3][:, :], ALU.mult), mm, gate[1])
        free[3] = [m]
        gate_free[buf] = m
        yready[8 + j] = m
        finished.add(j)
        yield 0.7

    gate_free = [None, None]
    BUDGET["v"] = 3.2
    kaF = None
    for j in range(8):
        buf = j % 2
        b = next_bank()
        mk = project(b, 2, h2H, h2L, h2ready)
        while j >= 2 and j - 2 not in finished:
            pump(1.0)
        ms = []
        for hh in range(2):
            ms.append(op("act", lambda e, b=b, hh=hh: e.activation(QA[0:64, buf, hh, :], bank[b][64 * hh:64 * hh + 64, :],
                                                                   ACT.Copy, scale=0.125),
                         mk, att_free[buf], qa1, wfp, fm, x1out[-1], x1out[-2]))
        free[b] = [ms[-1]]
        pump(BUDGET["v"])
        b = next_bank()
        mk = project(b, 2, h2H, h2L, h2ready)
        for hh in range(2):
            ms.append(op("act", lambda e, b=b, hh=hh: e.activation(KA[0:64, buf, hh, :], bank[b][64 * hh:64 * hh + 64, :],
                                                                   ACT.Copy), mk, att_free[buf], x1out[-1], x1out[-2]))
        free[b] = [ms[-1]]
        for hh in range(2):
            kd = fl.dma(dka[buf], lambda e, hh=hh, buf=buf, j=j: e.dma_start(KA[64:65, buf, hh, :],
                                                                             NF[2 * j + hh:2 * j + hh + 1, :]),
                        nf["m"], att_free[buf], x1out[-1], x1out[-2], kaF)
        pump(BUDGET["v"])
        b = next_bank()
        mk = project(b, 2, h2H, h2L, h2ready)
        g_ = T[:, buf, :]
        gt = op("act", lambda e, b=b, g_=g_: e.activation(g_, bank[b][:, :], ACT.Silu), mk, gate_free[buf], nf["m"])
        free[b] = [gt]
        pump(BUDGET["v"])
        beside.append(attend(j, [*ms, kd, qa1], (g_, gt)))
    att_done = None

    def wait_attention():
        drain_beside()

    SGU = {}
    VVx = at("VVx", 12, [128, 4, 1024])
    wait_attention()
    att_done = [mm_last(fl), free[3][0]]
    va1 = seq_project(0, VV, ACT.Gelu, att_done)

    def sgu_const():
        d = slot("ws")
        fl.dma(d, lambda e: e.dma_start(WS[:, :, :], t["wsT"]), att_done)
        ld = fl.dma(d, lambda e: e.dma_start(BSB[:, :, :], t["bsb"]), att_done)
        for h in range(8):
            SGU["w", h] = op("pool", lambda e, h=h: e.affine_select(
                out=WS[:, h, :], in_=WS[:, h, :], compare_op=ALU.is_ge, fill=0.0, base=0,
                pattern=[[1, 128]], channel_multiplier=-1), ld)
        yield 2.0
        for h in range(8):
            b = 4 + h // 4
            mm = op("pe", lambda e, h=h, b=b: e.matmul(bank[b][:, 128 * (h % 4):128 * (h % 4) + 128], ONE[:, :],
                                                       WS[:, h, :], start=h % 4 == 0, stop=h % 4 == 3,
                                                       skip_group_check=True), SGU["w", h], free[b])
            if h % 4 == 3:
                for g in range(h - 3, h + 1):
                    m = op("dve", lambda e, g=g, b=b: e.scalar_tensor_tensor(
                        out=CON[:, g, :], in0=bank[b][:, 128 * (g % 4):128 * (g % 4) + 128],
                        scalar=col["lnb"][:, g:g + 1], in1=BSB[:, g, :], op0=ALU.mult, op1=ALU.add), mm, ld,
                        att_done)
                    SGU["c", g] = m
                free[b] = [m]
                yield 2.0

    beside.append(sgu_const())
    va2 = seq_project(1, VV, ACT.Gelu, att_done)
    lnm = []

    def layer_norm():
        for q in range(4):
            x = VV[:, q, :]
            mu, va, rr, yy = (ST[:, 32 + 4 * q + i:33 + 4 * q + i] for i in range(4))
            m = op("dve", lambda e, x=x, mu=mu: e.tensor_reduce(mu, x, AX, ALU.add), va1, va2)
            m = op("dve", lambda e, mu=mu: e.tensor_scalar(mu, mu, 1.0 / 1024, None, ALU.mult), m)
            m = op("dve", lambda e, x=x, mu=mu: e.tensor_scalar(x, x, mu, None, ALU.subtract), m)
            s = op("act", lambda e, x=x, va=va: e.activation(SQ[:, :], x, ACT.Square, accum_out=va), m,
                   lnm[-1] if lnm else None, att_done)
            yield 2.0
            m = op("dve", lambda e, va=va: e.tensor_scalar(va, va, 1.0 / 1024, EPS, ALU.mult, ALU.add), s)
            m = op("act", lambda e, va=va, yy=yy: e.activation(yy, va, ACT.Sqrt), m)
            m = op("dve", lambda e, rr=rr, yy=yy: e.reciprocal(rr, yy), m)
            m = op("dve", lambda e, rr=rr, yy=yy: e.tensor_tensor(yy, rr, rr, ALU.mult), m)
            m = op("dve", lambda e, va=va, yy=yy: e.tensor_tensor(yy, yy, va, ALU.mult), m)
            m = op("dve", lambda e, yy=yy: e.tensor_scalar(yy, yy, -0.5, 1.5, ALU.mult, ALU.add), m)
            m = op("dve", lambda e, rr=rr, yy=yy: e.tensor_tensor(rr, rr, yy, ALU.mult), m)
            lnm.append(op("dve", lambda e, x=x, rr=rr: e.tensor_scalar(x, x, rr, None, ALU.mult), m))
            yield 2.0

    beside.append(layer_norm())
    mixed = {}

    def mix(h):
        b = 5 + h % 2
        for q in range(4):
            mm = op("pe", lambda e, h=h, q=q, b=b: e.matmul(
                bank[b][:, 128 * q:128 * q + 128], VV[:, q, 128 * h:128 * h + 128], WS[:, h, :],
                start=q == 0, stop=q == 3, skip_group_check=True), lnm, SGU["w", h], free[b])
        mixed[h] = mm

    sgfree = [None, None]
    for h in range(8):
        b = next_bank()
        mk = project(b, 2, h2H, h2L, h2ready)
        u_ = T[:, 0, :]
        mu_ = op("act", lambda e, b=b: e.activation(T[:, 0, :], bank[b][:, :], ACT.Gelu), mk, sgfree[0])
        free[b] = [mu_]
        pump(5.0)
        if h == 0:
            drain_beside()
        b = next_bank()
        mk = project(b, 2, h2H, h2L, h2ready)
        mg_ = op("act", lambda e, b=b: e.activation(T[:, 1, :], bank[b][:, :], ACT.Silu), mk, sgfree[1])
        free[b] = [mg_]
        if h == 0:
            mix(0)
        if h + 1 < 8:
            mix(h + 1)
        y = YF[:, h, :].rearrange("p (n t) -> p n t", t=128)
        bb = 5 + h % 2
        m = op("dve", lambda e, y=y, h=h, bb=bb: e.scalar_tensor_tensor(
            out=y, in0=bank[bb][:, :].rearrange("p (n t) -> p n t", t=128), scalar=col["lng"][:, h:h + 1],
            in1=CON[:, h:h + 1, :].to_broadcast([128, 4, 128]), op0=ALU.mult, op1=ALU.add),
            mixed[h], SGU["c", h])
        free[bb] = [m]
        m = op("dve", lambda e, h=h: e.tensor_tensor(YF[:, h, :], YF[:, h, :], T[:, 0, :], ALU.mult), m, mu_)
        sgfree[0] = m
        m = op("dve", lambda e, h=h: e.tensor_tensor(YF[:, h, :], YF[:, h, :], T[:, 1, :], ALU.mult), m, mg_)
        sgfree[1] = m
        yready[h] = m
    mk_p = mk

    ysplit = [split(yH[:, k, :], yL[:, k, :], YF[:, k, :], yready[k], mk_p) for k in range(16)]
    acc = None
    mixd = mixed[7]
    x2 = []
    tq = [None, None]
    for d in range(16):
        i, s_, ld = load(scratch["x1"][d], x1out)
        b = next_bank()
        mk = project(b, 2, yH, yL, ysplit)
        x = X2[:, d, :]
        m = op("dve", lambda e, b=b, x=x, d=d, s_=s_: e.scalar_tensor_tensor(
            out=x, in0=bank[b][:, :], scalar=MOD[:, 32 + d:33 + d], in1=s_, op0=ALU.mult, op1=ALU.add),
            mk, ld, mixd, lnm)
        free[b] = [m]
        si_free[i] = m
        x2.append(m)
        q1 = op("act", lambda e, x=x, d=d: e.activation(T[:, d % 2, :], x, ACT.Square), m, tq[d % 2], sgfree)
        if d == 0:
            acc = op("dve", lambda e: e.tensor_copy(SO[:, 0, :], T[:, 0, :]), q1)
        else:
            acc = op("dve", lambda e, d=d: e.tensor_tensor(SO[:, 0, :], SO[:, 0, :], T[:, d % 2, :], ALU.add), q1, acc)
        tq[d % 2] = acc
    mm = op("pe", lambda e: e.matmul(bank[3][:, :], ONE[:, :], SO[:, 0, :], start=True, stop=True), acc, free[3])
    r3 = inv_rms(RS[:, 0, :], 3, mm)
    dout = [slot(f"out{i}") for i in range(4)]
    last = [None] * 4
    for d in range(16):
        x = X2[:, d, :]
        m = op("dve", lambda e, x=x, d=d: e.scalar_tensor_tensor(out=x, in0=x, scalar=col["fg2"][:, d:d + 1],
                                                                 in1=RS[:, 0, :], op0=ALU.mult, op1=ALU.mult),
               r3, x2[d], q1)
        last[d % 4] = fl.dma(dout[d % 4], lambda e, x=x, d=d: e.dma_start(out[d], x), m, last[d % 4])
    finals = [*last, *so_free, *x1out]

    for sem, value in finals:
        nc.sync.wait_ge(sem, value)


def hm_last(fl):
    return fl.sems["pe"], fl.count["pe"]


mm_last = hm_last


def lay_out(i):
    import numpy as _np

    f = _np.ascontiguousarray

    def chan(w):
        k, n = w.shape
        return f(w.reshape(k // 1024, 8, 128, n // 128, 128).transpose(3, 0, 2, 1, 4)).reshape(
            n // 128, k // 1024, 128, 1024)

    def col(v):
        return v.reshape(-1, 128).T

    w1 = i["w_in"][0]
    w2 = i["w_in_2"][0]
    wide = _np.concatenate([w2[:, 1024:2048], w2[:, 5120:6144]], axis=1)
    wvv = f(wide.reshape(8, 2, 128, 4, 512).transpose(3, 0, 2, 1, 4)).reshape(4, 8, 128, 1024)
    bf = _np.zeros((128, 1), _np.float32)
    bf[:16, 0] = i["b_f_2"][0]
    cols = _np.concatenate([
        col(i["norm_g"][0]), col(i["final_g"]), col(i["norm_g_2"][0]), col(i["final_g_2"]),
        col(i["conv_w"][0].reshape(-1)), col(i["b_glu"][0]), col(i["d_skip"][0].reshape(-1)),
        col(i["b_ada_2"][0]), col(i["c_2"][0]), col(i["ln_v_g_2"][0]), col(i["ln_v_b_2"][0]), bf], axis=1)
    pairs = lambda a: f(a[0].reshape(32, 128).T)

    def b_rows(b):
        o = _np.zeros((8, 4, 2, 16, 2, 64), _np.float32)
        v = b[0].reshape(8, 4, 2, 64, 16)
        for g in range(2):
            o[:, :, g, :, g, :] = v[:, :, g].transpose(0, 1, 3, 2)
        return f(o.reshape(8, 128, 128).transpose(1, 0, 2))

    def c_rows(c):
        return f(c[0].reshape(32, 2, 16, 64).transpose(1, 3, 0, 2)).reshape(128, 32, 16)

    return {
        "xT": f(i["x"][0].T).reshape(16, 128, 512),
        "w1": chan(w1), "wg": chan(i["w_glu"][0]), "wa": chan(i["w_out_a"][0]), "wb": chan(i["w_out_b"][0]),
        "wo": chan(i["w_o"][0]), "w2": chan(w2[:, :7168]), "wvv": wvv,
        "wf": f(w2[:, 7168:].reshape(16, 128, 16).transpose(1, 0, 2)), "w3": chan(i["w_out_2"][0]),
        "ada": f(i["w_ada_2"][0].reshape(16, 128, 6, 1024).transpose(2, 0, 1, 3)),
        "cols": f(cols), "are": pairs(i["a_re"]), "aim": pairs(i["a_im"]),
        "ldt": pairs(_np.repeat(i["log_dt"][0], 64)[None]),
        "bre": b_rows(i["b_re"]), "bim": b_rows(i["b_im"]), "cre": c_rows(i["c_re"]), "cim": c_rows(i["c_im"]),
        "wsT": f(i["w_s_2"][0].transpose(2, 0, 1)),
        "bsb": f(_np.broadcast_to(i["b_s_2"][0][None], (128, 8, 128))),
    }


def kernel(**inputs):
    import numpy as _np
    import concourse.bacc as _bacc
    from concourse import mybir as _mybir
    from concourse.bass_utils import run_bass_kernel_spmd as _run

    arrays = lay_out({k: _np.asarray(v) for k, v in inputs.items()})
    nc = _bacc.Bacc("TRN2", target_bir_lowering=False, num_devices=1)
    t = {n: nc.dram_tensor("in_" + n, arrays[n].shape, _mybir.dt.float32, kind="ExternalInput").ap() for n in PARAMS}
    out = nc.dram_tensor("out_y", (16, 128, 512), _mybir.dt.float32, kind="ExternalOutput").ap()
    program(nc, t, out)
    r = _run(nc, [{"in_" + n: arrays[n] for n in PARAMS}], core_ids=[0])
    got = r.results[0]["out_y"]
    return _np.ascontiguousarray(got.reshape(2048, 512).T).reshape(1, 512, 2048)
```

```python
from collections import deque

import numpy as np

import concourse.bass as bass
from concourse import mybir

F32 = mybir.dt.float32
F32R = mybir.dt.float32r
I32 = mybir.dt.int32
ALU = mybir.AluOpType
ACT = mybir.ActivationFunctionType
AX = mybir.AxisListType.X

S = 512
EPS = 1e-6
KB = 1024
BASE = 16512
MAGIC = 12582912.0
NW = 3
NB = 3
AHEAD = 2

PARAMS = [
    "xT", "w1", "wg", "wa", "wb", "wo", "w2", "wvv", "wf", "w3", "ada", "cols", "are", "aim", "ldt",
    "bstk", "cre", "cim", "wsT", "bsb",
]
COLS = [("g1", 16), ("fg", 16), ("g2", 16), ("fg2", 16), ("cw", 48), ("bglu", 8), ("dsk", 8),
        ("bada", 48), ("c2", 16), ("lng", 8), ("lnb", 8), ("bf", 1)]


class Flow:

    def __init__(self, engines, sems):
        self.engines = engines
        self.sems = sems
        self.count = {e: 0 for e in sems}
        self.seen = {e: {} for e in engines}

    def _wait(self, eng, after):
        todo = list(after)
        while todo:
            t = todo.pop()
            if t is None:
                continue
            if isinstance(t, list):
                todo.extend(t)
                continue
            sem, value = t
            if self.seen[eng].get(id(sem), 0) < value:
                self.seen[eng][id(sem)] = value
                self.engines[eng].wait_ge(sem, value)

    def op(self, eng, fn, *after):
        self._wait(eng, after)
        fn(self.engines[eng]).then_inc(self.sems[eng], 1)
        self.count[eng] += 1
        return self.sems[eng], self.count[eng]

    def quiet(self, eng, fn, *after):
        self._wait(eng, after)
        fn(self.engines[eng])

    def dma(self, slot, fn, *after):
        self._wait("sp", after)
        fn(self.engines["sp"]).then_inc(slot[0], 16)
        slot[1] += 16
        return slot[0], slot[1]


def stream_order(t):
    out = []

    def tiles(tag, w, m):
        for c in range(w.shape[1]):
            out.append((tag, w[m, c]))

    for c in range(2):
        for m in range(2):
            out.append(("u", t["w1"][64 + m, c]))
    for m in range(2, 8):
        tiles("u", t["w1"], 64 + m)
    for m in range(8):
        tiles("zb", t["w1"], 72 + m)
    for m in range(32):
        tiles("gate", t["w1"], 80 + m)
    n = 0
    for c in range(16):
        for part in (0, 2, 1, 3):
            for kc in range(2):
                out.append(("a", t["w1"][16 * part + c, kc]))
                if n % 20 < 16 and n < 120:
                    out.append(("ada", t["ada"][n // 20, n % 20]))
                n += 1
    for m in range(16):
        tiles("wa", t["wa"], m)
    for m in range(8):
        tiles("wg", t["wg"], m)
    for m in range(16):
        tiles("wb", t["wb"], m)
    for m in range(16):
        tiles("wo", t["wo"], m)
    for half in (2, 3):
        tiles("v", t["wvv"], half)
    for j in range(8):
        for m in (24 + j, 32 + j, 48 + j):
            tiles("qkg", t["w2"], m)
    for h in range(4):
        for m in (h, 16 + h):
            tiles("ug", t["w2"], m)
    for half in (0, 1):
        tiles("v", t["wvv"], half)
    for h in range(4, 8):
        for m in (h, 16 + h):
            tiles("ug", t["w2"], m)
    for m in range(16):
        tiles("w3", t["w3"], m)
    return out


def program(nc, t, out):
    sem_names = ["pe", "act", "dve", "pool"]
    fl = Flow({"pe": nc.tensor, "act": nc.scalar, "dve": nc.vector, "pool": nc.gpsimd, "sp": nc.sync},
              {e: nc.alloc_semaphore("s_" + e) for e in sem_names})
    op, quiet = fl.op, fl.quiet

    def slot(name):
        return [nc.alloc_semaphore("d_" + name), 0]

    def at(name, kb, shape, dt=F32):
        return nc.alloc_sbuf_tensor_at(name, shape, dt, offset=BASE + int(kb * KB))

    bank = [nc.alloc_psum_tensor(f"bank{i}", [128, 512], F32) for i in range(8)]
    free = [[] for _ in range(8)]

    scratch = {n: nc.dram_tensor("scr_" + n, [k, 128, 512], F32, kind="Internal").ap()
               for n, k in (("zb", 8), ("ga", 16), ("gb", 16), ("x1", 16))}

    hH, hL = at("hH", 0, [128, 16, 512], F32R), at("hL", 32, [128, 16, 512], F32R)
    MA = at("MA", 0, [128, 16, 512])
    ybH, ybL = at("ybH", 32, [128, 8, 512], F32R), at("ybL", 48, [128, 8, 512], F32R)
    mL = at("mL", 32, [128, 16, 512], F32R)
    X1 = at("X1", 0, [128, 16, 512])
    QA = at("QA", 0, [65, 2, 2, 512])
    KA = at("KA", 8, [65, 2, 2, 512])
    PR = at("PR", 16, [128, 4, 512])
    PT = at("PT", 24, [128, 4, 512])
    WS = at("WS", 0, [128, 8, 128])
    BSB = at("BSB", 4, [128, 8, 128])
    CON = at("CON", 8, [128, 8, 128])
    SQ = at("SQ", 12, [128, 1024])
    MX = at("MX", 16, [128, 2, 512])
    YF = at("YF", 32, [128, 16, 512])
    X2 = at("X2", 0, [128, 16, 512])
    AH, AL = at("AH", 64, [128, 16, 512], F32R), at("AL", 96, [128, 16, 512], F32R)
    XS = at("XS", 96, [128, 16, 512])
    XG = at("XG", 80, [128, 8, 512])
    BH, BL = at("BH", 64, [128, 8, 512], F32R), at("BL", 80, [128, 8, 512], F32R)
    mH = at("mH", 96, [128, 16, 512], F32R)
    h2H, h2L = at("h2H", 64, [128, 16, 512], F32R), at("h2L", 96, [128, 16, 512], F32R)
    yH, yL = at("yH", 64, [128, 16, 512], F32R), at("yL", 96, [128, 16, 512], F32R)
    CB = at("CB", 64, [128, 2, 32, 32])
    CR = at("CR", 72, [128, 2, 32, 16])
    SM = at("SM", 76, [128, 32, 32])
    E0 = at("E0", 80, [128, 2, 32, 32])
    W0 = at("W0", 88, [128, 2, 32, 16])
    BRAW = at("BRAW", 92, [96, 2, 2, 128])
    BSTK = at("BSTK", 94, [96, 2, 2, 128], F32R)
    URAW = at("URAW", 96, [96, 2, 512])
    USTK = at("USTK", 100, [96, 2, 512], F32R)
    TAB = at("TAB", 104, [128, 2, 2, 512])
    V = at("V", 112, [128, 4, 512])
    HH = at("HH", 120, [128, 2, 2, 512])
    YK = at("YK", 64, [128, 16, 512])
    W = at("W", 128, [128, NW, 1024])
    WH, WL = at("WH", 140, [128, NB, 1024], F32R), at("WL", 152, [128, NB, 1024], F32R)
    U = at("U", 164, [128, 8, 512])
    VV = at("VV", 164, [128, 4, 1024])
    SO = at("SO", 180, [128, 2, 512])
    SI = at("SI", 184, [128, 2, 512])
    T = at("T", 188, [128, 4, 512])
    CV = at("CV", 196, [128, 514])
    ACC = at("ACC", 198.25, [128, 1024])
    RS = at("RS", 198.25, [128, 2, 512])
    ncol = sum(n for _, n in COLS)
    PC = at("PC", 202.25, [128, ncol])
    ONE = at("ONE", 203.25, [128, 128])
    IDT = at("IDT", 203.75, [128, 128])
    CAU = at("CAU", 204.25, [128, 128])
    MOD = at("MOD", 204.75, [128, 48])
    SC = at("SC", 205, [128, 16])
    ST = at("ST", 205.25, [128, 80])
    NF = at("NF", 205.75, [16, 512])
    col, k = {}, 0
    for name, n in COLS:
        col[name] = PC[:, k:k + n]
        k += n

    order = stream_order(t)
    wsl = [slot(f"w{i}") for i in range(NW)]
    landed, wfree, parts, used = {}, {}, {}, {}
    state = {"next": 0, "split": 0, "use": 0, "cur": [], "lag": 0}
    ada = {"n": 0, "acc": None, "free": None}

    def fetch(i):
        if i < len(order):
            src = order[i][1]
            landed[i] = fl.dma(wsl[i % NW], lambda e, i=i, src=src: e.dma_start(W[:, i % NW, :], src),
                               wfree.get(i - NW))

    low_on = {"every": 0}

    def ada_chunk(i):
        n = ada["n"]
        cb, kt = n // 16, n % 16
        w, c = W[:, i % NW, :], SC[:, kt:kt + 1]
        if kt == 0:
            m = op("dve", lambda e: e.tensor_scalar(ACC[:, :], w, c, None, ALU.mult),
                   landed[i], ada["free"], ada["c"])
        else:
            m = op("dve", lambda e: e.scalar_tensor_tensor(out=ACC[:, :], in0=w, scalar=c, in1=ACC[:, :],
                                                           op0=ALU.mult, op1=ALU.add),
                   landed[i], ada["acc"])
        ada["acc"] = m
        wfree[i] = m
        ada["n"] += 1
        if kt == 15:
            def reduce(cb=cb, m=m):
                for q in range(8):
                    mm = op("pe", lambda e: e.matmul(bank[3][:, q:q + 1], ACC[:, q * 128:(q + 1) * 128],
                                                     ONE[:, 0:1], start=True, stop=True), m, free[3])
                k0 = cb * 8
                free[3] = [op("dve", lambda e: e.tensor_tensor(MOD[:, k0:k0 + 8], bank[3][:, 0:8],
                                                               col["bada"][:, k0:k0 + 8], ALU.add), mm)]
                ada["free"] = free[3]
                ada["mod"] = free[3]
            ada["due"] = (state["use"] + 3, reduce)

    def prepare():
        i = state["next"]
        if i >= len(order):
            return False
        state["next"] += 1
        if order[i][0] == "ada":
            ada_chunk(i)
        else:
            n = state["split"]
            state["split"] += 1
            b = n % NB
            w, wh, wl = W[:, i % NW, :], WH[:, b, :], WL[:, b, :]
            mh = op("act", lambda e: e.activation(wh, w, ACT.Copy), landed[i], used.get(n - NB))
            who = "pool" if low_on["every"] and n % low_on["every"] == 0 else "dve"
            ml = op(who, lambda e: e.tensor_tensor(wl, w, wh.bitcast(F32), ALU.subtract),
                    mh, landed[i], used.get(n - NB))
            wfree[i] = [mh, ml]
            parts[n] = (b, [mh, ml])
        fetch(i + NW)
        return True

    def chunk():
        n = state["use"]
        state["use"] += 1
        if "due" in ada and ada["due"][0] <= n:
            ada.pop("due")[1]()
        while state["split"] <= n + AHEAD and prepare():
            pass
        return n, parts[n][0], parts[n][1]

    beside = deque()
    debt = [0.0]

    def pump(budget):
        debt[0] += budget
        while beside and debt[0] > 0:
            try:
                cost = next(beside[0])
                debt[0] -= cost
            except StopIteration:
                beside.popleft()
        if not beside:
            debt[0] = 0.0

    def drain_beside():
        while beside:
            pump(1.0)

    BUDGET = {"v": 0.0}

    def products8(b, kc, nch, XH, XL, ready):
        n, s, m = chunk()
        for k8 in range(8):
            k = 8 * kc + k8
            wh, wl = WH[:, s, 128 * k8:128 * k8 + 128], WL[:, s, 128 * k8:128 * k8 + 128]
            first, last = k == 0, k == 8 * nch - 1
            quiet("pe", lambda e: e.matmul(bank[b][:, :], wh, XH[:, k, :], start=first, stop=False),
                  m, ready[k], free[b] if first else None)
            quiet("pe", lambda e: e.matmul(bank[b][:, :], wh, XL[:, k, :], start=False, stop=False))

            def low(e):
                return e.matmul(bank[b][:, :], wl, XH[:, k, :], start=False, stop=last)

            if k8 == 7:
                mark = op("pe", low)
            else:
                quiet("pe", low)
        used[n] = mark
        return mark

    def project(b, nch, XH, XL, ready):
        for kc in range(nch):
            mark = products8(b, kc, nch, XH, XL, ready)
            if kc < nch - 1:
                pump(BUDGET["v"])
        return mark

    ring = {"n": 1}

    def next_bank():
        ring["n"] += 1
        return ring["n"] % 3

    def split(H, L, src, after, war=None):
        mh = op("act", lambda e: e.activation(H, src, ACT.Copy), after, war)
        ml = op("dve", lambda e: e.tensor_tensor(L, src, H.bitcast(F32), ALU.subtract), mh, after, war)
        return [mh, ml]

    d_par = slot("par")
    pc = fl.dma(d_par, lambda e: e.dma_start(PC[:, :], t["cols"]))
    one = op("pool", lambda e: e.memset(ONE[:, :], 1.0))
    z1 = op("pool", lambda e: e.memset(IDT[:, :], 0.0))
    z2 = op("pool", lambda e: e.memset(CAU[:, :], 0.0))
    idt = op("pool", lambda e: e.affine_select(out=IDT[:, :], in_=IDT[:, :], compare_op=ALU.not_equal,
                                               fill=1.0, base=0, pattern=[[-1, 128]],
                                               channel_multiplier=1), z1)
    cau = op("pool", lambda e: e.affine_select(out=CAU[:, :], in_=CAU[:, :], compare_op=ALU.is_ge,
                                               fill=-1e30, base=0, pattern=[[-1, 128]],
                                               channel_multiplier=1), z2)

    dx = [slot(f"x{i}") for i in range(8)]
    fetch(0)
    xin = [fl.dma(dx[i], lambda e, i=i: e.dma_start(XS[:, 2 * i:2 * i + 2, :],
                                                    t["xT"][2 * i:2 * i + 2].rearrange("k p s -> p k s")))
           for i in range(8)]
    for i in range(1, NW):
        fetch(i)
    d_ssm = [slot(f"ssm{i}") for i in range(3)]

    def token_sums(x, b, *after):
        for q in range(4):
            mm = op("pe", lambda e: e.matmul(bank[b][:, q:q + 1], x[:, 128 * q:128 * q + 128], ONE[:, 0:1],
                                             start=True, stop=True), free[b], one, *after)
        return mm

    def inv_rms(i, b, mm, pre=None, times=None):
        r, v, y = R4(i), R4(4), R4(5)
        m = op("dve", lambda e: e.tensor_scalar(v, bank[b][:, 0:4], 1.0 / 2048, EPS if pre is None else 0.0,
                                                ALU.mult, ALU.add), mm)
        free[b] = [m]
        if pre is not None:
            m = op("dve", lambda e: e.tensor_tensor(v, v, pre, ALU.mult), m)
            m = op("dve", lambda e: e.tensor_tensor(v, v, pre, ALU.mult), m)
            m = op("dve", lambda e: e.tensor_scalar(v, v, EPS, None, ALU.add), m)
        m = op("act", lambda e: e.activation(y, v, ACT.Sqrt), m)
        m = op("dve", lambda e: e.reciprocal(r, y), m)
        m = op("dve", lambda e: e.tensor_tensor(y, r, r, ALU.mult), m)
        m = op("dve", lambda e: e.tensor_tensor(y, y, v, ALU.mult), m)
        m = op("dve", lambda e: e.tensor_scalar(y, y, -0.5, 1.5, ALU.mult, ALU.add), m)
        m = op("dve", lambda e: e.tensor_tensor(r, r, y, ALU.mult), m)
        if times is not None:
            m = op("dve", lambda e: e.tensor_tensor(r, r, times, ALU.mult), m)
        return m

    def spread(i, b, *after):
        for q in range(4):
            mm = op("pe", lambda e: e.matmul(bank[b][:, 128 * q:128 * q + 128],
                                             R4(i)[:, q:q + 1].to_broadcast([128, 128]), IDT[:, :],
                                             start=True, stop=True), free[b], idt, *after)
        return mm

    def R4(i):
        return ST[:, 56 + 4 * i:60 + 4 * i]

    prepare()
    acc = None
    tfree = [None, None]
    xg = {}
    for k in range(16):
        tk = T[:, k % 2, :]
        sq = op("act", lambda e, tk=tk, k=k: e.activation(tk, XS[:, k, :], ACT.Square), xin[k // 2], tfree[k % 2])
        if k == 0:
            acc = op("dve", lambda e, tk=tk: e.tensor_copy(SO[:, 0, :], tk), sq)
        else:
            acc = op("dve", lambda e, tk=tk: e.tensor_tensor(SO[:, 0, :], SO[:, 0, :], tk, ALU.add), sq, acc)
        tfree[k % 2] = acc
        if k % 2:
            xg[k] = op("pool", lambda e: e.tensor_scalar(XG[:, k // 2, :], XS[:, k, :], col["g1"][:, k:k + 1],
                                                         None, ALU.mult), xin[k // 2], pc)
    for i in range(2):
        prepare()
    rs = inv_rms(0, 0, token_sums(SO[:, 0, :], 0, acc))
    rs = spread(0, 3, rs)
    rs_sb = op("act", lambda e: e.activation(RS[:, 0, :], bank[3][:, :], ACT.Copy), rs)
    hready = []
    for k in range(16):
        x = XS[:, k, :] if k % 2 == 0 else XG[:, k // 2, :]
        if k % 2 == 0:
            m = op("dve", lambda e: e.scalar_tensor_tensor(out=x, in0=x, scalar=col["g1"][:, k:k + 1],
                                                           in1=RS[:, 0, :], op0=ALU.mult, op1=ALU.mult), rs_sb, pc)
        else:
            m = op("pool", lambda e: e.tensor_tensor(x, x, RS[:, 0, :], ALU.mult), rs_sb, xg[k])
        hready.append(split(hH[:, k, :], hL[:, k, :], x, m))
    free[3] = [rs_sb]
    xs_free = hready[-1]
    ada["free"] = hready[-1]
    ada["c"] = op("act", lambda e: e.activation(SC[:, :], col["c2"], ACT.Silu), pc)

    dve_last = [None]

    def dv(fn, *after):
        dve_last[0] = op("dve", fn, dve_last[0], *after)
        return dve_last[0]

    def ts(o, a, s1, s2, o0, o1=None, *after):
        if o1 is None:
            return dv(lambda e: e.tensor_scalar(o, a, s1, None, o0), *after)
        return dv(lambda e: e.tensor_scalar(o, a, s1, s2, o0, o1), *after)

    def tt(o, a, b, o0, *after):
        return dv(lambda e: e.tensor_tensor(o, a, b, o0), *after)

    def stt(o, a, s, b, o0, o1, *after):
        return dv(lambda e: e.scalar_tensor_tensor(out=o, in0=a, scalar=s, in1=b, op0=o0, op1=o1), *after)

    def exp_steps(dst, x, n, r, sc, *after):
        ts(dst, x, -87.3, 88.7, ALU.max, ALU.min, *after)
        ts(n, dst, 1.4426950408889634, MAGIC, ALU.mult, ALU.add)
        ts(n, n, -MAGIC, None, ALU.add)
        stt(r, n, -0.693359375, dst, ALU.mult, ALU.add)
        stt(r, n, 2.12194440e-4, r, ALU.mult, ALU.add)
        yield 0.5
        ts(dst, r, 1.0 / 5040, None, ALU.mult)
        for c in (1.0 / 720, 1.0 / 120, 1.0 / 24, 1.0 / 6, 0.5, 1.0):
            stt(dst, dst, c, r, ALU.add, ALU.mult)
        yield 0.7
        ts(dst, dst, 1.0, None, ALU.add)
        ts(sc, n, 127.0, 8388608.0, ALU.add, ALU.mult)
        tt(dst, dst, sc.bitcast(F32), ALU.mult)
        stt(dst, x, -87.3, dst, ALU.is_gt, ALU.mult)
        yield 0.5

    def sm(i):
        return SM[:, i, :]

    SMI = at("SMI", 76 + 3.75, [128, 32], I32)

    ssm = {}

    def ssm_params():
        da = fl.dma(d_ssm[0], lambda e: e.dma_start(sm(0), t["are"]))
        db = fl.dma(d_ssm[1], lambda e: e.dma_start(sm(1), t["aim"]))
        dc = fl.dma(d_ssm[2], lambda e: e.dma_start(sm(2), t["ldt"]))
        d_c = slot("cr")
        fl.dma(d_c, lambda e: e.dma_start(CR[:, 0], t["cre"]))
        dcr = fl.dma(d_c, lambda e: e.dma_start(CR[:, 1], t["cim"]))
        cz = op("pool", lambda e: e.memset(CB[:, :, :, :], 0.0))
        yield 0.1
        are, aim, ldt, dt, zr, zi, n, r, mag = (sm(i) for i in range(9))
        yield from exp_steps(dt, ldt, n, r, SMI[:, :], dc)
        tt(zr, are, dt, ALU.mult, da)
        tt(zi, aim, dt, ALU.mult, db)
        yield from exp_steps(mag, zr, n, r, SMI[:, :])
        m, y, q, y2, sn, cs, aq, sq_, t0 = (sm(i) for i in range(9, 18))
        ts(m, zi, 0.6366197723675814, MAGIC, ALU.mult, ALU.add)
        ts(m, m, -MAGIC, None, ALU.add)
        rest = np.pi / 2
        for i, bits in enumerate((7, 19, 30, 60)):
            part = float(np.floor(rest * 2.0 ** bits) / 2.0 ** bits) if i < 3 else float(rest)
            rest -= part
            stt(y, m, -part, zi if i == 0 else y, ALU.mult, ALU.add)
        ts(q, m, 0.25, MAGIC, ALU.mult, ALU.add)
        ts(q, q, -MAGIC, None, ALU.add)
        stt(q, q, -4.0, m, ALU.mult, ALU.add)
        yield 0.9
        tt(y2, y, y, ALU.mult)
        ts(sn, y2, 1.0 / 362880, None, ALU.mult)
        for c in (-1.0 / 5040, 1.0 / 120, -1.0 / 6):
            stt(sn, sn, c, y2, ALU.add, ALU.mult)
        stt(sn, sn, 1.0, y, ALU.add, ALU.mult)
        ts(cs, y2, -1.0 / 3628800, None, ALU.mult)
        for c in (1.0 / 40320, -1.0 / 720, 1.0 / 24, -0.5):
            stt(cs, cs, c, y2, ALU.add, ALU.mult)
        ts(cs, cs, 1.0, None, ALU.add)
        yield 1.3
        stt(aq, q, -1.0, q, ALU.mult, ALU.max)
        ts(t0, aq, -1.0, 2.0, ALU.mult, ALU.add)
        tt(sq_, t0, q, ALU.mult)
        ts(aq, aq, -1.0, 1.0, ALU.mult, ALU.add)
        sinz, cosz, t1, t2 = (sm(i) for i in range(18, 22))
        tt(t1, sn, aq, ALU.mult)
        tt(t2, cs, sq_, ALU.mult)
        tt(sinz, t1, t2, ALU.add)
        tt(t1, cs, aq, ALU.mult)
        tt(t2, sn, sq_, ALU.mult)
        tt(cosz, t1, t2, ALU.subtract)
        yield 1.0
        lr, li, fr, fi, den = (sm(i) for i in range(22, 27))
        tt(lr, mag, cosz, ALU.mult)
        ts(lr, lr, -1.0, None, ALU.add)
        tt(li, mag, sinz, ALU.mult)
        tt(den, are, are, ALU.mult)
        tt(t1, aim, aim, ALU.mult)
        tt(den, den, t1, ALU.add)
        dv(lambda e: e.reciprocal(den, den))
        tt(t1, lr, are, ALU.mult)
        tt(t2, li, aim, ALU.mult)
        tt(t1, t1, t2, ALU.add)
        tt(fr, t1, den, ALU.mult)
        tt(t1, li, are, ALU.mult)
        tt(t2, lr, aim, ALU.mult)
        tt(t1, t1, t2, ALU.subtract)
        tt(fi, t1, den, ALU.mult)
        yield 1.6
        t3, t4 = (V[:, i, :].rearrange("p (j c) -> p j c", c=16) for i in range(2))
        frb = fr.unsqueeze(2).to_broadcast([128, 32, 16])
        fib = fi.unsqueeze(2).to_broadcast([128, 32, 16])
        tt(t3, CR[:, 0], frb, ALU.mult, dcr, xs_free)
        tt(t4, CR[:, 1], fib, ALU.mult)
        for g in range(2):
            p = slice(64 * g, 64 * g + 64)
            tt(CB[p, 0, :, 16 * g:16 * g + 16], t3[p], t4[p], ALU.subtract, cz)
        tt(t3, CR[:, 0], fib, ALU.mult)
        tt(t4, CR[:, 1], frb, ALU.mult)
        yield 3.0
        tt(t3, t3, t4, ALU.add)
        for g in range(2):
            p = slice(64 * g, 64 * g + 64)
            ts(CB[p, 1, :, 16 * g:16 * g + 16], t3[p], -1.0, None, ALU.mult)
        ssm["cb"] = dve_last[0]
        yield 1.2
        pr, pi, nr, ni = (sm(i) for i in range(27, 30)), None, None, None
        pr, pi, nr = pr
        ni = sm(0)
        tmp, tmp2 = (V[:, i, :].rearrange("p (j n) -> p j n", n=16) for i in (2, 3))
        dv(lambda e: e.tensor_copy(pr, cosz))
        dv(lambda e: e.tensor_copy(pi, sinz))
        for big, levels in ((E0, 5), (W0, 4)):
            dv(lambda e, big=big: e.memset(big[:, 0, :, 0:1], 1.0))
            dv(lambda e, big=big: e.memset(big[:, 1, :, 0:1], 0.0))
            for lv in range(levels):
                w = 1 << lv
                a_r, a_i = big[:, 0, :, 0:w], big[:, 1, :, 0:w]
                o_r, o_i = big[:, 0, :, w:2 * w], big[:, 1, :, w:2 * w]
                b_r = pr.unsqueeze(2).to_broadcast([128, 32, w])
                b_i = pi.unsqueeze(2).to_broadcast([128, 32, w])
                x1_, x2_ = tmp[:, :, 0:w], tmp2[:, :, 0:w]
                tt(x1_, a_r, b_r, ALU.mult, xs_free)
                tt(x2_, a_i, b_i, ALU.mult)
                tt(o_r, x1_, x2_, ALU.subtract)
                tt(x1_, a_r, b_i, ALU.mult)
                tt(x2_, a_i, b_r, ALU.mult)
                tt(o_i, x1_, x2_, ALU.add)
                yield 0.5 + 0.2 * w
                tt(t1, pr, pr, ALU.mult)
                tt(t2, pi, pi, ALU.mult)
                tt(nr, pr, pi, ALU.mult)
                tt(pr, t1, t2, ALU.subtract)
                ts(pi, nr, 2.0, None, ALU.mult)
                yield 0.5
        ssm["turn"] = dve_last[0]
        ssm["mag"] = mag

    uready = [None] * 8
    ssm["y"] = [None] * 8

    def ssm_tiles():
        mag = ssm["mag"]
        tabfree, hfree, tab, hm = [None] * 2, [None] * 2, {}, {}
        bufree = [None, None]
        bu, stk, raw = {}, {}, {}
        dstk, dstb = [slot(f"stk{i}") for i in range(2)], [slot(f"stb{i}") for i in range(2)]
        rawfree, stkfree = [None, None], [None, None]

        def table(j):
            b = j % 2
            er = E0[:, 0, j:j + 1, :].to_broadcast([128, 16, 32])
            ei = E0[:, 1, j:j + 1, :].to_broadcast([128, 16, 32])
            wr = W0[:, 0, j, :].unsqueeze(2).to_broadcast([128, 16, 32])
            wi = W0[:, 1, j, :].unsqueeze(2).to_broadcast([128, 16, 32])
            c = TAB[:, b, 0, :].rearrange("p (a i) -> p a i", i=32)
            s = TAB[:, b, 1, :].rearrange("p (a i) -> p a i", i=32)
            x1_ = T[:, 2, :].rearrange("p (a i) -> p a i", i=32)
            x2_ = T[:, 3, :].rearrange("p (a i) -> p a i", i=32)
            P = "pool"
            m = op(P, lambda e: e.tensor_tensor(c, er, wr, ALU.mult), ssm["turn"], tabfree[b])
            m2 = op(P, lambda e: e.tensor_tensor(x1_, ei, wi, ALU.mult), tab.get(j - 1))
            m = op(P, lambda e: e.tensor_tensor(c, c, x1_, ALU.subtract), m, m2)
            m3 = op(P, lambda e: e.tensor_tensor(s, er, wi, ALU.mult))
            m4 = op(P, lambda e: e.tensor_tensor(x2_, ei, wr, ALU.mult))
            tab[j] = op(P, lambda e: e.tensor_tensor(s, s, x2_, ALU.add), m3, m4)

        def stack_load(j):
            ut, i, s = j // 4, j % 4, j % 2
            for z in range(3):
                du = fl.dma(dstk[s], lambda e: e.dma_start(URAW[32 * z:32 * z + 32, s, :],
                                                           U[32 * i:32 * i + 32, ut, :]),
                            uready[ut], rawfree[s], xs_free)
            db = fl.dma(dstb[s], lambda e: e.dma_start(BRAW[:, s, :, :], t["bstk"][j]), rawfree[s], xs_free)
            raw[j] = (du, db)

        def stack_high(j):
            s = j % 2
            du, db = raw[j]
            mu = op("act", lambda e: e.activation(USTK[:, s, :], URAW[:, s, :], ACT.Copy), du, stkfree[s])
            mb = op("act", lambda e: e.activation(BSTK[:, s, :, :], BRAW[:, s, :, :], ACT.Copy), db, stkfree[s])
            stk[j] = [mu, mb]

        def stack_low(j):
            s = j % 2
            mu, mb = stk[j]
            ul, bl = USTK[0:32, s, :], BSTK[64:96, s, :, :]
            m1 = op("pool", lambda e: e.tensor_tensor(ul, URAW[0:32, s, :], ul.bitcast(F32), ALU.subtract), mu)
            m2 = op("dve", lambda e: e.tensor_tensor(bl, BRAW[64:96, s, :, :], bl.bitcast(F32), ALU.subtract), mb)
            rawfree[s] = [m1, m2]
            stk[j] = [m1, m2, mu, mb]

        def products(j):
            b = 4 + 2 * (j % 2)
            s = j % 2
            for z in range(2):
                bu[j] = op("pe", lambda e: e.matmul(bank[b + z][:, :], BSTK[:, s, z, :], USTK[:, s, :],
                                                    start=True, stop=True), stk[j], bufree[j % 2])
            stkfree[s] = bu[j]

        def readout(j):
            ut, i = j // 4, j % 4
            o = bank[3][32 * i:32 * i + 32, :]
            quiet("pe", lambda e: e.matmul(o, CB[:, 0, j, :], HH[:, j % 2, 0, :], start=True, stop=False),
                  hm[j], ssm["cb"], free[3])
            hfree[j % 2] = op("pe", lambda e: e.matmul(o, CB[:, 1, j, :], HH[:, j % 2, 1, :],
                                                       start=False, stop=True))

        def skip_term(ut):
            m = op("dve", lambda e: e.scalar_tensor_tensor(out=U[:, ut, :], in0=U[:, ut, :],
                                                           scalar=col["dsk"][:, ut:ut + 1], in1=bank[3][:, :],
                                                           op0=ALU.mult, op1=ALU.add), hfree[1])
            free[3] = [m]
            ssm["y"][ut] = m

        stack_load(0)
        stack_load(1)
        table(0)
        for i in range(2):
            stack_high(i)
            stack_low(i)
            stack_load(i + 2)
        products(0)
        yield 0.1
        for j in range(32):
            if j + 1 < 32:
                table(j + 1)
                products(j + 1)
            if j + 2 < 32:
                stack_high(j + 2)
            c, s = TAB[:, j % 2, 0, :], TAB[:, j % 2, 1, :]
            br, bi = bank[4 + 2 * (j % 2)][:, :], bank[5 + 2 * (j % 2)][:, :]
            v = [V[:, i, :] for i in range(4)]
            a = op("dve", lambda e: e.tensor_tensor(v[0], c, br, ALU.mult), tab[j], bu[j], dve_last[0])
            b = op("dve", lambda e: e.tensor_tensor(v[1], s, bi, ALU.mult))
            yield 1.2
            c2 = op("dve", lambda e: e.tensor_tensor(v[2], c, bi, ALU.mult))
            d = op("dve", lambda e: e.tensor_tensor(v[3], s, br, ALU.mult))
            bufree[j % 2] = d
            yield 1.2
            if j + 2 < 32:
                stack_low(j + 2)
            if j + 4 < 32:
                stack_load(j + 4)
            a = op("dve", lambda e: e.tensor_tensor(v[0], v[0], v[1], ALU.add), a, b)
            b = op("dve", lambda e: e.tensor_tensor(v[2], v[2], v[3], ALU.subtract), c2, d)
            yield 1.2
            rb = mag[:, j:j + 1].to_broadcast([128, 512])
            a = op("dve", lambda e: e.tensor_tensor_scan(v[1], rb, v[0], 0.0, ALU.mult, ALU.add), a)
            yield 1.1
            b = op("dve", lambda e: e.tensor_tensor_scan(v[3], rb, v[2], 0.0, ALU.mult, ALU.add), b)
            yield 1.1
            if j >= 1 and j % 4 == 0:
                skip_term(j // 4 - 1)
                yield 0.6
            hr, hi = HH[:, j % 2, 0, :], HH[:, j % 2, 1, :]
            c2 = op("dve", lambda e: e.tensor_tensor(v[0], c, v[1], ALU.mult), a)
            d = op("dve", lambda e: e.tensor_tensor(v[2], s, v[3], ALU.mult), b)
            yield 1.2
            f = op("dve", lambda e: e.tensor_tensor(hr, v[0], v[2], ALU.subtract), c2, d, hfree[j % 2])
            f = op("dve", lambda e: e.tensor_tensor(v[0], s, v[1], ALU.mult), f)
            g = op("dve", lambda e: e.tensor_tensor(v[2], c, v[3], ALU.mult))
            tabfree[j % 2] = g
            yield 1.8
            hm[j] = op("dve", lambda e: e.tensor_tensor(hi, v[0], v[2], ALU.add), f, g)
            dve_last[0] = hm[j]
            yield 3.5
            debt[0] += 2.9
            readout(j)
        yield 3.0
        skip_term(7)

    BUDGET["v"] = 3.2
    beside.append(ssm_params())
    def keep_u(m, b, mk):
        uready[m] = op("act", lambda e: e.activation(U[:, m, :], bank[b][:, :], ACT.Copy), mk)
        free[b] = [uready[m]]
        pump(BUDGET["v"])

    for kc in range(2):
        for b in range(2):
            mk = products8(b, kc, 2, hH, hL, hready)
            if kc == 1:
                keep_u(b, b, mk)
    for m in range(2, 8):
        b = next_bank()
        keep_u(m, b, project(b, 2, hH, hL, hready))
    drain_beside()
    beside.append(ssm_tiles())
    BUDGET["v"] = 4.0
    low_on["every"] = 3
    so = [slot(f"so{i}") for i in range(2)]
    so_free = [None, None]
    so_n = [0]

    def spill(func, b, mk, dst):
        i = so_n[0] % 2
        so_n[0] += 1
        m = op("act", lambda e: e.activation(SO[:, i, :], bank[b][:, :], func), mk, so_free[i], acc)
        free[b] = [m]
        so_free[i] = fl.dma(so[i], lambda e: e.dma_start(dst, SO[:, i, :]), m)
        return so_free[i]

    stored = {}
    for m in range(8):
        b = next_bank()
        mk = project(b, 2, hH, hL, hready)
        stored["zb", m] = spill(ACT.Silu, b, mk, scratch["zb"][m])
        pump(BUDGET["v"])
    for m in range(32):
        b = next_bank()
        mk = project(b, 2, hH, hL, hready)
        which, i = ("ga", m) if m < 16 else ("gb", m - 16)
        stored[which, i] = spill(ACT.Sigmoid, b, mk, scratch[which][i])
        pump(BUDGET["v"])
    drain_beside()
    low_on["every"] = 0
    ssm_done = [ssm["y"][7], hm_last(fl)]

    cvz = op("dve", lambda e: e.memset(CV[:, 0:2], 0.0))
    aready = []
    t1free = t0free = t2free = None
    for c in range(16):
        cv, cg, bg, za = None, None, None, None
        b = next_bank()
        mk = project(b, 2, hH, hL, hready)
        v_ = op("act", lambda e, b=b: e.activation(T[:, 0, :], bank[b][:, :], ACT.Copy), mk, t0free)
        free[b] = [v_]
        b = next_bank()
        mk = project(b, 2, hH, hL, hready)
        m = op("dve", lambda e, b=b: e.tensor_tensor(CV[:, 2:514], bank[b][:, :], T[:, 0, :], ALU.mult), mk, v_)
        t0free = m
        free[b] = [m]

        def w(i, c=c):
            return col["cw"][:, 16 * i + c:16 * i + c + 1]

        o = T[:, 1, :]
        m = op("dve", lambda e, o=o, w=w: e.tensor_scalar(o, CV[:, 0:512], w(0), None, ALU.mult), m, cvz, t1free)
        m = op("dve", lambda e, o=o, w=w: e.scalar_tensor_tensor(out=o, in0=CV[:, 1:513], scalar=w(1), in1=o,
                                                                 op0=ALU.mult, op1=ALU.add), m)
        m = op("dve", lambda e, o=o, w=w: e.scalar_tensor_tensor(out=o, in0=CV[:, 2:514], scalar=w(2), in1=o,
                                                                 op0=ALU.mult, op1=ALU.add), m)
        b = next_bank()
        mk = project(b, 2, hH, hL, hready)
        m = op("dve", lambda e, b=b, o=o: e.tensor_tensor(o, o, bank[b][:, :], ALU.mult), mk, m)
        free[b] = [m]
        b = next_bank()
        mk = project(b, 2, hH, hL, hready)
        z = op("act", lambda e, b=b: e.activation(T[:, 2, :], bank[b][:, :], ACT.Silu), mk, t2free, ssm_done)
        free[b] = [z]
        m = op("dve", lambda e, o=o: e.tensor_tensor(o, o, T[:, 2, :], ALU.mult), m, z)
        t2free = m
        aready.append(split(AH[:, c, :], AL[:, c, :], o, m, ssm_done))
        t1free = aready[-1]

    ybready = [None] * 8

    def yb_parts():
        gl = []
        for i in range(8):
            gl.append(op("act", lambda e, i=i: e.activation(U[:, i, :], U[:, i, :], ACT.Gelu_apprx_tanh),
                         ssm["y"][i]))
        yield 4.0
        for i in range(8):
            ybready[i] = split(ybH[:, i, :], ybL[:, i, :], U[:, i, :], gl[i], mk_h)
            yield 1.2

    mk_h = mk
    beside.append(yb_parts())
    si = [slot(f"si{i}") for i in range(2)]
    si_free = [None, None]
    si_n = [0]

    def load(src, after=None):
        i = si_n[0] % 2
        si_n[0] += 1
        return i, SI[:, i, :], fl.dma(si[i], lambda e: e.dma_start(SI[:, i, :], src), after, si_free[i])

    BUDGET["v"] = 3.0
    ma = []
    for d in range(16):
        i, s_, ld = load(scratch["ga"][d], stored["ga", d])
        b = next_bank()
        mk = project(b, 2, AH, AL, aready)
        m = op("dve", lambda e, b=b, d=d, s_=s_: e.tensor_tensor(MA[:, d, :], bank[b][:, :], s_, ALU.mult), mk, ld)
        free[b] = [m]
        si_free[i] = m
        ma.append(m)
        pump(BUDGET["v"])
    drain_beside()
    mk_a = mk

    bready = []
    tf = [None, None]
    for g in range(8):
        i, s_, ld = load(scratch["zb"][g], stored["zb", g])
        b = next_bank()
        mk = project(b, 1, ybH, ybL, ybready)
        o = T[:, g % 2, :]
        m = op("act", lambda e, b=b, g=g, o=o: e.activation(o, bank[b][:, :], ACT.Sigmoid,
                                                            bias=col["bglu"][:, g:g + 1]), mk, tf[g % 2])
        free[b] = [m]
        m = op("dve", lambda e, g=g, o=o: e.tensor_tensor(o, o, U[:, g, :], ALU.mult), m)
        m = op("dve", lambda e, o=o, s_=s_: e.tensor_tensor(o, o, s_, ALU.mult), m, ld)
        si_free[i] = m
        bready.append(split(BH[:, g, :], BL[:, g, :], o, m, mk_a))
        tf[g % 2] = bready[-1]
    mk_g = mk

    mready = []
    for d in range(16):
        i, s_, ld = load(scratch["gb"][d], stored["gb", d])
        b = next_bank()
        mk = project(b, 1, BH, BL, bready)
        o = T[:, d % 2, :]
        m = op("dve", lambda e, b=b, o=o, s_=s_: e.tensor_tensor(o, bank[b][:, :], s_, ALU.mult), mk, ld, tf[d % 2])
        free[b] = [m]
        si_free[i] = m
        m = op("dve", lambda e, o=o, d=d: e.tensor_tensor(o, o, MA[:, d, :], ALU.add), m, ma[d])
        mready.append(split(mH[:, d, :], mL[:, d, :], o, m, [mk_a, mk_g]))
        tf[d % 2] = mready[-1]

    a1, a2 = SO[:, 0, :], SO[:, 1, :]
    mk_b = mk
    g2s = ST[:, 0:16]
    gm = op("dve", lambda e: e.tensor_scalar(g2s, MOD[:, 16:32], 1.0, None, ALU.add), ada["mod"])
    gm = op("dve", lambda e: e.tensor_tensor(g2s, g2s, col["g2"], ALU.mult), gm)
    x1raw, yk, s1, s2 = [], [], None, None
    tq = [None, None]
    for d in range(16):
        i, s_, ld = load(t["xT"][d])
        b = next_bank()
        mk = project(b, 2, mH, mL, mready)
        x = X1[:, d, :]
        m = op("dve", lambda e, b=b, x=x, s_=s_: e.tensor_tensor(x, bank[b][:, :], s_, ALU.add), mk, ld)
        free[b] = [m]
        si_free[i] = m
        x1raw.append(m)
        yk.append(op("pool", lambda e: e.tensor_scalar(YK[:, d, :], x, col["fg"][:, d:d + 1], g2s[:, d:d + 1],
                                                       ALU.mult, ALU.mult), m, gm, mk_b))
        q1 = op("act", lambda e, x=x: e.activation(T[:, 2, :], x, ACT.Square), m, tq[0])
        q2 = op("act", lambda e, x=x, d=d: e.activation(T[:, 3, :], x, ACT.Square, scale=col["fg"][:, d:d + 1]),
                m, tq[1])
        if d == 0:
            s1 = op("dve", lambda e: e.tensor_copy(a1, T[:, 2, :]), q1, so_free)
            s2 = op("dve", lambda e: e.tensor_copy(a2, T[:, 3, :]), q2, so_free)
        else:
            s1 = op("dve", lambda e: e.tensor_tensor(a1, a1, T[:, 2, :], ALU.add), q1, s1)
            s2 = op("dve", lambda e: e.tensor_tensor(a2, a2, T[:, 3, :], ALU.add), q2, s2)
        tq = [s1, s2]
    mk_o = mk
    free[4] = ssm_done
    m1, m2 = token_sums(a1, 3, s1), token_sums(a2, 4, s2)
    r1 = inv_rms(0, 3, m1)
    r2 = inv_rms(1, 4, m2, pre=R4(0), times=R4(0))
    free[5] = ssm_done
    sp2, sp1 = spread(1, 4, r2), spread(0, 5, r1)
    rc2 = op("act", lambda e: e.activation(RS[:, 1, :], bank[4][:, :], ACT.Copy), sp2)

    h2ready, tf = [], [None] * 4
    for k in range(16):
        o = T[:, k % 4, :]
        sh = MOD[:, k:k + 1]
        m = op("dve" if k % 2 == 0 else "pool",
               lambda e: e.tensor_tensor(o, YK[:, k, :], RS[:, 1, :], ALU.mult), rc2, yk[k], tf[k % 4], s1, s2)
        mh = op("act", lambda e: e.activation(h2H[:, k, :], o, ACT.Identity, bias=sh), m, mk_b)
        ml = op("dve", lambda e: e.scalar_tensor_tensor(out=h2L[:, k, :], in0=o, scalar=sh,
                                                        in1=h2H[:, k, :].bitcast(F32), op0=ALU.add,
                                                        op1=ALU.subtract), mh, m, mk_o)
        h2ready.append([mh, ml])
        tf[k % 4] = [mh, ml]
    h2_all = tf
    free[4] = [rc2]
    x1out = [None, None]
    dx1 = [slot(f"dx1{i}") for i in range(2)]

    def residual():
        rc1 = op("act", lambda e: e.activation(RS[:, 0, :], bank[5][:, :], ACT.Copy), sp1)
        free[5] = [rc1]
        for k in range(16):
            x = X1[:, k, :]
            m = op("dve", lambda e: e.scalar_tensor_tensor(out=x, in0=x, scalar=col["fg"][:, k:k + 1],
                                                           in1=RS[:, 0, :], op0=ALU.mult, op1=ALU.mult),
                   rc1, x1raw[k], q2, yk[k])
            x1out[k % 2] = fl.dma(dx1[k % 2], lambda e: e.dma_start(scratch["x1"][k], x), m, x1out[k % 2])
            yield 0.6

    WF = at("WF", 32, [128, 16, 16])
    WFH, WFL = at("WFH", 33, [128, 16, 16], F32R), at("WFL", 34, [128, 16, 16], F32R)
    dwf = slot("wf")
    wf = fl.dma(dwf, lambda e: e.dma_start(WF[:, :, :], t["wf"]), mk_o)
    wfp = split(WFH[:, :, :], WFL[:, :, :], WF[:, :, :], wf, mk_o)
    fps = bank[3][0:16, :]
    EI = at("EI", 196, [16, 512], I32)
    nf = {}

    def forget():
        x, a, b_, c_ = (T[0:16, i, :] for i in range(4))
        n16, e16 = RS[0:16, 0, :], RS[0:16, 1, :]
        bf = col["bf"][0:16, 0:1]
        m = ts(x, fps, bf, None, ALU.add, None, fm, h2_all)
        free[3] = [m]
        stt(a, x, -1.0, x, ALU.mult, ALU.min)
        yield 1.0
        yield from exp_steps(b_, a, n16, c_, EI[:, :])
        yield 8.0
        ts(a, b_, 2.0, None, ALU.add)
        dv(lambda e: e.reciprocal(a, a))
        tt(a, a, b_, ALU.mult)
        tt(c_, a, a, ALU.mult)
        yield 3.0
        ts(b_, c_, 1.0 / 15, None, ALU.mult)
        for n in (13, 11, 9, 7, 5, 3):
            stt(b_, b_, 1.0 / n, c_, ALU.add, ALU.mult)
            yield 0.7
        stt(b_, b_, 1.0, a, ALU.add, ALU.mult)
        ts(x, x, 0.0, None, ALU.min)
        stt(x, b_, -2.0, x, ALU.mult, ALU.add)
        yield 2.0
        ts(x, x, -1.0, None, ALU.mult)
        ones = ONE[0:16, 0:1].to_broadcast([16, 512])
        nf["m"] = dv(lambda e: e.tensor_tensor_scan(NF[:, :], ones, x, 0.0, ALU.mult, ALU.add))
        yield 1.6

    def seq_project(half, dst, func, war):
        bs = [0, 1, 2, 7]
        for kc in range(8):
            n, s, m = chunk()
            for k2 in range(2):
                k = 2 * kc + k2
                wh, wl = WH[:, s, 512 * k2:512 * k2 + 512], WL[:, s, 512 * k2:512 * k2 + 512]
                for q in range(4):
                    b = bs[q]
                    o = slice(128 * q, 128 * q + 128)
                    quiet("pe", lambda e, b=b, o=o, k=k, wh=wh: e.matmul(bank[b][:, :], h2H[:, k, o], wh,
                                                                         start=k == 0, stop=False),
                          m, h2ready[k], free[b] if k == 0 else None)
                    quiet("pe", lambda e, b=b, o=o, k=k, wl=wl: e.matmul(bank[b][:, :], h2H[:, k, o], wl,
                                                                         start=False, stop=False))
                    mark = op("pe", lambda e, b=b, o=o, k=k, wh=wh: e.matmul(bank[b][:, :], h2L[:, k, o], wh,
                                                                             start=False, stop=k == 15))
                    if k == 15:
                        ev = op("act", lambda e, b=b, q=q: e.activation(
                            dst[:, q, 512 * half:512 * half + 512], bank[b][:, :], func), mark, war)
                        free[b] = [ev]
            used[n] = mark
            pump(BUDGET["v"])
        return ev

    free[6] = free[7] = ssm_done
    BUDGET["v"] = 3.0
    beside.append(residual())
    seq_project(0, VV, ACT.Copy, mk_g)
    for k in range(16):
        f_, l_ = k == 0, k == 15
        quiet("pe", lambda e, k=k, f_=f_: e.matmul(fps, WFH[:, k, :], h2H[:, k, :],
                                                   start=f_, stop=False), wfp, h2ready[k], free[3])
        quiet("pe", lambda e, k=k: e.matmul(fps, WFH[:, k, :], h2L[:, k, :], start=False, stop=False))
        if l_:
            fm = op("pe", lambda e, k=k: e.matmul(fps, WFL[:, k, :], h2H[:, k, :], start=False, stop=True))
        else:
            quiet("pe", lambda e, k=k: e.matmul(fps, WFL[:, k, :], h2H[:, k, :], start=False, stop=False))
    beside.append(forget())
    vb = seq_project(1, VV, ACT.Copy, mk_g)
    drain_beside()

    dka = [slot(f"ka{i}") for i in range(2)]
    qa1 = op("pool", lambda e: e.memset(QA[64:65, :, :, :], 1.0), x1out)
    att_free = [None, None]
    prfree = [None]
    ptfree = [None]
    AB = [4, 5, 6, 7]
    yready = {}
    stat = {"n": 0}

    finished = set()

    def attend(j, ready, gate):
        buf = j % 2
        osum = None
        for hh in range(2):
            h = 2 * j + hh
            p = slice(0, 65)
            den = []
            tops = []
            for q in range(4):
                w = 128 * (q + 1)
                b = AB[q]
                mm = op("pe", lambda e, q=q, w=w, b=b: e.matmul(bank[b][:, 0:w], QA[p, buf, hh, 128 * q:128 * q + 128],
                                                                KA[p, buf, hh, 0:w], start=True, stop=True),
                        ready, free[b])
                den.append(mm)
            if hh == 1:
                att_free[buf] = mm
            probs = []
            for q in range(4):
                w = 128 * (q + 1)
                b = AB[q]
                i = stat["n"] % 8
                stat["n"] += 1
                nm, rsum = ST[:, 16 + i:17 + i], ST[:, 24 + i:25 + i]
                m = op("dve", lambda e, b=b, w=w: e.tensor_tensor(bank[b][:, w - 128:w], bank[b][:, w - 128:w],
                                                                  CAU[:, :], ALU.add), den[q], cau)
                m = op("dve", lambda e, b=b, w=w, nm=nm: e.tensor_reduce(nm, bank[b][:, 0:w], AX, ALU.max,
                                                                         negate=True), m)
                m = op("act", lambda e, b=b, w=w, nm=nm, rsum=rsum, q=q: e.activation(
                    PR[:, q, 0:w], bank[b][:, 0:w], ACT.Exp, bias=nm, accum_out=rsum), m, prfree[0])
                free[b] = [m]
                m = op("dve", lambda e, rsum=rsum: e.reciprocal(rsum, rsum), m)
                m = op("dve", lambda e, q=q, w=w, rsum=rsum: e.tensor_scalar(PR[:, q, 0:w], PR[:, q, 0:w], rsum,
                                                                             None, ALU.mult), m)
                probs.append(m)
                yield 1.0
            yield 1.5
            yield 3.0
            pts = []
            for kt in range(4):
                b = AB[kt]
                for q in range(kt, 4):
                    mm = op("pe", lambda e, kt=kt, q=q, b=b: e.transpose(
                        bank[b][:, 128 * q:128 * q + 128], PR[:, q, 128 * kt:128 * kt + 128], IDT[:, :]),
                        probs[q], idt, free[b])
                c0 = 128 * kt
                who = "act" if kt % 2 == 0 else "dve"
                if who == "act":
                    m = op("act", lambda e, b=b, c0=c0, kt=kt: e.activation(PT[:, kt, c0:512], bank[b][:, c0:512],
                                                                            ACT.Copy), mm, ptfree[0])
                else:
                    m = op("dve", lambda e, b=b, c0=c0, kt=kt: e.tensor_copy(PT[:, kt, c0:512], bank[b][:, c0:512]),
                           mm, ptfree[0])
                free[b] = [m]
                pts.append(m)
            prfree[0] = mm
            yield 1.0
            yield 3.0
            o = bank[3][64 * hh:64 * hh + 64, :]
            for kt in range(4):
                c0 = 128 * kt
                mm = op("pe", lambda e, kt=kt, c0=c0, o=o, h=h: e.matmul(
                    o[:, c0:512], VV[:, kt, 64 * h:64 * h + 64], PT[:, kt, c0:512], start=kt == 0, stop=kt == 3,
                    skip_group_check=True), pts[kt], vb, free[3] if hh == 0 else None)
            ptfree[0] = mm
        m = op("dve", lambda e: e.tensor_tensor(YF[:, 8 + j, :], gate[0], bank[3][:, :], ALU.mult), mm, gate[1])
        free[3] = [m]
        gate_free[buf] = m
        yready[8 + j] = m
        finished.add(j)
        yield 0.7

    gate_free = [None, None]
    BUDGET["v"] = 3.2
    for j in range(8):
        buf = j % 2
        b = next_bank()
        mk = project(b, 2, h2H, h2L, h2ready)
        while j >= 2 and j - 2 not in finished:
            pump(1.0)
        ms = []
        for hh in range(2):
            ms.append(op("act", lambda e, b=b, hh=hh: e.activation(QA[0:64, buf, hh, :], bank[b][64 * hh:64 * hh + 64, :],
                                                                   ACT.Copy, scale=0.125),
                         mk, att_free[buf], qa1, x1out))
        free[b] = [ms[-1]]
        pump(BUDGET["v"])
        b = next_bank()
        mk = project(b, 2, h2H, h2L, h2ready)
        for hh in range(2):
            ms.append(op("act", lambda e, b=b, hh=hh: e.activation(KA[0:64, buf, hh, :], bank[b][64 * hh:64 * hh + 64, :],
                                                                   ACT.Copy), mk, att_free[buf], x1out))
        free[b] = [ms[-1]]
        for hh in range(2):
            kd = fl.dma(dka[buf], lambda e, hh=hh, buf=buf, j=j: e.dma_start(KA[64:65, buf, hh, :],
                                                                             NF[2 * j + hh:2 * j + hh + 1, :]),
                        nf["m"], att_free[buf], x1out)
        pump(BUDGET["v"])
        b = next_bank()
        mk = project(b, 2, h2H, h2L, h2ready)
        g_ = SI[:, buf, :]
        gt = op("act", lambda e, b=b, g_=g_: e.activation(g_, bank[b][:, :], ACT.Silu), mk, gate_free[buf],
                si_free[buf])
        free[b] = [gt]
        pump(BUDGET["v"])
        beside.append(attend(j, [*ms, kd, qa1], (g_, gt)))

    SGU = {}
    sgfree = [None, None]
    gated = {}

    def gates(h):
        i = h % 2
        u_, g_ = T[:, i, :], T[:, 2 + i, :]
        b = next_bank()
        mk = project(b, 2, h2H, h2L, h2ready)
        mu_ = op("act", lambda e: e.activation(u_, bank[b][:, :], ACT.Gelu), mk, sgfree[i], nf["m"])
        free[b] = [mu_]
        pump(BUDGET["v"])
        b = next_bank()
        mk = project(b, 2, h2H, h2L, h2ready)
        mg_ = op("act", lambda e: e.activation(g_, bank[b][:, :], ACT.Silu), mk, sgfree[i])
        free[b] = [mg_]
        m = op("dve", lambda e: e.tensor_tensor(YF[:, h, :], u_, g_, ALU.mult), mu_, mg_)
        sgfree[i] = m
        gated[h] = m
        pump(BUDGET["v"])
        return mk

    for h in range(4):
        gates(h)
    drain_beside()
    att_done = [hm_last(fl), free[3]]
    si_free = [*gate_free]
    va1 = seq_project(0, VV, ACT.Gelu, att_done)

    def sgu_const():
        d = slot("ws")
        fl.dma(d, lambda e: e.dma_start(WS[:, :, :], t["wsT"]), att_done)
        ld = fl.dma(d, lambda e: e.dma_start(BSB[:, :, :], t["bsb"]), att_done)
        for h in range(8):
            SGU["w", h] = op("pool", lambda e, h=h: e.affine_select(
                out=WS[:, h, :], in_=WS[:, h, :], compare_op=ALU.is_ge, fill=0.0, base=0,
                pattern=[[1, 128]], channel_multiplier=-1), ld)
        yield 2.0
        for h in range(8):
            b = 4 + h // 4
            mm = op("pe", lambda e, h=h, b=b: e.matmul(bank[b][:, 128 * (h % 4):128 * (h % 4) + 128], ONE[:, :],
                                                       WS[:, h, :], start=h % 4 == 0, stop=h % 4 == 3,
                                                       skip_group_check=True), SGU["w", h], free[b])
            if h % 4 == 3:
                for g in range(h - 3, h + 1):
                    m = op("dve", lambda e, g=g, b=b: e.scalar_tensor_tensor(
                        out=CON[:, g, :], in0=bank[b][:, 128 * (g % 4):128 * (g % 4) + 128],
                        scalar=col["lnb"][:, g:g + 1], in1=BSB[:, g, :], op0=ALU.mult, op1=ALU.add), mm, ld,
                        att_done)
                    SGU["c", g] = m
                free[b] = [m]
                yield 2.0

    beside.append(sgu_const())
    va2 = seq_project(1, VV, ACT.Gelu, att_done)
    lnm = []

    def layer_norm():
        mu, va, rr, yy = (ST[:, 32 + 4 * i:36 + 4 * i] for i in range(4))
        ms = [op("dve", lambda e: e.tensor_reduce(mu[:, q:q + 1], VV[:, q, :], AX, ALU.add), va1, va2)
              for q in range(4)]
        m = op("dve", lambda e: e.tensor_scalar(mu, mu, 1.0 / 1024, None, ALU.mult), ms)
        yield 4.6
        xs = []
        for q in range(4):
            x = VV[:, q, :]
            xs.append(op("dve", lambda e: e.tensor_scalar(x, x, mu[:, q:q + 1], None, ALU.subtract), m))
        yield 4.0
        s = None
        for q in range(4):
            s = op("act", lambda e: e.activation(SQ[:, :], VV[:, q, :], ACT.Square, accum_out=va[:, q:q + 1]),
                   xs[q], s, att_done)
            if q % 2:
                yield 3.0
        m = op("dve", lambda e: e.tensor_scalar(va, va, 1.0 / 1024, EPS, ALU.mult, ALU.add), s)
        m = op("act", lambda e: e.activation(yy, va, ACT.Sqrt), m)
        m = op("dve", lambda e: e.reciprocal(rr, yy), m)
        m = op("dve", lambda e: e.tensor_tensor(yy, rr, rr, ALU.mult), m)
        m = op("dve", lambda e: e.tensor_tensor(yy, yy, va, ALU.mult), m)
        m = op("dve", lambda e: e.tensor_scalar(yy, yy, -0.5, 1.5, ALU.mult, ALU.add), m)
        m = op("dve", lambda e: e.tensor_tensor(rr, rr, yy, ALU.mult), m)
        yield 3.0
        for q in range(4):
            x = VV[:, q, :]
            lnm.append(op("dve", lambda e: e.tensor_scalar(x, x, rr[:, q:q + 1], None, ALU.mult), m))
        yield 4.0

    beside.append(layer_norm())
    mixed = {}
    mfree = [None, None]

    def mix():
        for h in range(8):
            b = 6 + h % 2
            for q in range(4):
                mm = op("pe", lambda e: e.matmul(
                    bank[b][:, 128 * q:128 * q + 128], VV[:, q, 128 * h:128 * h + 128], WS[:, h, :],
                    start=q == 0, stop=q == 3, skip_group_check=True), lnm, SGU["w", h], free[b])
            o = MX[:, h % 2, :]
            o3 = o.rearrange("p (n t) -> p n t", t=128)
            m = op("dve", lambda e: e.scalar_tensor_tensor(
                out=o3, in0=bank[b][:, :].rearrange("p (n t) -> p n t", t=128), scalar=col["lng"][:, h:h + 1],
                in1=CON[:, h:h + 1, :].to_broadcast([128, 4, 128]), op0=ALU.mult, op1=ALU.add),
                mm, SGU["c", h])
            free[b] = [m]
            mixed[h] = (m, mm)
            yield 3.0
            debt[0] += 1.8
            if h >= 4:
                while h not in gated:
                    yield 5.0
            yready[h] = op("dve", lambda e: e.tensor_tensor(YF[:, h, :], YF[:, h, :], o, ALU.mult), m, gated[h])
            yield 0.6

    beside.append(mix())
    for h in range(4, 8):
        mk = gates(h)
    mk_p = mk
    while 7 not in yready:
        pump(1.0)
    mixd = [mixed[h][1] for h in range(8)]

    ysplit = [split(yH[:, k, :], yL[:, k, :], YF[:, k, :], yready[k], mk_p) for k in range(16)]
    acc = None
    x2 = []
    tq = [None, None]
    for d in range(16):
        i, s_, ld = load(scratch["x1"][d], x1out)
        b = next_bank()
        mk = project(b, 2, yH, yL, ysplit)
        x = X2[:, d, :]
        m = op("dve", lambda e, b=b, x=x, d=d, s_=s_: e.scalar_tensor_tensor(
            out=x, in0=bank[b][:, :], scalar=MOD[:, 32 + d:33 + d], in1=s_, op0=ALU.mult, op1=ALU.add),
            mk, ld, mixd, lnm, mixed[7][0])
        free[b] = [m]
        si_free[i] = m
        x2.append(m)
        q1 = op("act", lambda e, x=x, d=d: e.activation(T[:, d % 2, :], x, ACT.Square), m, tq[d % 2], sgfree)
        if d == 0:
            acc = op("dve", lambda e: e.tensor_copy(SO[:, 0, :], T[:, 0, :]), q1)
        else:
            acc = op("dve", lambda e, d=d: e.tensor_tensor(SO[:, 0, :], SO[:, 0, :], T[:, d % 2, :], ALU.add), q1, acc)
        tq[d % 2] = acc
    r3 = spread(2, 4, inv_rms(2, 3, token_sums(SO[:, 0, :], 3, acc)))
    dout = [slot(f"out{i}") for i in range(4)]
    last = [None] * 4
    for d in range(16):
        x = X2[:, d, :]
        m = op("dve", lambda e, x=x, d=d: e.scalar_tensor_tensor(out=x, in0=x, scalar=col["fg2"][:, d:d + 1],
                                                                 in1=bank[4][:, :], op0=ALU.mult, op1=ALU.mult),
               r3, x2[d], q1)
        last[d % 4] = fl.dma(dout[d % 4], lambda e, x=x, d=d: e.dma_start(out[d], x), m, last[d % 4])
    finals = [*last, *so_free, *x1out]

    for sem, value in finals:
        nc.sync.wait_ge(sem, value)


def hm_last(fl):
    return fl.sems["pe"], fl.count["pe"]


mm_last = hm_last


def lay_out(i):
    import numpy as _np

    f = _np.ascontiguousarray

    def chan(w):
        k, n = w.shape
        return f(w.reshape(k // 1024, 8, 128, n // 128, 128).transpose(3, 0, 2, 1, 4)).reshape(
            n // 128, k // 1024, 128, 1024)

    def col(v):
        return v.reshape(-1, 128).T

    w1 = i["w_in"][0]
    w2 = i["w_in_2"][0]
    wide = _np.concatenate([w2[:, 1024:2048], w2[:, 5120:6144]], axis=1)
    wvv = f(wide.reshape(8, 2, 128, 4, 512).transpose(3, 0, 2, 1, 4)).reshape(4, 8, 128, 1024)
    bf = _np.zeros((128, 1), _np.float32)
    bf[:16, 0] = i["b_f_2"][0]
    cols = _np.concatenate([
        col(i["norm_g"][0]), col(i["final_g"]), col(i["norm_g_2"][0]), col(i["final_g_2"]),
        col(i["conv_w"][0].reshape(-1)), col(i["b_glu"][0]), col(i["d_skip"][0].reshape(-1)),
        col(i["b_ada_2"][0]), col(i["c_2"][0]), col(i["ln_v_g_2"][0]), col(i["ln_v_b_2"][0]), bf], axis=1)
    pairs = lambda a: f(a[0].reshape(32, 128).T)

    def b_rows(b):
        o = _np.zeros((8, 4, 2, 16, 2, 64), _np.float32)
        v = b[0].reshape(8, 4, 2, 64, 16)
        for g in range(2):
            o[:, :, g, :, g, :] = v[:, :, g].transpose(0, 1, 3, 2)
        return o.reshape(32, 32, 128)

    def c_rows(c):
        return f(c[0].reshape(32, 2, 16, 64).transpose(1, 3, 0, 2)).reshape(128, 32, 16)

    return {
        "xT": f(i["x"][0].T).reshape(16, 128, 512),
        "w1": chan(w1), "wg": chan(i["w_glu"][0]), "wa": chan(i["w_out_a"][0]), "wb": chan(i["w_out_b"][0]),
        "wo": chan(i["w_o"][0]), "w2": chan(w2[:, :7168]), "wvv": wvv,
        "wf": f(w2[:, 7168:].reshape(16, 128, 16).transpose(1, 0, 2)), "w3": chan(i["w_out_2"][0]),
        "ada": f(i["w_ada_2"][0].reshape(16, 128, 6, 1024).transpose(2, 0, 1, 3)),
        "cols": f(cols), "are": pairs(i["a_re"]), "aim": pairs(i["a_im"]),
        "ldt": pairs(_np.repeat(i["log_dt"][0], 64)[None]),
        "bstk": f(_np.tile(_np.stack([b_rows(i["b_re"]), b_rows(i["b_im"])], axis=2), (1, 3, 1, 1))),
        "cre": c_rows(i["c_re"]), "cim": c_rows(i["c_im"]),
        "wsT": f(i["w_s_2"][0].transpose(2, 0, 1)),
        "bsb": f(_np.broadcast_to(i["b_s_2"][0][None], (128, 8, 128))),
    }


def kernel(**inputs):
    import numpy as _np
    import concourse.bacc as _bacc
    from concourse import mybir as _mybir
    from concourse.bass_utils import run_bass_kernel_spmd as _run

    arrays = lay_out({k: _np.asarray(v) for k, v in inputs.items()})
    nc = _bacc.Bacc("TRN2", target_bir_lowering=False, num_devices=1)
    t = {n: nc.dram_tensor("in_" + n, arrays[n].shape, _mybir.dt.float32, kind="ExternalInput").ap() for n in PARAMS}
    out = nc.dram_tensor("out_y", (16, 128, 512), _mybir.dt.float32, kind="ExternalOutput").ap()
    program(nc, t, out)
    r = _run(nc, [{"in_" + n: arrays[n] for n in PARAMS}], core_ids=[0])
    got = r.results[0]["out_y"]
    return _np.ascontiguousarray(got.reshape(2048, 512).T).reshape(1, 512, 2048)
```

```python
from collections import deque

import numpy as np

from concourse import mybir

F32 = mybir.dt.float32
F32R = mybir.dt.float32r
I32 = mybir.dt.int32
ALU = mybir.AluOpType
ACT = mybir.ActivationFunctionType
AX = mybir.AxisListType.X

S = 512
EPS = 1e-6
KB = 1024
BASE = 16512
MAGIC = 12582912.0
NW = 3
NB = 3
AHEAD = 2

PARAMS = [
    "xT", "w1", "wg", "wa", "wb", "wo", "w2", "wvv", "wf", "w3", "ada", "cols", "are", "aim", "ldt",
    "bstk", "cre", "cim", "wsT", "bsb",
]
COLS = [("g1", 16), ("fg", 16), ("g2", 16), ("fg2", 16), ("cw", 48), ("bglu", 8), ("dsk", 8),
        ("bada", 48), ("c2", 16), ("lng", 8), ("lnb", 8), ("bf", 1)]

class Flow:

    def __init__(self, engines, sems):
        self.engines = engines
        self.sems = sems
        self.count = {e: 0 for e in sems}
        self.seen = {e: {} for e in engines}

    def _wait(self, eng, after):
        todo = list(after)
        while todo:
            t = todo.pop()
            if t is None:
                continue
            if isinstance(t, list):
                todo.extend(t)
                continue
            sem, value = t
            if self.seen[eng].get(id(sem), 0) < value:
                self.seen[eng][id(sem)] = value
                self.engines[eng].wait_ge(sem, value)

    def op(self, eng, fn, *after):
        self._wait(eng, after)
        fn(self.engines[eng]).then_inc(self.sems[eng], 1)
        self.count[eng] += 1
        return self.sems[eng], self.count[eng]

    def quiet(self, eng, fn, *after):
        self._wait(eng, after)
        fn(self.engines[eng])

    def dma(self, slot, fn, *after):
        self._wait("sp", after)
        fn(self.engines["sp"]).then_inc(slot[0], 16)
        slot[1] += 16
        return slot[0], slot[1]

def stream_order(t):
    out = []

    def tiles(tag, w, m):
        for c in range(w.shape[1]):
            out.append((tag, w[m, c]))

    for c in range(2):
        for m in range(2):
            out.append(("u", t["w1"][64 + m, c]))
    for m in range(2, 8):
        tiles("u", t["w1"], 64 + m)
    for m in range(8):
        tiles("zb", t["w1"], 72 + m)
    for m in range(32):
        tiles("gate", t["w1"], 80 + m)
    n = 0
    for c in range(16):
        for part in (0, 2, 1, 3):
            for kc in range(2):
                out.append(("a", t["w1"][16 * part + c, kc]))
                if n % 20 < 16 and n < 120:
                    out.append(("ada", t["ada"][n // 20, n % 20]))
                n += 1
    for m in range(16):
        tiles("wa", t["wa"], m)
    for m in range(8):
        tiles("wg", t["wg"], m)
    for m in range(16):
        tiles("wb", t["wb"], m)
    for m in range(16):
        tiles("wo", t["wo"], m)
    for half in (2, 3):
        tiles("v", t["wvv"], half)
    for j in range(8):
        for m in (24 + j, 32 + j, 48 + j):
            tiles("qkg", t["w2"], m)
    for h in range(4):
        for m in (h, 16 + h):
            tiles("ug", t["w2"], m)
    for half in (0, 1):
        tiles("v", t["wvv"], half)
    for h in range(4, 8):
        for m in (h, 16 + h):
            tiles("ug", t["w2"], m)
    for m in range(16):
        for c in (1, 0):
            out.append(("w3", t["w3"][m, c]))
    return out

def program(nc, t, out):
    sem_names = ["pe", "act", "dve", "pool"]
    fl = Flow({"pe": nc.tensor, "act": nc.scalar, "dve": nc.vector, "pool": nc.gpsimd, "sp": nc.sync},
              {e: nc.alloc_semaphore("s_" + e) for e in sem_names})
    op, quiet = fl.op, fl.quiet

    def slot(name):
        return [nc.alloc_semaphore("d_" + name), 0]

    def at(name, kb, shape, dt=F32):
        return nc.alloc_sbuf_tensor_at(name, shape, dt, offset=BASE + int(kb * KB))

    bank = [nc.alloc_psum_tensor(f"bank{i}", [128, 512], F32) for i in range(8)]
    free = [[] for _ in range(8)]

    scratch = {n: nc.dram_tensor("scr_" + n, [k, 128, 512], F32, kind="Internal").ap()
               for n, k in (("zb", 8), ("ga", 16), ("gb", 16), ("x1", 16))}

    hH, hL = at("hH", 0, [128, 16, 512], F32R), at("hL", 32, [128, 16, 512], F32R)
    MA = at("MA", 0, [128, 16, 512])
    ybH, ybL = at("ybH", 32, [128, 8, 512], F32R), at("ybL", 48, [128, 8, 512], F32R)
    mL = at("mL", 32, [128, 16, 512], F32R)
    X1 = at("X1", 0, [128, 16, 512])
    QA = at("QA", 0, [128, 2, 2, 512], F32R)
    KA = at("KA", 8, [128, 2, 2, 512], F32R)
    PR = at("PR", 16, [128, 1280])
    PT = at("PT", 21, [128, 1280])
    QB = [at("QB0", 180, [128, 2, 512], F32R), at("QB1", 198.25, [128, 2, 512], F32R)]
    KBT = [[at(f"KB{i}{j}", kb, [128, 512], F32R) for j, kb in enumerate(kbs)]
          for i, kbs in enumerate(((26, 28), (30, 196)))]
    WS = at("WS", 0, [128, 8, 128])
    BSB = at("BSB", 4, [128, 8, 128])
    CON = at("CON", 8, [128, 8, 128])
    SQ = at("SQ", 12, [128, 1024])
    MX = at("MX", 16, [128, 2, 512])
    YF = at("YF", 32, [128, 16, 512])
    X2 = at("X2", 0, [128, 16, 512])
    AH, AL = at("AH", 64, [128, 16, 512], F32R), at("AL", 96, [128, 16, 512], F32R)
    XS = at("XS", 96, [128, 16, 512])
    BH, BL = at("BH", 64, [128, 8, 512], F32R), at("BL", 80, [128, 8, 512], F32R)
    mH = at("mH", 96, [128, 16, 512], F32R)
    h2H, h2L = at("h2H", 64, [128, 16, 512], F32R), at("h2L", 96, [128, 16, 512], F32R)
    yH, yL = at("yH", 64, [128, 16, 512], F32R), at("yL", 96, [128, 16, 512], F32R)
    CB = at("CB", 64, [128, 2, 32, 32])
    CR = at("CR", 72, [128, 2, 32, 16])
    SM = at("SM", 76, [128, 32, 32])
    E0 = at("E0", 80, [128, 2, 32, 32])
    W0 = at("W0", 88, [128, 2, 32, 16])
    BRAW = at("BRAW", 92, [96, 2, 2, 128])
    BSTK = at("BSTK", 94, [96, 2, 2, 128], F32R)
    URAW = at("URAW", 96, [96, 2, 512])
    USTK = at("USTK", 100, [96, 2, 512], F32R)
    TAB = at("TAB", 104, [128, 2, 2, 512])
    V = at("V", 112, [128, 4, 512])
    HH = at("HH", 120, [128, 2, 2, 512])
    YK = at("YK", 64, [128, 16, 512])
    W = at("W", 128, [128, NW, 1024])
    WH, WL = at("WH", 140, [128, NB, 1024], F32R), at("WL", 152, [128, NB, 1024], F32R)
    U = at("U", 164, [128, 8, 512])
    VV = at("VV", 164, [128, 4, 1024])
    SO = at("SO", 180, [128, 2, 512])
    SI = at("SI", 184, [128, 2, 512])
    T = at("T", 188, [128, 4, 512])
    CV = at("CV", 196, [128, 514])
    ACC = at("ACC", 198.25, [128, 1024])
    yH8 = [at("yH8", 198.25, [128, 512], F32R)[:, :], at("yH9", 182, [128, 512], F32R)[:, :]]
    yL8 = [at("yL8", 200.25, [128, 512], F32R)[:, :], at("yL9", 196, [128, 512], F32R)[:, :]]
    RS = at("RS", 198.25, [128, 2, 512])
    ncol = sum(n for _, n in COLS)
    PC = at("PC", 202.25, [128, ncol])
    ONE = at("ONE", 203.25, [128, 128])
    IDT = at("IDT", 203.75, [128, 128])
    CAU = at("CAU", 204.25, [128, 128])
    MOD = at("MOD", 204.75, [128, 48])
    SC = at("SC", 205, [128, 16])
    ST = at("ST", 205.25, [128, 80])
    NF = at("NF", 205.75, [16, 512])
    RSA = at("RSA", 205.75, [128, 512])
    col, k = {}, 0
    for name, n in COLS:
        col[name] = PC[:, k:k + n]
        k += n

    order = stream_order(t)
    wsl = [slot(f"w{i}") for i in range(NW)]
    landed, wfree, parts, used = {}, {}, {}, {}
    state = {"next": 0, "split": 0, "use": 0, "cur": [], "lag": 0}
    ada = {"n": 0, "acc": None, "free": None}

    def fetch(i):
        if i < len(order):
            src = order[i][1]
            landed[i] = fl.dma(wsl[i % NW], lambda e, i=i, src=src: e.dma_start(W[:, i % NW, :], src),
                               wfree.get(i - NW))

    low_on = {"every": 0}

    def ada_chunk(i):
        n = ada["n"]
        cb, kt = n // 16, n % 16
        w, c = W[:, i % NW, :], SC[:, kt:kt + 1]
        if kt == 0:
            m = op("dve", lambda e: e.tensor_scalar(ACC[:, :], w, c, None, ALU.mult),
                   landed[i], ada["free"], ada["c"])
        else:
            m = op("dve", lambda e: e.scalar_tensor_tensor(out=ACC[:, :], in0=w, scalar=c, in1=ACC[:, :],
                                                           op0=ALU.mult, op1=ALU.add),
                   landed[i], ada["acc"])
        ada["acc"] = m
        wfree[i] = m
        ada["n"] += 1
        if kt == 15:
            def reduce(cb=cb, m=m):
                for q in range(8):
                    mm = op("pe", lambda e: e.matmul(bank[3][:, q:q + 1], ACC[:, q * 128:(q + 1) * 128],
                                                     ONE[:, 0:1], start=True, stop=True), m, free[3])
                k0 = cb * 8
                free[3] = [op("dve", lambda e: e.tensor_tensor(MOD[:, k0:k0 + 8], bank[3][:, 0:8],
                                                               col["bada"][:, k0:k0 + 8], ALU.add), mm)]
                ada["free"] = free[3]
                ada["mod"] = free[3]
            ada["due"] = (state["use"] + 3, reduce)

    def prepare():
        i = state["next"]
        if i >= len(order):
            return False
        state["next"] += 1
        if order[i][0] == "ada":
            ada_chunk(i)
        else:
            n = state["split"]
            state["split"] += 1
            b = n % NB
            w, wh, wl = W[:, i % NW, :], WH[:, b, :], WL[:, b, :]
            mh = op("act", lambda e: e.activation(wh, w, ACT.Copy), landed[i], used.get(n - NB))
            who = "pool" if low_on["every"] and n % low_on["every"] == 0 else "dve"
            ml = op(who, lambda e: e.tensor_tensor(wl, w, wh.bitcast(F32), ALU.subtract),
                    mh, landed[i], used.get(n - NB))
            wfree[i] = [mh, ml]
            parts[n] = (b, [mh, ml])
        fetch(i + NW)
        return True

    def chunk():
        n = state["use"]
        state["use"] += 1
        if "due" in ada and ada["due"][0] <= n:
            ada.pop("due")[1]()
        while state["split"] <= n + AHEAD and prepare():
            pass
        return n, parts[n][0], parts[n][1]

    beside = deque()
    debt = [0.0]

    def pump(budget):
        debt[0] += budget
        while beside and debt[0] > 0:
            try:
                cost = next(beside[0])
                debt[0] -= cost
            except StopIteration:
                beside.popleft()
        if not beside:
            debt[0] = 0.0

    def drain_beside():
        while beside:
            pump(1.0)

    BUDGET = {"v": 0.0}

    def products8(b, kc, nch, XH, XL, ready, first=0):
        n, s, m = chunk()
        k0, k1 = 8 * first, 8 * (nch - 1 - first) + 7
        for k8 in range(8):
            k = 8 * kc + k8
            wh, wl = WH[:, s, 128 * k8:128 * k8 + 128], WL[:, s, 128 * k8:128 * k8 + 128]
            xh, xl = XH[k] if isinstance(XH, list) else XH[:, k, :], XL[k] if isinstance(XL, list) else XL[:, k, :]
            quiet("pe", lambda e: e.matmul(bank[b][:, :], wh, xh, start=k == k0, stop=False),
                  m, ready[k], free[b] if k == k0 else None)
            quiet("pe", lambda e: e.matmul(bank[b][:, :], wh, xl, start=False, stop=False))

            def low(e):
                return e.matmul(bank[b][:, :], wl, xh, start=False, stop=k == k1)

            if k8 == 7:
                mark = op("pe", low)
            else:
                quiet("pe", low)
        used[n] = mark
        return mark

    def project(b, nch, XH, XL, ready):
        for kc in range(nch):
            mark = products8(b, kc, nch, XH, XL, ready)
            if kc < nch - 1:
                pump(BUDGET["v"])
        return mark

    ring = {"n": 1}

    def next_bank():
        ring["n"] += 1
        return ring["n"] % 3

    def split(H, L, src, after, *war):
        mh = op("act", lambda e: e.activation(H, src, ACT.Copy), after, *war)
        ml = op("dve", lambda e: e.tensor_tensor(L, src, H.bitcast(F32), ALU.subtract), mh, after, *war)
        return [mh, ml]

    d_par = slot("par")
    pc = fl.dma(d_par, lambda e: e.dma_start(PC[:, :], t["cols"]))
    one = op("pool", lambda e: e.memset(ONE[:, :], 1.0))
    z1 = op("pool", lambda e: e.memset(IDT[:, :], 0.0))
    z2 = op("pool", lambda e: e.memset(CAU[:, :], 0.0))
    idt = op("pool", lambda e: e.affine_select(out=IDT[:, :], in_=IDT[:, :], compare_op=ALU.not_equal,
                                               fill=1.0, base=0, pattern=[[-1, 128]],
                                               channel_multiplier=1), z1)
    cau = op("pool", lambda e: e.affine_select(out=CAU[:, :], in_=CAU[:, :], compare_op=ALU.is_ge,
                                               fill=-1e30, base=0, pattern=[[-1, 128]],
                                               channel_multiplier=1), z2)

    def root_table(*after):
        return op("act", lambda e: e.activation(ST[:, 79:80], ONE[:, 0:1], ACT.Sqrt), one, *after)

    root_table()

    dx = [slot(f"x{i}") for i in range(8)]
    xin = []
    for i in range(8):
        if i in (0, 1, 4):
            fetch({0: 0, 1: 1, 4: 2}[i])
        xin.append(fl.dma(dx[i], lambda e: e.dma_start(XS[:, 2 * i:2 * i + 2, :],
                                                       t["xT"][2 * i:2 * i + 2].rearrange("k p s -> p k s"))))
    d_ssm = [slot(f"ssm{i}") for i in range(3)]

    def token_sums(xs, b, *after, qs=range(4)):
        for q in qs:
            for i, x in enumerate(xs):
                mm = op("pe", lambda e: e.matmul(bank[b][:, q:q + 1], x[:, 128 * q:128 * q + 128], ONE[:, 0:1],
                                                 start=i == 0, stop=i == len(xs) - 1), free[b], one, *after)
        return mm

    def inv_rms(i, b, mm, pre=None, times=None, qs=slice(0, 4)):
        r, v, y = R4(i)[:, qs], R4(4)[:, qs], R4(5)[:, qs]
        m = op("dve", lambda e: e.tensor_scalar(v, bank[b][:, qs], 1.0 / 2048, EPS if pre is None else 0.0,
                                                ALU.mult, ALU.add), mm)
        free[b] = [m]
        if pre is not None:
            m = op("dve", lambda e: e.tensor_tensor(v, v, pre, ALU.mult), m)
            m = op("dve", lambda e: e.tensor_tensor(v, v, pre, ALU.mult), m)
            m = op("dve", lambda e: e.tensor_scalar(v, v, EPS, None, ALU.add), m)
        m = op("act", lambda e: e.activation(y, v, ACT.Sqrt), m)
        m = op("dve", lambda e: e.reciprocal(r, y), m)
        m = op("dve", lambda e: e.tensor_tensor(y, r, r, ALU.mult), m)
        m = op("dve", lambda e: e.tensor_tensor(y, y, v, ALU.mult), m)
        m = op("dve", lambda e: e.tensor_scalar(y, y, -0.5, 1.5, ALU.mult, ALU.add), m)
        m = op("dve", lambda e: e.tensor_tensor(r, r, y, ALU.mult), m)
        if times is not None:
            m = op("dve", lambda e: e.tensor_tensor(r, r, times, ALU.mult), m)
        return m

    def spread(i, b, *after, qs=range(4)):
        for q in qs:
            mm = op("pe", lambda e: e.matmul(bank[b][:, 128 * q:128 * q + 128],
                                             R4(i)[:, q:q + 1].to_broadcast([128, 128]), IDT[:, :],
                                             start=True, stop=True), free[b], idt, *after)
        return mm

    def R4(i):
        return ST[:, 56 + 4 * i:60 + 4 * i]

    acc = None
    tfree = [None] * 4
    hready = []
    for k in range(16):
        if k in (0, 2, 8):
            prepare()
        x, g1, tk = XS[:, k, :], col["g1"][:, k:k + 1], T[:, k % 4, :]
        mh = op("act", lambda e: e.activation(hH[:, k, :], x, ACT.Identity, scale=g1), xin[k // 2], pc)
        ml = op("dve", lambda e: e.scalar_tensor_tensor(out=hL[:, k, :], in0=x, scalar=g1,
                                                        in1=hH[:, k, :].bitcast(F32), op0=ALU.mult,
                                                        op1=ALU.subtract), xin[k // 2], pc, mh)
        hready.append([mh, ml])
        sq = op("act", lambda e: e.activation(tk, x, ACT.Square), xin[k // 2], tfree[k % 4])
        if k == 0:
            acc = op("pool", lambda e: e.tensor_copy(SO[:, 0, :], tk), sq)
        else:
            acc = op("pool", lambda e: e.tensor_tensor(SO[:, 0, :], SO[:, 0, :], tk, ALU.add), sq, acc)
        tfree[k % 4] = acc
    xs_free = [*hready[-1], sq, acc]
    ada["free"] = hready[-1]
    ada["c"] = op("act", lambda e: e.activation(SC[:, :], col["c2"], ACT.Silu), pc)

    dve_last = [None]

    def dv(fn, *after):
        dve_last[0] = op("dve", fn, dve_last[0], *after)
        return dve_last[0]

    def ts(o, a, s1, s2, o0, o1=None, *after):
        if o1 is None:
            return dv(lambda e: e.tensor_scalar(o, a, s1, None, o0), *after)
        return dv(lambda e: e.tensor_scalar(o, a, s1, s2, o0, o1), *after)

    def tt(o, a, b, o0, *after):
        return dv(lambda e: e.tensor_tensor(o, a, b, o0), *after)

    def stt(o, a, s, b, o0, o1, *after):
        return dv(lambda e: e.scalar_tensor_tensor(out=o, in0=a, scalar=s, in1=b, op0=o0, op1=o1), *after)

    def exp_steps(dst, x, n, r, sc, *after):
        ts(dst, x, -87.3, 88.7, ALU.max, ALU.min, *after)
        ts(n, dst, 1.4426950408889634, MAGIC, ALU.mult, ALU.add)
        ts(n, n, -MAGIC, None, ALU.add)
        stt(r, n, -0.693359375, dst, ALU.mult, ALU.add)
        stt(r, n, 2.12194440e-4, r, ALU.mult, ALU.add)
        yield 1.1
        ts(dst, r, 1.0 / 5040, None, ALU.mult)
        for c in (1.0 / 720, 1.0 / 120, 1.0 / 24, 1.0 / 6, 0.5, 1.0):
            stt(dst, dst, c, r, ALU.add, ALU.mult)
        yield 1.6
        ts(dst, dst, 1.0, None, ALU.add)
        ts(sc, n, 127.0, 8388608.0, ALU.add, ALU.mult)
        tt(dst, dst, sc.bitcast(F32), ALU.mult)
        stt(dst, x, -87.3, dst, ALU.is_gt, ALU.mult)
        yield 1.0

    def sm(i):
        return SM[:, i, :]

    SMI = at("SMI", 76 + 3.75, [128, 32], I32)

    ssm = {}

    def ssm_params(tiles):
        da = fl.dma(d_ssm[0], lambda e: e.dma_start(sm(0), t["are"]))
        db = fl.dma(d_ssm[1], lambda e: e.dma_start(sm(1), t["aim"]))
        dc = fl.dma(d_ssm[2], lambda e: e.dma_start(sm(2), t["ldt"]))
        d_c = slot("cr")
        fl.dma(d_c, lambda e: e.dma_start(CR[:, 0], t["cre"]))
        dcr = fl.dma(d_c, lambda e: e.dma_start(CR[:, 1], t["cim"]))
        cz = op("pool", lambda e: e.memset(CB[:, :, :, :], 0.0))
        yield 0.1
        are, aim, ldt, dt, zr, zi, n, r, mag = (sm(i) for i in range(9))
        yield from exp_steps(dt, ldt, n, r, SMI[:, :], dc)
        tt(zr, are, dt, ALU.mult, da)
        tt(zi, aim, dt, ALU.mult, db)
        yield from exp_steps(mag, zr, n, r, SMI[:, :])
        m, y, q, y2, sn, cs, aq, sq_, t0 = (sm(i) for i in range(9, 18))
        ts(m, zi, 0.6366197723675814, MAGIC, ALU.mult, ALU.add)
        ts(m, m, -MAGIC, None, ALU.add)
        rest = np.pi / 2
        for i, bits in enumerate((7, 19, 30, 60)):
            part = float(np.floor(rest * 2.0 ** bits) / 2.0 ** bits) if i < 3 else float(rest)
            rest -= part
            stt(y, m, -part, zi if i == 0 else y, ALU.mult, ALU.add)
        ts(q, m, 0.25, MAGIC, ALU.mult, ALU.add)
        ts(q, q, -MAGIC, None, ALU.add)
        stt(q, q, -4.0, m, ALU.mult, ALU.add)
        yield 2.7
        tt(y2, y, y, ALU.mult)
        ts(sn, y2, 1.0 / 362880, None, ALU.mult)
        for c in (-1.0 / 5040, 1.0 / 120, -1.0 / 6):
            stt(sn, sn, c, y2, ALU.add, ALU.mult)
        stt(sn, sn, 1.0, y, ALU.add, ALU.mult)
        ts(cs, y2, -1.0 / 3628800, None, ALU.mult)
        for c in (1.0 / 40320, -1.0 / 720, 1.0 / 24, -0.5):
            stt(cs, cs, c, y2, ALU.add, ALU.mult)
        ts(cs, cs, 1.0, None, ALU.add)
        yield 3.2
        stt(aq, q, -1.0, q, ALU.mult, ALU.max)
        ts(t0, aq, -1.0, 2.0, ALU.mult, ALU.add)
        tt(sq_, t0, q, ALU.mult)
        ts(aq, aq, -1.0, 1.0, ALU.mult, ALU.add)
        sinz, cosz, t1, t2 = (sm(i) for i in range(18, 22))
        tt(t1, sn, aq, ALU.mult)
        tt(t2, cs, sq_, ALU.mult)
        tt(sinz, t1, t2, ALU.add)
        tt(t1, cs, aq, ALU.mult)
        tt(t2, sn, sq_, ALU.mult)
        tt(cosz, t1, t2, ALU.subtract)
        yield 2.6
        lr, li, fr, fi, den = (sm(i) for i in range(22, 27))
        tt(lr, mag, cosz, ALU.mult)
        ts(lr, lr, -1.0, None, ALU.add)
        tt(li, mag, sinz, ALU.mult)
        tt(den, are, are, ALU.mult)
        tt(t1, aim, aim, ALU.mult)
        tt(den, den, t1, ALU.add)
        dv(lambda e: e.reciprocal(den, den))
        tt(t1, lr, are, ALU.mult)
        tt(t2, li, aim, ALU.mult)
        tt(t1, t1, t2, ALU.add)
        tt(fr, t1, den, ALU.mult)
        tt(t1, li, are, ALU.mult)
        tt(t2, lr, aim, ALU.mult)
        tt(t1, t1, t2, ALU.subtract)
        tt(fi, t1, den, ALU.mult)
        yield 3.8
        t3, t4 = (V[:, i, :].rearrange("p (j c) -> p j c", c=16) for i in range(2))
        frb = fr.unsqueeze(2).to_broadcast([128, 32, 16])
        fib = fi.unsqueeze(2).to_broadcast([128, 32, 16])
        tt(t3, CR[:, 0], frb, ALU.mult, dcr, xs_free)
        tt(t4, CR[:, 1], fib, ALU.mult)
        for g in range(2):
            p = slice(64 * g, 64 * g + 64)
            tt(CB[p, 0, :, 16 * g:16 * g + 16], t3[p], t4[p], ALU.subtract, cz)
        tt(t3, CR[:, 0], fib, ALU.mult)
        tt(t4, CR[:, 1], frb, ALU.mult)
        yield 4.2
        tt(t3, t3, t4, ALU.add)
        for g in range(2):
            p = slice(64 * g, 64 * g + 64)
            ts(CB[p, 1, :, 16 * g:16 * g + 16], t3[p], -1.0, None, ALU.mult)
        ssm["cb"] = dve_last[0]
        yield 1.6
        pr, pi, nr = (sm(i) for i in range(27, 30))
        tmp, tmp2 = (V[:, i, :].rearrange("p (j n) -> p j n", n=16) for i in (2, 3))
        dv(lambda e: e.tensor_copy(pr, cosz))
        dv(lambda e: e.tensor_copy(pi, sinz))
        for big, levels in ((E0, 5), (W0, 4)):
            dv(lambda e, big=big: e.memset(big[:, 0, :, 0:1], 1.0))
            dv(lambda e, big=big: e.memset(big[:, 1, :, 0:1], 0.0))
            next(tiles)
            for lv in range(levels):
                if lv == 3 and big is W0:
                    next(tiles)
                w = 1 << lv
                a_r, a_i = big[:, 0, :, 0:w], big[:, 1, :, 0:w]
                o_r, o_i = big[:, 0, :, w:2 * w], big[:, 1, :, w:2 * w]
                b_r = pr.unsqueeze(2).to_broadcast([128, 32, w])
                b_i = pi.unsqueeze(2).to_broadcast([128, 32, w])
                x1_, x2_ = tmp[:, :, 0:w], tmp2[:, :, 0:w]
                tt(x1_, a_r, b_r, ALU.mult, xs_free)
                tt(x2_, a_i, b_i, ALU.mult)
                tt(o_r, x1_, x2_, ALU.subtract)
                tt(x1_, a_r, b_i, ALU.mult)
                tt(x2_, a_i, b_r, ALU.mult)
                tt(o_i, x1_, x2_, ALU.add)
                yield 1.3 + 0.2 * w
                tt(t1, pr, pr, ALU.mult)
                tt(t2, pi, pi, ALU.mult)
                tt(nr, pr, pi, ALU.mult)
                tt(pr, t1, t2, ALU.subtract)
                ts(pi, nr, 2.0, None, ALU.mult)
                yield 1.1
        ssm["turn"] = dve_last[0]
        ssm["mag"] = mag

    uready = [None] * 8
    ssm["y"] = [None] * 8

    def ssm_tiles():
        tabfree, hfree, tab, hm = [None] * 2, [None] * 2, {}, {}
        bufree = [None, None]
        bu, stk, raw = {}, {}, {}
        dstk, dstb = [slot(f"stk{i}") for i in range(2)], [slot(f"stb{i}") for i in range(2)]
        rawfree, stkfree = [None, None], [None, None]

        def table(j, part):
            b = j % 2
            er = E0[:, 0, j:j + 1, :].to_broadcast([128, 16, 32])
            ei = E0[:, 1, j:j + 1, :].to_broadcast([128, 16, 32])
            wr = W0[:, 0, j, :].unsqueeze(2).to_broadcast([128, 16, 32])
            wi = W0[:, 1, j, :].unsqueeze(2).to_broadcast([128, 16, 32])
            c = TAB[:, b, 0, :].rearrange("p (a i) -> p a i", i=32)
            s = TAB[:, b, 1, :].rearrange("p (a i) -> p a i", i=32)
            x1_ = T[:, 2, :].rearrange("p (a i) -> p a i", i=32)
            x2_ = T[:, 3, :].rearrange("p (a i) -> p a i", i=32)
            P = "pool"
            if part == 0:
                m = op(P, lambda e: e.tensor_tensor(c, er, wr, ALU.mult), ssm["turn"], tabfree[b])
                m2 = op(P, lambda e: e.tensor_tensor(x1_, ei, wi, ALU.mult), tab.get(j - 1))
                op(P, lambda e: e.tensor_tensor(c, c, x1_, ALU.subtract), m, m2)
                return
            m3 = op(P, lambda e: e.tensor_tensor(s, er, wi, ALU.mult))
            m4 = op(P, lambda e: e.tensor_tensor(x2_, ei, wr, ALU.mult))
            tab[j] = op(P, lambda e: e.tensor_tensor(s, s, x2_, ALU.add), m3, m4)

        def stack_load(j):
            ut, i, s = j // 4, j % 4, j % 2
            for z in range(3):
                du = fl.dma(dstk[s], lambda e: e.dma_start(URAW[32 * z:32 * z + 32, s, :],
                                                           U[32 * i:32 * i + 32, ut, :]),
                            uready[ut], rawfree[s], xs_free)
            db = fl.dma(dstb[s], lambda e: e.dma_start(BRAW[:, s, :, :], t["bstk"][j]), rawfree[s], xs_free)
            raw[j] = (du, db)

        def stack_high(j):
            s = j % 2
            du, db = raw[j]
            mu = op("act", lambda e: e.activation(USTK[:, s, :], URAW[:, s, :], ACT.Copy), du, stkfree[s])
            mb = op("act", lambda e: e.activation(BSTK[:, s, :, :], BRAW[:, s, :, :], ACT.Copy), db, stkfree[s])
            stk[j] = [mu, mb]

        def stack_low(j):
            s = j % 2
            mu, mb = stk[j]
            ul, bl = USTK[0:32, s, :], BSTK[64:96, s, :, :]
            m1 = op("pool", lambda e: e.tensor_tensor(ul, URAW[0:32, s, :], ul.bitcast(F32), ALU.subtract), mu)
            m2 = op("dve", lambda e: e.tensor_tensor(bl, BRAW[64:96, s, :, :], bl.bitcast(F32), ALU.subtract), mb)
            rawfree[s] = [m1, m2]
            stk[j] = [m1, m2, mu, mb]

        def products(j):
            b = 4 + 2 * (j % 2)
            s = j % 2
            for z in range(2):
                bu[j] = op("pe", lambda e: e.matmul(bank[b + z][:, :], BSTK[:, s, z, :], USTK[:, s, :],
                                                    start=True, stop=True), stk[j], bufree[j % 2])
            stkfree[s] = bu[j]

        def readout(j):
            ut, i = j // 4, j % 4
            o = bank[3][32 * i:32 * i + 32, :]
            quiet("pe", lambda e: e.matmul(o, CB[:, 0, j, :], HH[:, j % 2, 0, :], start=True, stop=False),
                  hm[j], ssm["cb"], free[3])
            hfree[j % 2] = op("pe", lambda e: e.matmul(o, CB[:, 1, j, :], HH[:, j % 2, 1, :],
                                                       start=False, stop=True))

        def skip_term(ut):
            m = op("dve", lambda e: e.scalar_tensor_tensor(out=U[:, ut, :], in0=U[:, ut, :],
                                                           scalar=col["dsk"][:, ut:ut + 1], in1=bank[3][:, :],
                                                           op0=ALU.mult, op1=ALU.add), hfree[1])
            free[3] = [m]
            ssm["y"][ut] = m

        stack_load(0)
        stack_load(1)
        yield
        for i in range(2):
            stack_high(i)
            stack_low(i)
            stack_load(i + 2)
        yield
        products(0)
        yield
        table(0, 0)
        table(0, 1)
        mag = ssm["mag"]
        yield 3.0
        for j in range(32):
            if j + 1 < 32:
                table(j + 1, 0)
                products(j + 1)
            if j + 2 < 32:
                stack_high(j + 2)
            c, s = TAB[:, j % 2, 0, :], TAB[:, j % 2, 1, :]
            br, bi = bank[4 + 2 * (j % 2)][:, :], bank[5 + 2 * (j % 2)][:, :]
            v = [V[:, i, :] for i in range(4)]
            a = op("dve", lambda e: e.tensor_tensor(v[0], c, br, ALU.mult), tab[j], bu[j], dve_last[0])
            b = op("dve", lambda e: e.tensor_tensor(v[1], s, bi, ALU.mult))
            yield 1.2
            c2 = op("dve", lambda e: e.tensor_tensor(v[2], c, bi, ALU.mult))
            d = op("dve", lambda e: e.tensor_tensor(v[3], s, br, ALU.mult))
            bufree[j % 2] = d
            yield 1.2
            if j + 2 < 32:
                stack_low(j + 2)
            if j + 4 < 32:
                stack_load(j + 4)
            a = op("dve", lambda e: e.tensor_tensor(v[0], v[0], v[1], ALU.add), a, b)
            b = op("dve", lambda e: e.tensor_tensor(v[2], v[2], v[3], ALU.subtract), c2, d)
            yield 1.2
            rb = mag[:, j:j + 1].to_broadcast([128, 512])
            a = op("dve", lambda e: e.tensor_tensor_scan(v[1], rb, v[0], 0.0, ALU.mult, ALU.add), a)
            yield 1.1
            if j + 1 < 32:
                table(j + 1, 1)
            b = op("dve", lambda e: e.tensor_tensor_scan(v[3], rb, v[2], 0.0, ALU.mult, ALU.add), b)
            yield 1.1
            if j >= 1:
                readout(j - 1)
            hr, hi = HH[:, j % 2, 0, :], HH[:, j % 2, 1, :]
            c2 = op("dve", lambda e: e.tensor_tensor(v[0], c, v[1], ALU.mult), a)
            d = op("dve", lambda e: e.tensor_tensor(v[2], s, v[3], ALU.mult), b)
            yield 1.2
            f = op("dve", lambda e: e.tensor_tensor(hr, v[0], v[2], ALU.subtract), c2, d, hfree[j % 2])
            f = op("dve", lambda e: e.tensor_tensor(v[0], s, v[1], ALU.mult), f)
            g = op("dve", lambda e: e.tensor_tensor(v[2], c, v[3], ALU.mult))
            tabfree[j % 2] = g
            yield 1.8
            hm[j] = op("dve", lambda e: e.tensor_tensor(hi, v[0], v[2], ALU.add), f, g)
            dve_last[0] = hm[j]
            yield 0.6
            if j >= 1 and j % 4 == 0:
                skip_term(j // 4 - 1)
                yield 0.6
        yield 3.0
        readout(31)
        skip_term(7)

    BUDGET["v"] = 3.2
    tiles = ssm_tiles()
    beside.append(ssm_params(tiles))
    def keep_u(m, b, mk):
        uready[m] = op("dve", lambda e: e.tensor_tensor(U[:, m, :], bank[b][:, :], RSA[:, :], ALU.mult), mk, rsa)
        free[b] = [uready[m]]
        pump(BUDGET["v"])

    for kc in range(2):
        for b in range(2):
            mk = products8(b, kc, 2, hH, hL, hready)
            if (kc, b) == (1, 0):
                sums = token_sums([SO[:, 0, :]], 3, acc)
                rs = inv_rms(0, 3, sums)
            if (kc, b) == (1, 0):
                mk0 = mk
    rsa = op("act", lambda e: e.activation(RSA[:, :], bank[3][:, :], ACT.Copy), spread(0, 3, rs))
    free[3] = [rsa]
    keep_u(0, 0, mk0)
    keep_u(1, 1, mk)
    for m in range(2, 8):
        b = next_bank()
        keep_u(m, b, project(b, 2, hH, hL, hready))
    beside.append(tiles)
    BUDGET["v"] = 4.4
    low_on["every"] = 2
    so = [slot(f"so{i}") for i in range(2)]
    so_free = [None, None]
    so_n = [0]

    def spill(func, b, mk, dst):
        i = so_n[0] % 2
        so_n[0] += 1
        m = op("dve", lambda e: e.tensor_tensor(SO[:, i, :], bank[b][:, :], RSA[:, :], ALU.mult), mk, rsa,
               so_free[i], sums)
        free[b] = [m]
        m = op("act", lambda e: e.activation(SO[:, i, :], SO[:, i, :], func), m)
        so_free[i] = fl.dma(so[i], lambda e: e.dma_start(dst, SO[:, i, :]), m)
        return so_free[i]

    stored = {}
    for m in range(8):
        b = next_bank()
        mk = project(b, 2, hH, hL, hready)
        stored["zb", m] = spill(ACT.Silu, b, mk, scratch["zb"][m])
        pump(BUDGET["v"])
    for m in range(32):
        b = next_bank()
        mk = project(b, 2, hH, hL, hready)
        which, i = ("ga", m) if m < 16 else ("gb", m - 16)
        stored[which, i] = spill(ACT.Sigmoid, b, mk, scratch[which][i])
        pump(BUDGET["v"])
    drain_beside()
    low_on["every"] = 0
    ssm_done = [ssm["y"][7], hm_last(fl)]

    RSS = SI[:, 1, :]
    rss = op("dve", lambda e: e.tensor_tensor(RSS, RSA[:, :], RSA[:, :], ALU.mult), rsa)
    cvz = op("dve", lambda e: e.memset(CV[:, 0:2], 0.0))
    aready = []
    t1free = t0free = t2free = None
    for c in range(16):
        b = next_bank()
        mk = project(b, 2, hH, hL, hready)
        v_ = op("act", lambda e, b=b: e.activation(T[:, 0, :], bank[b][:, :], ACT.Copy), mk, t0free)
        free[b] = [v_]
        b = next_bank()
        mk = project(b, 2, hH, hL, hready)
        m = op("dve", lambda e, b=b: e.tensor_tensor(CV[:, 2:514], bank[b][:, :], T[:, 0, :], ALU.mult), mk, v_)
        t0free = m
        free[b] = [m]
        m = op("dve", lambda e: e.tensor_tensor(CV[:, 2:514], CV[:, 2:514], RSS, ALU.mult), m, rss)

        def w(i, c=c):
            return col["cw"][:, 16 * i + c:16 * i + c + 1]

        o = T[:, 1, :]
        m = op("dve", lambda e, o=o, w=w: e.tensor_scalar(o, CV[:, 0:512], w(0), None, ALU.mult), m, cvz, t1free)
        m = op("dve", lambda e, o=o, w=w: e.scalar_tensor_tensor(out=o, in0=CV[:, 1:513], scalar=w(1), in1=o,
                                                                 op0=ALU.mult, op1=ALU.add), m)
        m = op("dve", lambda e, o=o, w=w: e.scalar_tensor_tensor(out=o, in0=CV[:, 2:514], scalar=w(2), in1=o,
                                                                 op0=ALU.mult, op1=ALU.add), m)
        cv_free = m
        b = next_bank()
        mk = project(b, 2, hH, hL, hready)
        m = op("dve", lambda e, b=b, o=o: e.tensor_tensor(o, o, bank[b][:, :], ALU.mult), mk, m)
        free[b] = [m]
        b = next_bank()
        mk = project(b, 2, hH, hL, hready)
        z = op("dve", lambda e: e.tensor_tensor(T[:, 2, :], bank[b][:, :], RSA[:, :], ALU.mult), mk, t2free, rsa,
               ssm_done)
        free[b] = [z]
        z = op("act", lambda e: e.activation(T[:, 2, :], T[:, 2, :], ACT.Silu), z)
        z = op("pool", lambda e: e.tensor_tensor(T[:, 2, :], T[:, 2, :], RSA[:, :], ALU.mult), z, rsa)
        m = op("dve", lambda e, o=o: e.tensor_tensor(o, o, T[:, 2, :], ALU.mult), m, z)
        t2free = m
        aready.append(split(AH[:, c, :], AL[:, c, :], o, m, ssm_done))
        t1free = aready[-1]

    ybready = [None] * 8

    def yb_parts():
        gl = []
        for i in range(8):
            gl.append(op("act", lambda e, i=i: e.activation(U[:, i, :], U[:, i, :], ACT.Gelu_apprx_tanh),
                         ssm["y"][i]))
        yield 4.0
        for i in range(8):
            ybready[i] = split(ybH[:, i, :], ybL[:, i, :], U[:, i, :], gl[i], mk_h)
            yield 1.2

    mk_h = mk
    beside.append(yb_parts())
    si = [slot(f"si{i}") for i in range(2)]
    si_free = [None, aready[-1]]
    si_n = [0]

    def load(src, after=None):
        i = si_n[0] % 2
        si_n[0] += 1
        return i, SI[:, i, :], fl.dma(si[i], lambda e: e.dma_start(SI[:, i, :], src), after, si_free[i])

    BUDGET["v"] = 3.0
    ma = []
    for d in range(16):
        i, s_, ld = load(scratch["ga"][d], stored["ga", d])
        b = next_bank()
        mk = project(b, 2, AH, AL, aready)
        m = op("dve", lambda e, b=b, d=d, s_=s_: e.tensor_tensor(MA[:, d, :], bank[b][:, :], s_, ALU.mult), mk, ld)
        free[b] = [m]
        si_free[i] = m
        ma.append(m)
        pump(BUDGET["v"])
    drain_beside()
    mk_a = mk

    bready = []
    tf = [None, None]
    for g in range(8):
        i, s_, ld = load(scratch["zb"][g], stored["zb", g])
        b = next_bank()
        mk = project(b, 1, ybH, ybL, ybready)
        o = T[:, g % 2, :]
        m = op("act", lambda e, b=b, g=g, o=o: e.activation(o, bank[b][:, :], ACT.Sigmoid,
                                                            bias=col["bglu"][:, g:g + 1]), mk, tf[g % 2])
        free[b] = [m]
        m = op("dve", lambda e, g=g, o=o: e.tensor_tensor(o, o, U[:, g, :], ALU.mult), m)
        m = op("dve", lambda e, o=o, s_=s_: e.tensor_tensor(o, o, s_, ALU.mult), m, ld)
        si_free[i] = m
        bready.append(split(BH[:, g, :], BL[:, g, :], o, m, mk_a))
        tf[g % 2] = bready[-1]
    mk_g = mk

    mready = []
    for d in range(16):
        i, s_, ld = load(scratch["gb"][d], stored["gb", d])
        b = next_bank()
        mk = project(b, 1, BH, BL, bready)
        o = T[:, d % 2, :]
        m = op("dve", lambda e, b=b, o=o, s_=s_: e.tensor_tensor(o, bank[b][:, :], s_, ALU.mult), mk, ld, tf[d % 2])
        free[b] = [m]
        si_free[i] = m
        m = op("dve", lambda e, o=o, d=d: e.tensor_tensor(o, o, MA[:, d, :], ALU.add), m, ma[d])
        mready.append(split(mH[:, d, :], mL[:, d, :], o, m, [mk_a, mk_g]))
        tf[d % 2] = mready[-1]

    a1, a2 = SO[:, 0, :], SO[:, 1, :]
    mk_b = mk
    g2s = ST[:, 0:16]
    gm = op("dve", lambda e: e.tensor_scalar(g2s, MOD[:, 16:32], 1.0, None, ALU.add), ada["mod"])
    gm = op("dve", lambda e: e.tensor_tensor(g2s, g2s, col["g2"], ALU.mult), gm)
    x1raw, yk, s1, s2 = [], [], None, None
    tq = [None, None]
    for d in range(16):
        if d == 15:
            root_table()
        i, s_, ld = load(t["xT"][d])
        b = next_bank()
        mk = project(b, 2, mH, mL, mready)
        x = X1[:, d, :]
        m = op("dve", lambda e, b=b, x=x, s_=s_: e.tensor_tensor(x, bank[b][:, :], s_, ALU.add), mk, ld)
        free[b] = [m]
        si_free[i] = m
        x1raw.append(m)
        yk.append(op("pool", lambda e: e.tensor_scalar(YK[:, d, :], x, col["fg"][:, d:d + 1], g2s[:, d:d + 1],
                                                       ALU.mult, ALU.mult), m, gm, mk_b))
        q1 = op("act", lambda e, x=x: e.activation(T[:, 2, :], x, ACT.Square), m, tq[0])
        q2 = op("act", lambda e, x=x, d=d: e.activation(T[:, 3, :], x, ACT.Square, scale=col["fg"][:, d:d + 1]),
                m, tq[1])
        if d == 0:
            s1 = op("dve", lambda e: e.tensor_copy(a1, T[:, 2, :]), q1, so_free)
            s2 = op("dve", lambda e: e.tensor_copy(a2, T[:, 3, :]), q2, so_free)
        else:
            if d < 15:
                s1 = op("dve", lambda e: e.tensor_tensor(a1, a1, T[:, 2, :], ALU.add), q1, s1)
            s2 = op("dve", lambda e: e.tensor_tensor(a2, a2, T[:, 3, :], ALU.add), q2, s2)
        tq = [s1, s2]
    mk_o = mk
    free[4] = ssm_done
    m1, m2 = token_sums([a1, T[:, 2, :]], 3, s1, q1), token_sums([a2], 4, s2)
    r1 = inv_rms(0, 3, m1)
    r2 = inv_rms(1, 4, m2, pre=R4(0), times=R4(0))
    free[5] = ssm_done
    sp2, sp1 = spread(1, 4, r2), spread(0, 5, r1)
    rc2 = op("act", lambda e: e.activation(RS[:, 1, :], bank[4][:, :], ACT.Copy), sp2)

    h2ready, tf = [], [None] * 4

    def modulated(k):
        o = T[:, k % 4, :]
        sh = MOD[:, k:k + 1]
        m = op("dve" if k % 2 == 0 else "pool",
               lambda e: e.tensor_tensor(o, YK[:, k, :], RS[:, 1, :], ALU.mult), rc2, yk[k], tf[k % 4], s1, s2, m1, m2)
        mh = op("act", lambda e: e.activation(h2H[:, k, :], o, ACT.Identity, bias=sh), m, mk_b)
        ml = op("dve", lambda e: e.scalar_tensor_tensor(out=h2L[:, k, :], in0=o, scalar=sh,
                                                        in1=h2H[:, k, :].bitcast(F32), op0=ALU.add,
                                                        op1=ALU.subtract), mh, m, mk_o)
        h2ready.append([mh, ml])
        tf[k % 4] = [mh, ml]

    for k in range(4):
        modulated(k)
    free[4] = [rc2]
    x1out = [None, None]
    dx1 = [slot(f"dx1{i}") for i in range(2)]

    def residual():
        rc1 = op("act", lambda e: e.activation(RS[:, 0, :], bank[5][:, :], ACT.Copy), sp1)
        free[5] = [rc1]
        for k in range(16):
            x = X1[:, k, :]
            m = op("dve", lambda e: e.scalar_tensor_tensor(out=x, in0=x, scalar=col["fg"][:, k:k + 1],
                                                           in1=RS[:, 0, :], op0=ALU.mult, op1=ALU.mult),
                   rc1, x1raw[k], q2, yk[k])
            x1out[k % 2] = fl.dma(dx1[k % 2], lambda e: e.dma_start(scratch["x1"][k], x), m, x1out[k % 2])
            yield 0.6

    WF = at("WF", 32, [128, 16, 16])
    WFH, WFL = at("WFH", 33, [128, 16, 16], F32R), at("WFL", 34, [128, 16, 16], F32R)
    dwf = slot("wf")
    wf = fl.dma(dwf, lambda e: e.dma_start(WF[:, :, :], t["wf"]), mk_o)
    wfp = split(WFH[:, :, :], WFL[:, :, :], WF[:, :, :], wf, mk_o)
    fps = bank[3][0:16, :]
    EI = at("EI", 196, [16, 512], I32)
    nf = {}

    def forget():
        x, a, b_, c_ = (T[0:16, i, :] for i in range(4))
        n16, e16 = RS[0:16, 0, :], RS[0:16, 1, :]
        bf = col["bf"][0:16, 0:1]
        m = ts(x, fps, bf, None, ALU.add, None, fm, tf)
        free[3] = [m]
        stt(a, x, -1.0, x, ALU.mult, ALU.min)
        yield 1.0
        yield from exp_steps(b_, a, n16, c_, EI[:, :])
        yield 8.0
        ts(a, b_, 2.0, None, ALU.add)
        dv(lambda e: e.reciprocal(a, a))
        tt(a, a, b_, ALU.mult)
        tt(c_, a, a, ALU.mult)
        yield 3.0
        ts(b_, c_, 1.0 / 15, None, ALU.mult)
        for n in (13, 11, 9, 7, 5, 3):
            stt(b_, b_, 1.0 / n, c_, ALU.add, ALU.mult)
            yield 0.7
        stt(b_, b_, 1.0, a, ALU.add, ALU.mult)
        ts(x, x, 0.0, None, ALU.min)
        stt(x, b_, -2.0, x, ALU.mult, ALU.add)
        yield 2.0
        ts(x, x, -1.0, None, ALU.mult)
        ones = ONE[0:16, 0:1].to_broadcast([16, 512])
        nf["m"] = dv(lambda e: e.tensor_tensor_scan(NF[:, :], ones, x, 0.0, ALU.mult, ALU.add))
        yield 1.6

    def seq_project(half, dst, func, war):
        bs = [0, 1, 2, 7]
        for kc in range(8):
            n, s, m = chunk()
            while len(h2ready) < min(16, 2 * kc + 6):
                modulated(len(h2ready))
            for k2 in range(2):
                k = 2 * kc + k2
                wh, wl = WH[:, s, 512 * k2:512 * k2 + 512], WL[:, s, 512 * k2:512 * k2 + 512]
                for q in range(4):
                    b = bs[q]
                    o = slice(128 * q, 128 * q + 128)
                    quiet("pe", lambda e, b=b, o=o, k=k, wh=wh: e.matmul(bank[b][:, :], h2H[:, k, o], wh,
                                                                         start=k == 0, stop=False),
                          m, h2ready[k], free[b] if k == 0 else None)
                    quiet("pe", lambda e, b=b, o=o, k=k, wl=wl: e.matmul(bank[b][:, :], h2H[:, k, o], wl,
                                                                         start=False, stop=False))
                    mark = op("pe", lambda e, b=b, o=o, k=k, wh=wh: e.matmul(bank[b][:, :], h2L[:, k, o], wh,
                                                                             start=False, stop=k == 15))
                    if k == 15:
                        ev = op("act", lambda e, b=b, q=q: e.activation(
                            dst[:, q, 512 * half:512 * half + 512], bank[b][:, :], func), mark, war)
                        free[b] = [ev]
            used[n] = mark
            pump(BUDGET["v"])
        return ev

    free[6] = free[7] = ssm_done
    BUDGET["v"] = 1.3
    beside.append(residual())
    seq_project(0, VV, ACT.Copy, mk_g)
    BUDGET["v"] = 3.0
    for k in range(16):
        f_, l_ = k == 0, k == 15
        quiet("pe", lambda e, k=k, f_=f_: e.matmul(fps, WFH[:, k, :], h2H[:, k, :],
                                                   start=f_, stop=False), wfp, h2ready[k], free[3])
        quiet("pe", lambda e, k=k: e.matmul(fps, WFH[:, k, :], h2L[:, k, :], start=False, stop=False))
        if l_:
            fm = op("pe", lambda e, k=k: e.matmul(fps, WFL[:, k, :], h2H[:, k, :], start=False, stop=True))
        else:
            quiet("pe", lambda e, k=k: e.matmul(fps, WFL[:, k, :], h2H[:, k, :], start=False, stop=False))
    beside.append(forget())
    vb = seq_project(1, VV, ACT.Copy, mk_g)
    drain_beside()

    dka = [slot(f"ka{i}") for i in range(2)]
    att_start = [x1out, h2ready, nf["m"], m1, m2, s2, so_free, cv_free]
    qa1 = []
    for i in range(2):
        for tile, scale in [(QB[i][64:128, hh, :], 1.0) for hh in range(2)] + [(KBT[i][hh][64:128, :], 0.0)
                                                                               for hh in range(2)]:
            qa1.append(op("act", lambda e: e.activation(tile, ONE[64:128, 0:1].to_broadcast([64, 512]), ACT.Copy,
                                                        scale=scale), att_start, one))
    att_free = [None, None]
    raw_free = [None, None]
    prfree = [None]
    ptfree = [None]
    AB = [4, 5, 6, 7]
    P0 = (0, 512, 896, 1152)
    yready = {}
    stat = {"n": 0}

    finished = set()

    def attend(j, ready, gate):
        buf = j % 2
        for hh in range(2):
            h = 2 * j + hh
            den = []
            for q in range(4):
                w = 128 * (q + 1)
                b = AB[q]
                quiet("pe", lambda e: e.matmul(bank[b][:, 0:w], QA[:, buf, hh, 128 * q:128 * q + 128],
                                               KA[:, buf, hh, 0:w], start=True, stop=False), ready, free[b])
                mm = op("pe", lambda e: e.matmul(bank[b][:, 0:w], QB[buf][:, hh, 128 * q:128 * q + 128],
                                                 KBT[buf][hh][:, 0:w], start=False, stop=True))
                den.append(mm)
            if hh == 1:
                att_free[buf] = mm
            probs = []
            for q in range(4):
                w = 128 * (q + 1)
                b = AB[q]
                i = stat["n"] % 8
                stat["n"] += 1
                nm, rsum = ST[:, 16 + i:17 + i], ST[:, 24 + i:25 + i]
                m = op("dve", lambda e, b=b, w=w: e.tensor_tensor(bank[b][:, w - 128:w], bank[b][:, w - 128:w],
                                                                  CAU[:, :], ALU.add), den[q], cau)
                m = op("dve", lambda e, b=b, w=w, nm=nm: e.tensor_reduce(nm, bank[b][:, 0:w], AX, ALU.max,
                                                                         negate=True), m)
                m = op("act", lambda e, b=b, w=w, nm=nm, rsum=rsum, q=q: e.activation(
                    PR[:, 64 * q * (q + 1):64 * q * (q + 1) + w], bank[b][:, 0:w], ACT.Exp, bias=nm, accum_out=rsum), m, prfree[0])
                free[b] = [m]
                m = op("dve", lambda e, rsum=rsum: e.reciprocal(rsum, rsum), m)
                m = op("dve", lambda e, q=q, w=w, rsum=rsum: e.tensor_scalar(PR[:, 64 * q * (q + 1):64 * q * (q + 1) + w], PR[:, 64 * q * (q + 1):64 * q * (q + 1) + w], rsum,
                                                                             None, ALU.mult), m)
                probs.append(m)
                yield 1.0
            yield 4.5
            pts = []
            for kt in range(4):
                b = AB[kt]
                for q in range(kt, 4):
                    mm = op("pe", lambda e, kt=kt, q=q, b=b: e.transpose(
                        bank[b][:, 128 * q:128 * q + 128], PR[:, 64 * q * (q + 1) + 128 * kt:64 * q * (q + 1) + 128 * kt + 128], IDT[:, :]),
                        probs[q], idt, free[b])
                c0 = 128 * kt
                who = "act" if kt % 2 == 0 else "dve"
                if who == "act":
                    m = op("act", lambda e, b=b, c0=c0, kt=kt: e.activation(PT[:, P0[kt]:P0[kt] + 512 - c0], bank[b][:, c0:512],
                                                                            ACT.Copy), mm, ptfree[0])
                else:
                    m = op("dve", lambda e, b=b, c0=c0, kt=kt: e.tensor_copy(PT[:, P0[kt]:P0[kt] + 512 - c0], bank[b][:, c0:512]),
                           mm, ptfree[0])
                free[b] = [m]
                pts.append(m)
            prfree[0] = mm
            yield 4.0
            o = bank[3][64 * hh:64 * hh + 64, :]
            for kt in range(4):
                c0 = 128 * kt
                mm = op("pe", lambda e, kt=kt, c0=c0, o=o, h=h: e.matmul(
                    o[:, c0:512], VV[:, kt, 64 * h:64 * h + 64], PT[:, P0[kt]:P0[kt] + 512 - c0], start=kt == 0, stop=kt == 3,
                    skip_group_check=True), pts[kt], vb, free[3] if hh == 0 else None)
            ptfree[0] = mm
        m = op("dve", lambda e: e.tensor_tensor(YF[:, 8 + j, :], gate[0], bank[3][:, :], ALU.mult), mm, gate[1])
        free[3] = [m]
        gate_free[buf] = m
        yready[8 + j] = m
        finished.add(j)
        yield 0.7

    gate_free = [None, None]
    BUDGET["v"] = 2.8
    for j in range(8):
        buf = j % 2
        b = next_bank()
        mk = project(b, 2, h2H, h2L, h2ready)
        while j >= 2 and j - 2 not in finished:
            pump(1.0)
        ms = []
        rows = (slice(0, 64), slice(64, 128))
        for hh in range(2):
            src, h_, l_ = bank[b][rows[hh], :], QA[rows[hh], buf, hh, :], QA[rows[1 - hh], buf, hh, :]
            m = op("act", lambda e: e.activation(h_, src, ACT.Copy, scale=0.125), mk, att_free[buf], att_start)
            ms.append(op("act", lambda e: e.activation(QB[buf][0:64, hh, :], src, ACT.Copy, scale=0.125)))
            ms.append(op("dve", lambda e: e.scalar_tensor_tensor(out=l_, in0=src, scalar=0.125,
                                                                 in1=h_.bitcast(F32), op0=ALU.mult,
                                                                 op1=ALU.subtract),
                         mk, m, ms[-1], att_free[buf], att_start))
        free[b] = ms[-2:]
        pump(BUDGET["v"])
        b = next_bank()
        mk = project(b, 2, h2H, h2L, h2ready)
        for hh in range(2):
            src, h_ = bank[b][rows[hh], :], KA[rows[hh], buf, hh, :]
            for i in range(2):
                m = op("act", lambda e: e.activation(KA[rows[i], buf, hh, :], src, ACT.Copy), mk, att_free[buf],
                       att_start)
            ms.append(op("dve", lambda e: e.tensor_tensor(KBT[buf][hh][0:64, :], src, h_.bitcast(F32),
                                                          ALU.subtract), mk, m, att_free[buf], att_start))
            ms.append(m)
        free[b] = ms[-2:]
        for hh in range(2):
            for i in range(2):
                p = 64 + 32 * i
                kd = fl.dma(dka[hh], lambda e: e.dma_start(T[p:p + 1, 1 + hh, :], NF[2 * j + hh:2 * j + hh + 1, :]),
                            nf["m"], raw_free[hh], att_start)
            for i in range(2):
                p = 64 + 32 * i
                m = op("act", lambda e: e.activation(KBT[buf][hh][p:p + 1, :], T[p:p + 1, 1 + hh, :], ACT.Copy),
                       kd, att_free[buf], qa1)
            low = KBT[buf][hh][96:97, :]
            raw_free[hh] = op("dve", lambda e: e.tensor_tensor(low, T[96:97, 1 + hh, :], low.bitcast(F32),
                                                               ALU.subtract), kd, m)
            ms.append(raw_free[hh])
        pump(BUDGET["v"])
        b = next_bank()
        mk = project(b, 2, h2H, h2L, h2ready)
        g_ = SI[:, buf, :]
        gt = op("act", lambda e, b=b, g_=g_: e.activation(g_, bank[b][:, :], ACT.Silu), mk, gate_free[buf],
                si_free[buf])
        free[b] = [gt]
        pump(BUDGET["v"])
        beside.append(attend(j, [*ms, qa1], (g_, gt)))

    SGU = {}
    sgfree = [raw_free[:], raw_free[:]]
    gated = {}

    def gates(h, then=None):
        i = h % 2
        u_, g_ = T[:, i, :], T[:, 2 + i, :]
        b = next_bank()
        mk = project(b, 2, h2H, h2L, h2ready)
        mu_ = op("act", lambda e: e.activation(u_, bank[b][:, :], ACT.Gelu), mk, sgfree[i], nf["m"])
        free[b] = [mu_]
        pump(BUDGET["v"])
        b = next_bank()
        mk = project(b, 2, h2H, h2L, h2ready)
        mg_ = op("act", lambda e: e.activation(g_, bank[b][:, :], ACT.Silu), mk, sgfree[i])
        free[b] = [mg_]
        m = op("pool" if h == 7 else "dve", lambda e: e.tensor_tensor(YF[:, h, :], u_, g_, ALU.mult), mu_, mg_)
        sgfree[i] = m
        gated[h] = m
        if then is not None:
            then(mk)
        pump(BUDGET["v"])
        return mk

    BUDGET["v"] = 3.8
    for h in range(4):
        gates(h)
    drain_beside()
    att_done = [hm_last(fl), free[3]]
    si_free = [*gate_free]
    va1 = seq_project(0, VV, ACT.Gelu, att_done)

    def sgu_const():
        d = slot("ws")
        fl.dma(d, lambda e: e.dma_start(WS[:, :, :], t["wsT"]), att_done)
        ld = fl.dma(d, lambda e: e.dma_start(BSB[:, :, :], t["bsb"]), att_done)
        yield 8.0
        for h in range(8):
            SGU["w", h] = op("pool", lambda e, h=h: e.affine_select(
                out=WS[:, h, :], in_=WS[:, h, :], compare_op=ALU.is_ge, fill=0.0, base=0,
                pattern=[[1, 128]], channel_multiplier=-1), ld)
        yield 8.0
        for h in range(8):
            b = 4 + h // 4
            mm = op("pe", lambda e, h=h, b=b: e.matmul(bank[b][:, 128 * (h % 4):128 * (h % 4) + 128], ONE[:, :],
                                                       WS[:, h, :], start=h % 4 == 0, stop=h % 4 == 3,
                                                       skip_group_check=True), SGU["w", h], free[b])
            if h % 4 == 3:
                for g in range(h - 3, h + 1):
                    m = op("dve", lambda e, g=g, b=b: e.scalar_tensor_tensor(
                        out=CON[:, g, :], in0=bank[b][:, 128 * (g % 4):128 * (g % 4) + 128],
                        scalar=col["lnb"][:, g:g + 1], in1=BSB[:, g, :], op0=ALU.mult, op1=ALU.add), mm, ld,
                        att_done)
                    SGU["c", g] = m
                free[b] = [m]
                yield 2.0

    beside.append(sgu_const())
    va2 = seq_project(1, VV, ACT.Gelu, att_done)
    lnm = []

    def layer_norm():
        mu, va, rr, yy = (ST[:, 32 + 4 * i:36 + 4 * i] for i in range(4))
        ms = [op("dve", lambda e: e.tensor_reduce(mu[:, q:q + 1], VV[:, q, :], AX, ALU.add), va1, va2)
              for q in range(4)]
        m = op("dve", lambda e: e.tensor_scalar(mu, mu, 1.0 / 1024, None, ALU.mult), ms)
        yield 4.6
        xs = []
        for q in range(4):
            x = VV[:, q, :]
            xs.append(op("dve", lambda e: e.tensor_scalar(x, x, mu[:, q:q + 1], None, ALU.subtract), m))
        yield 4.0
        s = None
        for q in range(4):
            s = op("act", lambda e: e.activation(SQ[:, :], VV[:, q, :], ACT.Square, accum_out=va[:, q:q + 1]),
                   xs[q], s, att_done)
            if q % 2:
                yield 3.0
        m = op("dve", lambda e: e.tensor_scalar(va, va, 1.0 / 1024, EPS, ALU.mult, ALU.add), s)
        m = op("act", lambda e: e.activation(yy, va, ACT.Sqrt), m)
        m = op("dve", lambda e: e.reciprocal(rr, yy), m)
        m = op("dve", lambda e: e.tensor_tensor(yy, rr, rr, ALU.mult), m)
        m = op("dve", lambda e: e.tensor_tensor(yy, yy, va, ALU.mult), m)
        m = op("dve", lambda e: e.tensor_scalar(yy, yy, -0.5, 1.5, ALU.mult, ALU.add), m)
        m = op("dve", lambda e: e.tensor_tensor(rr, rr, yy, ALU.mult), m)
        yield 3.0
        for q in range(4):
            x = VV[:, q, :]
            lnm.append(op("dve", lambda e: e.tensor_scalar(x, x, rr[:, q:q + 1], None, ALU.mult), m))
        yield 4.0

    beside.append(layer_norm())
    mixed = {}
    mfree = [None, None]

    def mix():
        for h in range(8):
            b = 6 + h % 2
            for q in range(4):
                mm = op("pe", lambda e: e.matmul(
                    bank[b][:, 128 * q:128 * q + 128], VV[:, q, 128 * h:128 * h + 128], WS[:, h, :],
                    start=q == 0, stop=q == 3, skip_group_check=True), lnm, SGU["w", h], free[b])
            o = MX[:, h % 2, :]
            o3 = o.rearrange("p (n t) -> p n t", t=128)
            m = op("dve", lambda e: e.scalar_tensor_tensor(
                out=o3, in0=bank[b][:, :].rearrange("p (n t) -> p n t", t=128), scalar=col["lng"][:, h:h + 1],
                in1=CON[:, h:h + 1, :].to_broadcast([128, 4, 128]), op0=ALU.mult, op1=ALU.add),
                mm, SGU["c", h])
            free[b] = [m]
            mixed[h] = (m, mm)
            yield 3.0
            debt[0] += 1.8
            if h >= 4:
                while h not in gated:
                    yield 5.0
            yready[h] = op("dve", lambda e: e.tensor_tensor(YF[:, h, :], YF[:, h, :], o, ALU.mult), m, gated[h])
            yield 0.6

    beside.append(mix())
    yHs, yLs = ([a[:, k, :] if k not in (8, 9) else b[k - 8] for k in range(16)]
                for a, b in ((yH, yH8), (yL, yL8)))
    ysplit = [None] * 16
    for k in (8, 9):
        ysplit[k] = split(yHs[k], yLs[k], YF[:, k, :], yready[k], yready[15])

    def split_y(ks, mk):
        for k in ks:
            ysplit[k] = split(yHs[k], yLs[k], YF[:, k, :], yready[k], mk)

    for h in range(4, 7):
        gates(h)
    mk_p = gates(7, lambda mk: split_y(range(10, 16), mk))
    while 7 not in yready:
        pump(1.0)
    mixd = [mixed[h][1] for h in range(8)]

    split_y(range(8), mk_p)
    acc = None
    x2 = []
    tq = [None, None]
    POOL = (3, 7, 11, 14)
    ld = {}

    def close(d, b, c, mk, into):
        x, s_ = X2[:, d, c], SI[:, ld[d][0], c]
        m = op("dve", lambda e: e.scalar_tensor_tensor(
            out=x, in0=bank[b][:, c], scalar=MOD[:, 32 + d:33 + d], in1=s_, op0=ALU.mult, op1=ALU.add),
            mk, ld[d][1], mixd, lnm, mixed[7][0])
        free[b] = [m]
        q = op("act", lambda e: e.activation(into, x, ACT.Square), m, tq[d % 2], sgfree)
        return m, q

    for d in range(15):
        i, s_, mark = load(scratch["x1"][d], x1out)
        ld[d] = (i, mark)
        b = next_bank()
        for kc in (1, 0):
            mk = products8(b, kc, 2, yHs, yLs, ysplit, first=1)
        m, q1 = close(d, b, slice(0, 512), mk, T[:, d % 2, :])
        si_free[i] = m
        if d == 0:
            acc = op("dve", lambda e: e.tensor_copy(SO[:, 0, :], T[:, 0, :]), q1)
        else:
            acc = op("dve", lambda e, d=d: e.tensor_tensor(SO[:, 0, :], SO[:, 0, :], T[:, d % 2, :], ALU.add), q1, acc)
        tq[d % 2] = acc
        if d in POOL:
            m = op("pool", lambda e: e.tensor_scalar(X2[:, d, :], X2[:, d, :], col["fg2"][:, d:d + 1], None,
                                                     ALU.mult), m, q1)
        x2.append([m, q1])

    root_table()
    i, s_, mark = load(scratch["x1"][15], x1out)
    ld[15] = (i, mark)
    chunks = [chunk(), chunk()]
    half = [slice(0, 256), slice(256, 512)]
    sets = []
    for (n, s, m), k0 in zip(chunks, (8, 0)):
        for k8 in range(8):
            sets.append((m, k0 + k8, WH[:, s, 128 * k8:128 * k8 + 128], WL[:, s, 128 * k8:128 * k8 + 128]))
    x2h = {}
    RF = [T[:, 2, half[0]], T[:, 3, half[1]]]

    def norm_steps(h, mk, b):
        c, qs = half[h], (2 * h, 2 * h + 1)
        x2h[h], q = close(15, b, c, mk, T[:, 1, c])
        yield
        mm = token_sums([SO[:, 0, :], T[:, 1, :]], 3 + 2 * h, acc, q, qs=qs)
        r = inv_rms(2, 3 + 2 * h, mm, qs=slice(2 * h, 2 * h + 2))
        yield
        sp = spread(2, 4 + 2 * h, r, qs=qs)
        rf = op("act", lambda e: e.activation(RF[h], bank[4 + 2 * h][:, c], ACT.Copy), sp, sgfree)
        for d2 in range(8):
            ms = []
            for d in (2 * d2, 2 * d2 + 1):
                x = X2[:, d, c]
                if d in POOL:
                    ms.append(op("pool", lambda e: e.tensor_tensor(x, x, RF[h], ALU.mult), rf, x2[d]))
                else:
                    ms.append(op("dve", lambda e: e.scalar_tensor_tensor(
                        out=x, in0=x, scalar=col["fg2"][:, d:d + 1], in1=RF[h], op0=ALU.mult,
                        op1=ALU.mult), rf, x2[d] if d < 15 else [x2h[h], q]))
            last[d2 % 4] = fl.dma(dout[d2 % 4], lambda e: e.dma_start(
                out[2 * d2:2 * d2 + 2, :, c].rearrange("k p s -> p k s"), X2[:, 2 * d2:2 * d2 + 2, c]), ms,
                last[d2 % 4])
            yield

    dout = [slot(f"out{i}") for i in range(4)]
    last = [None] * 4
    free[3] = free[3] + free[5] + free[6]
    first_half = None
    for h in range(2):
        b = next_bank()
        for j, (m, k, wh, wl) in enumerate(sets):
            if h == 1 and j in (6, 12):
                next(first_half)
            o, c = bank[b][:, half[h]], half[h]
            quiet("pe", lambda e: e.matmul(o, wh, yHs[k][:, c], start=j == 0, stop=False), m, ysplit[k],
                  free[b] if j == 0 else None)
            quiet("pe", lambda e: e.matmul(o, wh, yLs[k][:, c], start=False, stop=False))
            mk = op("pe", lambda e: e.matmul(o, wl, yHs[k][:, c], start=False, stop=j == 15))
        if h == 0:
            first_half = norm_steps(h, mk, b)
            next(first_half)
    second_half = norm_steps(1, mk, b)
    for steps, which in ((1, first_half), (1, second_half), (3, first_half), (1, second_half),
                         (3, first_half), (8, second_half)):
        for _ in range(steps):
            next(which)
    finals = [*last, *so_free, *x1out]

    for sem, value in finals:
        nc.sync.wait_ge(sem, value)

def hm_last(fl):
    return fl.sems["pe"], fl.count["pe"]

def lay_out(i):
    import numpy as _np

    f = _np.ascontiguousarray

    def chan(w):
        k, n = w.shape
        return f(w.reshape(k // 1024, 8, 128, n // 128, 128).transpose(3, 0, 2, 1, 4)).reshape(
            n // 128, k // 1024, 128, 1024)

    def col(v):
        return v.reshape(-1, 128).T

    w1 = i["w_in"][0]
    w2 = i["w_in_2"][0]
    wide = _np.concatenate([w2[:, 1024:2048], w2[:, 5120:6144]], axis=1)
    wvv = f(wide.reshape(8, 2, 128, 4, 512).transpose(3, 0, 2, 1, 4)).reshape(4, 8, 128, 1024)
    bf = _np.zeros((128, 1), _np.float32)
    bf[:16, 0] = i["b_f_2"][0]
    cols = _np.concatenate([
        col(i["norm_g"][0]), col(i["final_g"]), col(i["norm_g_2"][0]), col(i["final_g_2"]),
        col(i["conv_w"][0].reshape(-1)), col(i["b_glu"][0]), col(i["d_skip"][0].reshape(-1)),
        col(i["b_ada_2"][0]), col(i["c_2"][0]), col(i["ln_v_g_2"][0]), col(i["ln_v_b_2"][0]), bf], axis=1)
    pairs = lambda a: f(a[0].reshape(32, 128).T)

    def b_rows(b):
        o = _np.zeros((8, 4, 2, 16, 2, 64), _np.float32)
        v = b[0].reshape(8, 4, 2, 64, 16)
        for g in range(2):
            o[:, :, g, :, g, :] = v[:, :, g].transpose(0, 1, 3, 2)
        return o.reshape(32, 32, 128)

    def c_rows(c):
        return f(c[0].reshape(32, 2, 16, 64).transpose(1, 3, 0, 2)).reshape(128, 32, 16)

    return {
        "xT": f(i["x"][0].T).reshape(16, 128, 512),
        "w1": chan(w1), "wg": chan(i["w_glu"][0]), "wa": chan(i["w_out_a"][0]), "wb": chan(i["w_out_b"][0]),
        "wo": chan(i["w_o"][0]), "w2": chan(w2[:, :7168]), "wvv": wvv,
        "wf": f(w2[:, 7168:].reshape(16, 128, 16).transpose(1, 0, 2)), "w3": chan(i["w_out_2"][0]),
        "ada": f(i["w_ada_2"][0].reshape(16, 128, 6, 1024).transpose(2, 0, 1, 3)),
        "cols": f(cols), "are": pairs(i["a_re"]), "aim": pairs(i["a_im"]),
        "ldt": pairs(_np.repeat(i["log_dt"][0], 64)[None]),
        "bstk": f(_np.tile(_np.stack([b_rows(i["b_re"]), b_rows(i["b_im"])], axis=2), (1, 3, 1, 1))),
        "cre": c_rows(i["c_re"]), "cim": c_rows(i["c_im"]),
        "wsT": f(i["w_s_2"][0].transpose(2, 0, 1)),
        "bsb": f(_np.broadcast_to(i["b_s_2"][0][None], (128, 8, 128))),
    }

def kernel(**inputs):
    import numpy as _np
    import concourse.bacc as _bacc
    from concourse import mybir as _mybir
    from concourse.bass_utils import run_bass_kernel_spmd as _run

    arrays = lay_out({k: _np.asarray(v) for k, v in inputs.items()})
    nc = _bacc.Bacc("TRN2", target_bir_lowering=False, num_devices=1)
    t = {n: nc.dram_tensor("in_" + n, arrays[n].shape, _mybir.dt.float32, kind="ExternalInput").ap() for n in PARAMS}
    out = nc.dram_tensor("out_y", (16, 128, 512), _mybir.dt.float32, kind="ExternalOutput").ap()
    program(nc, t, out)
    r = _run(nc, [{"in_" + n: arrays[n] for n in PARAMS}], core_ids=[0])
    got = r.results[0]["out_y"]
    return _np.ascontiguousarray(got.reshape(2048, 512).T).reshape(1, 512, 2048)
```
